# Optimizing a Trainium2 kernel written in Bass

```python
import jax
import jax.numpy as jnp
from jax import lax
import numpy as np

D_MODEL = 1024
BATCH = 1
SEQ = 1024
DEPTH = 1
DEC_BATCH = 8
DEC_SEQ = 8
PAST_LEN = 8192
PAGE_SIZE = 128

DN_HEADS = 8
DN_HD = 128
DN_DIM = DN_HEADS * DN_HD
QKV_DIM = 3 * DN_DIM
CONV_W = 4
DN_CHUNK = 64
POOL_WINDOWS = (2, 4, 8, 16)
POOL_GROUPS = 4
POOL_DIM = D_MODEL
POOL_GD = POOL_DIM // POOL_GROUPS
POOL_MAX = 16
MEM_LEN = 256
CA_HEADS = 4
CA_HD = D_MODEL // CA_HEADS
MOE_GROUPS = 8
MOE_EPG = 8
MOE_EXPERTS = MOE_GROUPS * MOE_EPG
MOE_TOPK = 2
MOE_FF = D_MODEL // 4
MOE_BLOCK = 128
N_IN = QKV_DIM + DN_DIM + 2 * DN_HEADS + POOL_DIM + 2 * D_MODEL
LN_EPS = 1e-5
NORM_EPS = 1e-6

kernel_name = "hybrid_deltanet_pool_hmoe_decoder_step"

def layer_norm(x, g, b):
    xf = x.astype(jnp.float32)
    mu = jnp.mean(xf, -1, keepdims=True)
    var = jnp.mean(jnp.square(xf - mu), -1, keepdims=True)
    return ((xf - mu) * lax.rsqrt(var + LN_EPS) * g + b).astype(x.dtype)

def l2norm(x):
    return x * lax.rsqrt(jnp.sum(x * x, -1, keepdims=True) + NORM_EPS)

def causal_short_conv(u, prev, w):
    L = u.shape[1]
    full = jnp.concatenate([prev, u], axis=1)
    y = sum(full[:, i:i + L] * w[i] for i in range(CONV_W))
    return jax.nn.silu(y), full[:, -(CONV_W - 1):]

def gated_delta_rule(q, k, v, g, beta, S0):
    B, L, H, DK = q.shape
    DV = v.shape[-1]
    C = min(DN_CHUNK, L)
    n = -(-L // C)
    pad = n * C - L

    def to_chunks(t):
        t = jnp.pad(t, [(0, 0), (0, pad)] + [(0, 0)] * (t.ndim - 2))
        t = t.reshape((B, n, C) + t.shape[2:])
        return jnp.moveaxis(t, 3, 2)

    qc, kc, vc, gc, bc = (to_chunks(t) for t in (q, k, v, g, beta))
    gcum = jnp.cumsum(gc, axis=-1)
    idx = jnp.arange(C)
    causal = idx[:, None] >= idx[None, :]
    strict = idx[:, None] > idx[None, :]
    decay = jnp.exp(jnp.where(causal, gcum[..., :, None] - gcum[..., None, :], -jnp.inf))
    kb = kc * bc[..., None]
    A = jnp.where(strict, jnp.einsum('bnhid,bnhjd->bnhij', kb, kc) * decay, 0.0)
    rhs = jnp.concatenate([vc * bc[..., None], kb * jnp.exp(gcum)[..., None]], axis=-1)
    sol = lax.linalg.triangular_solve(A + jnp.eye(C, dtype=A.dtype), rhs,
                                      left_side=True, lower=True, unit_diagonal=True)
    u, w = sol[..., :DV], sol[..., DV:]
    qk = jnp.where(causal, jnp.einsum('bnhid,bnhjd->bnhij', qc, kc) * decay, 0.0)
    qg = qc * jnp.exp(gcum)[..., None]
    kg = kc * jnp.exp(gcum[..., -1:] - gcum)[..., None]
    glast = jnp.exp(gcum[..., -1])

    def step(S, inp):
        qg_i, kg_i, u_i, w_i, qk_i, gl_i = inp
        v_new = u_i - jnp.einsum('bhck,bhkv->bhcv', w_i, S)
        o = jnp.einsum('bhck,bhkv->bhcv', qg_i, S) + jnp.einsum('bhij,bhjv->bhiv', qk_i, v_new)
        S = S * gl_i[..., None, None] + jnp.einsum('bhck,bhcv->bhkv', kg_i, v_new)
        return S, o

    xs = tuple(jnp.moveaxis(t, 1, 0) for t in (qg, kg, u, w, qk, glast))
    S, o = lax.scan(step, S0, xs)
    o = jnp.moveaxis(jnp.moveaxis(o, 0, 1), 2, 3).reshape(B, n * C, H, DV)[:, :L]
    return o, S

def multiscale_pool(p, prev, pos0):
    B, L, P = p.shape
    full = jnp.concatenate([prev, p], axis=1)
    cs = jnp.cumsum(full.astype(jnp.float32), axis=1)
    cs = jnp.concatenate([jnp.zeros((B, 1, P), jnp.float32), cs], axis=1)
    off = POOL_MAX
    pos = pos0 + jnp.arange(L)
    outs = []
    for gi, win in enumerate(POOL_WINDOWS):
        sl = slice(gi * POOL_GD, (gi + 1) * POOL_GD)
        s = cs[:, off:off + L, sl] - cs[:, off - win:off - win + L, sl]
        cnt = jnp.minimum(win, pos + 1).astype(jnp.float32)
        outs.append(s / cnt[None, :, None])
    pooled = jnp.concatenate(outs, axis=-1) - p.astype(jnp.float32)
    return pooled, full[:, -(POOL_MAX - 1):]

def memory_kv(mem, w_ck, w_cv):
    B, M, _ = mem.shape
    return ((mem @ w_ck).reshape(B, M, CA_HEADS, CA_HD), (mem @ w_cv).reshape(B, M, CA_HEADS, CA_HD))

def memory_attention(x, mem_k, mem_v, w_cq, w_co):
    B, L, D = x.shape
    q = (x @ w_cq).reshape(B, L, CA_HEADS, CA_HD)
    s = jnp.einsum('blhd,bmhd->bhlm', q, mem_k, preferred_element_type=jnp.float32) * (CA_HD ** -0.5)
    p = jax.nn.softmax(s, axis=-1)
    o = jnp.einsum('bhlm,bmhd->blhd', p.astype(x.dtype), mem_v).reshape(B, L, D)
    return o @ w_co

def hier_moe(x, w_rg, w_re, w_gate, w_up, w_down):
    B, L, D = x.shape
    T = B * L
    xf = x.reshape(T, D)
    g_logits = (xf @ w_rg).astype(jnp.float32)
    g_prob = jax.nn.softmax(g_logits, axis=-1)
    g_sel = jnp.argmax(g_logits, axis=-1).astype(jnp.int32)
    g_w = jnp.take_along_axis(g_prob, g_sel[:, None], axis=-1)
    e_logits = (xf @ w_re).astype(jnp.float32).reshape(T, MOE_GROUPS, MOE_EPG)
    e_logits = jnp.take_along_axis(e_logits, g_sel[:, None, None], axis=1)[:, 0]
    top_v, top_i = lax.top_k(e_logits, MOE_TOPK)
    e_w = jax.nn.softmax(top_v, axis=-1) * g_w
    e_idx = g_sel[:, None] * MOE_EPG + top_i.astype(jnp.int32)

    A = T * MOE_TOPK
    E = MOE_EXPERTS
    blk = MOE_BLOCK
    e_flat = e_idx.reshape(A)
    tok = jnp.repeat(jnp.arange(T, dtype=jnp.int32), MOE_TOPK)
    wts = e_w.reshape(A)
    order = jnp.argsort(e_flat)
    e_sorted = e_flat[order]
    counts = jnp.zeros((E,), jnp.int32).at[e_flat].add(1)
    start = jnp.cumsum(counts) - counts
    padded = (counts + blk - 1) // blk * blk
    pend = jnp.cumsum(padded)
    pstart = pend - padded
    dest = pstart[e_sorted] + (jnp.arange(A, dtype=jnp.int32) - start[e_sorted])
    n_blocks = (A + E * (blk - 1) + blk - 1) // blk
    R = n_blocks * blk
    row_tok = jnp.zeros((R,), jnp.int32).at[dest].set(tok[order])
    row_w = jnp.zeros((R,), jnp.float32).at[dest].set(wts[order])
    block_start = jnp.arange(n_blocks, dtype=jnp.int32) * blk
    block_expert = jnp.minimum(jnp.searchsorted(pend, block_start, side='right'), E - 1).astype(jnp.int32)

    def block_fn(args):
        toks, e = args
        xb = xf[toks]
        h = jax.nn.silu(xb @ w_gate[e]) * (xb @ w_up[e])
        return h @ w_down[e]

    out_rows = lax.map(block_fn, (row_tok.reshape(n_blocks, blk), block_expert))
    y = jnp.zeros((T, D), jnp.float32).at[row_tok].add(out_rows.reshape(R, D).astype(jnp.float32) * row_w[:, None])
    return y.reshape(B, L, D).astype(x.dtype)

def decoder_layer(x, mem_k, mem_v, conv_prev, pool_prev, S0, pos0, alpha,
                  w_in, w_conv, a_log, dt_bias, w_onorm, w_pool, pool_scale, w_out, ln1_g, ln1_b,
                  w_cq, w_co, ln2_g, ln2_b, w_rg, w_re, w_gate, w_up, w_down, ln3_g, ln3_b):
    B, L, D = x.shape
    f32 = jnp.float32
    proj = x @ w_in
    o1 = QKV_DIM
    o2 = o1 + DN_DIM
    o3 = o2 + DN_HEADS
    o4 = o3 + DN_HEADS
    o5 = o4 + POOL_DIM
    o6 = o5 + D_MODEL
    qkv_raw, z, a_raw, b_raw, p_raw, gate_a, gate_b = jnp.split(proj, [o1, o2, o3, o4, o5, o6], axis=-1)

    qkv, conv_new = causal_short_conv(qkv_raw, conv_prev, w_conv)
    q, k, v = jnp.split(qkv.astype(f32), 3, axis=-1)
    q = l2norm(q.reshape(B, L, DN_HEADS, DN_HD)) * (DN_HD ** -0.5)
    k = l2norm(k.reshape(B, L, DN_HEADS, DN_HD))
    v = v.reshape(B, L, DN_HEADS, DN_HD)
    beta = jax.nn.sigmoid(b_raw.astype(f32))
    g = -jnp.exp(a_log.astype(f32)) * jax.nn.softplus(a_raw.astype(f32) + dt_bias.astype(f32))
    o, S_new = gated_delta_rule(q, k, v, g, beta, S0.astype(f32))
    o = o * lax.rsqrt(jnp.mean(o * o, -1, keepdims=True) + NORM_EPS) * w_onorm
    o = o * jax.nn.silu(z.astype(f32).reshape(B, L, DN_HEADS, DN_HD))
    branch_a = o.reshape(B, L, DN_DIM).astype(x.dtype)

    pooled, pool_new = multiscale_pool(p_raw, pool_prev, pos0)
    pooled = jnp.einsum('blgc,gcd->blgd', pooled.reshape(B, L, POOL_GROUPS, POOL_GD), w_pool.astype(f32))
    branch_b = (pooled.reshape(B, L, POOL_DIM) * pool_scale).astype(x.dtype)

    merged = jax.nn.sigmoid(gate_a) * branch_a + jax.nn.sigmoid(gate_b) * branch_b
    x1 = layer_norm(alpha * x + merged @ w_out, ln1_g, ln1_b)
    x2 = layer_norm(alpha * x1 + memory_attention(x1, mem_k, mem_v, w_cq, w_co), ln2_g, ln2_b)
    x3 = layer_norm(alpha * x2 + hier_moe(x2, w_rg, w_re, w_gate, w_up, w_down), ln3_g, ln3_b)
    return x3, S_new.astype(S0.dtype), conv_new, pool_new

def setup_inputs(seed: int = 0) -> dict:
    key = jax.random.key(seed)
    ks = jax.random.split(key, 40)
    f32 = jnp.float32
    beta_dn = (8 * DEPTH) ** -0.25

    def nrm(k, shape, scale):
        return jax.random.normal(k, shape, f32) * scale

    dt = jnp.exp(jax.random.uniform(ks[11], (DEPTH, DN_HEADS), f32, np.log(1e-3), np.log(1e-1)))
    return {
        "x_prompt": nrm(ks[0], (BATCH, SEQ, D_MODEL), 1.0),
        "x_sample": nrm(ks[1], (DEC_BATCH, DEC_SEQ, D_MODEL), 1.0),
        "cache_mem_k": nrm(ks[2], (DEPTH, DEC_BATCH, MEM_LEN, CA_HEADS, CA_HD), 1.0),
        "cache_mem_v": nrm(ks[3], (DEPTH, DEC_BATCH, MEM_LEN, CA_HEADS, CA_HD), 1.0),
        "state_delta": nrm(ks[4], (DEPTH, DEC_BATCH, DN_HEADS, DN_HD, DN_HD), 0.5),
        "state_conv": nrm(ks[5], (DEPTH, DEC_BATCH, CONV_W - 1, QKV_DIM), 1.0),
        "state_pool": nrm(ks[6], (DEPTH, DEC_BATCH, POOL_MAX - 1, POOL_DIM), 1.0),
        "mem_prompt": nrm(ks[7], (BATCH, MEM_LEN, D_MODEL), 1.0),
        "w_in": nrm(ks[8], (DEPTH, D_MODEL, N_IN), D_MODEL ** -0.5),
        "w_conv": nrm(ks[9], (DEPTH, CONV_W, QKV_DIM), CONV_W ** -0.5),
        "a_log": jnp.log(jax.random.uniform(ks[10], (DEPTH, DN_HEADS), f32, 1.0, 16.0)),
        "dt_bias": dt + jnp.log(-jnp.expm1(-dt)),
        "w_onorm": 1.0 + nrm(ks[12], (DEPTH, DN_HD), 0.05),
        "w_pool": nrm(ks[13], (DEPTH, POOL_GROUPS, POOL_GD, POOL_GD), POOL_GD ** -0.5),
        "pool_scale": 1.0 + nrm(ks[14], (DEPTH, POOL_DIM), 0.05),
        "w_out": nrm(ks[15], (DEPTH, D_MODEL, D_MODEL), beta_dn * D_MODEL ** -0.5),
        "ln1_g": 1.0 + nrm(ks[16], (DEPTH, D_MODEL), 0.05),
        "ln1_b": nrm(ks[17], (DEPTH, D_MODEL), 0.02),
        "w_cq": nrm(ks[18], (DEPTH, D_MODEL, D_MODEL), D_MODEL ** -0.5),
        "w_ck": nrm(ks[19], (DEPTH, D_MODEL, D_MODEL), D_MODEL ** -0.5),
        "w_cv": nrm(ks[20], (DEPTH, D_MODEL, D_MODEL), D_MODEL ** -0.5),
        "w_co": nrm(ks[21], (DEPTH, D_MODEL, D_MODEL), beta_dn * D_MODEL ** -0.5),
        "ln2_g": 1.0 + nrm(ks[22], (DEPTH, D_MODEL), 0.05),
        "ln2_b": nrm(ks[23], (DEPTH, D_MODEL), 0.02),
        "w_router_group": nrm(ks[24], (DEPTH, D_MODEL, MOE_GROUPS), D_MODEL ** -0.5),
        "w_router_expert": nrm(ks[25], (DEPTH, D_MODEL, MOE_EXPERTS), D_MODEL ** -0.5),
        "w_gate": nrm(ks[26], (DEPTH, MOE_EXPERTS, D_MODEL, MOE_FF), D_MODEL ** -0.5),
        "w_up": nrm(ks[27], (DEPTH, MOE_EXPERTS, D_MODEL, MOE_FF), D_MODEL ** -0.5),
        "w_down": nrm(ks[28], (DEPTH, MOE_EXPERTS, MOE_FF, D_MODEL), beta_dn * MOE_FF ** -0.5),
        "ln3_g": 1.0 + nrm(ks[29], (DEPTH, D_MODEL), 0.05),
        "ln3_b": nrm(ks[30], (DEPTH, D_MODEL), 0.02),
    }

def reference(x_prompt, x_sample, cache_mem_k, cache_mem_v, state_delta, state_conv, state_pool, mem_prompt,
              w_in, w_conv, a_log, dt_bias, w_onorm, w_pool, pool_scale, w_out, ln1_g, ln1_b,
              w_cq, w_ck, w_cv, w_co, ln2_g, ln2_b, w_router_group, w_router_expert, w_gate, w_up, w_down,
              ln3_g, ln3_b):
    alpha = (2 * DEPTH) ** 0.25
    h_p, h_s = x_prompt, x_sample
    Bp = x_prompt.shape[0]
    dtp = x_prompt.dtype
    d_p, c_p, p_p, mk_p, mv_p, d_s, c_s, p_s = [], [], [], [], [], [], [], []
    for l in range(DEPTH):
        lw = (w_in[l], w_conv[l], a_log[l], dt_bias[l], w_onorm[l], w_pool[l], pool_scale[l], w_out[l],
              ln1_g[l], ln1_b[l], w_cq[l], w_co[l], ln2_g[l], ln2_b[l], w_router_group[l], w_router_expert[l],
              w_gate[l], w_up[l], w_down[l], ln3_g[l], ln3_b[l])
        mk, mv = memory_kv(mem_prompt, w_ck[l], w_cv[l])
        S0 = jnp.zeros((Bp, DN_HEADS, DN_HD, DN_HD), dtp)
        conv0 = jnp.zeros((Bp, CONV_W - 1, QKV_DIM), dtp)
        pool0 = jnp.zeros((Bp, POOL_MAX - 1, POOL_DIM), dtp)
        h_p, dl, cl, pl = decoder_layer(h_p, mk, mv, conv0, pool0, S0, 0, alpha, *lw)
        d_p.append(dl)
        c_p.append(cl)
        p_p.append(pl)
        mk_p.append(mk)
        mv_p.append(mv)
        h_s, dl, cl, pl = decoder_layer(h_s, cache_mem_k[l], cache_mem_v[l], state_conv[l], state_pool[l],
                                        state_delta[l], PAST_LEN, alpha, *lw)
        d_s.append(dl)
        c_s.append(cl)
        p_s.append(pl)
    return (h_p, h_s, jnp.stack(d_p), jnp.stack(c_p), jnp.stack(p_p), jnp.stack(mk_p), jnp.stack(mv_p),
            jnp.stack(d_s), jnp.stack(c_s), jnp.stack(p_s))


_drawn_inputs = setup_inputs


def setup_inputs(seed=0):
    import zlib

    import numpy as np

    out = dict(_drawn_inputs(seed))
    spreads = {}
    factors = {'w_onorm': 5.741, 'pool_scale': 3.914, 'ln3_b': 2.771}
    for name, (base, spread) in spreads.items():
        noise = np.random.default_rng([zlib.crc32(name.encode()), seed]).standard_normal(out[name].shape)
        drawn = base * np.exp(spread * noise) if base else spread * noise
        out[name] = jnp.asarray(drawn.astype(out[name].dtype))
    for name, factor in factors.items():
        out[name] = (out[name] * factor).astype(out[name].dtype)
    return out
```

```python
from contextlib import ExitStack

import numpy as np
import concourse.bass as bass
from concourse import mybir

ALU = mybir.AluOpType
ACT = mybir.ActivationFunctionType
F32 = mybir.dt.float32
BF16 = mybir.dt.bfloat16
I32 = mybir.dt.int32
U32 = mybir.dt.uint32
AX_X = mybir.AxisListType.X

P = 128
D = 1024
KC = D // P
SEQ, NB, DS = 1024, 8, 8
NS = NB * DS
T = SEQ + NS
NT = SEQ // P + 1
H, HD = 8, 128
QKV = 3 * H * HD
CW = 4
POOLW = (2, 4, 8, 16)
PG = 256
PM = 16
MEM = 256
CAH, CAD = 4, 256
EG, EPG, E, FF = 8, 8, 64, 256
O_Z = QKV
O_A = O_Z + H * HD
O_P = O_A + 2 * H
O_GA = O_P + D
O_GB = O_GA + D
ALPHA = 2.0 ** 0.25
LN_EPS = 1e-5
NORM_EPS = 1e-6
LEVELS = 7
SLEVELS = 3
SEGS = ((0, 512), (512, 512), (1024, 64))
BLK = 64
NBLK = (2 * T + E * (BLK - 1)) // BLK
NBLK += NBLK % 2
SLOTS = NBLK * BLK
MIN_SLOTS = 2 * T
FILL_ROWS = (SLOTS - MIN_SLOTS) // H


def rows_of(t):
    return P if t < NT - 1 else NS


def constants():
    i = np.arange(P)
    level = np.zeros((P, LEVELS, P), np.float32)
    for n in range(LEVELS):
        s = 1 << n
        same = (i[:, None] // (2 * s)) == (i[None, :] // (2 * s))
        level[:, n] = same & ((i[:, None] // s) % 2 == 1) & ((i[None, :] // s) % 2 == 0)
    block8 = (i[:, None] // DS == i[None, :] // DS).astype(np.float32)
    upper = (i[:, None] <= i[None, :]).astype(np.float32)
    ident = np.eye(P, dtype=np.float32)
    ones = np.ones((P, P), np.float32)
    inseq = (i[:, None] // DS == np.arange(NB)[None, :]).astype(np.float32)
    early = np.ones((P, len(POOLW), PM), np.float32)
    for g, w in enumerate(POOLW):
        for t in range(w):
            early[:, g, t] = w / (t + 1)
    eps = np.tile(np.array([NORM_EPS, NORM_EPS * HD, LN_EPS, 1.0], np.float32), (P, 1))
    parts = [eps, ident, upper, ones, upper * block8, block8, inseq, early.reshape(P, -1), level.reshape(P, -1)]
    return np.concatenate(parts, axis=1)


C_EPS = 0
C_ID, C_UP, C_ONE, C_UP8, C_BLK8 = (4 + n * P for n in range(5))
C_SEQ = 4 + 5 * P
C_EARLY = C_SEQ + NB
C_LEVEL = C_EARLY + len(POOLW) * PM
C_ALL = C_LEVEL + LEVELS * P

S_GC, S_KG, S_KBE, S_BETA, S_G, S_EGL, S_EGLS = 0, 9, 18, 27, 36, 45, 53
S_ALL = 64
R_CONV, R_PS, R_ON = 0, CW * 24, CW * 24 + 8
R_ALL = R_ON + 1


def routing_constants():
    i = np.arange(P)
    row = np.ones((P, 1), np.float32)
    strict = (i[:, None] < i[None, :]).astype(np.float32)
    valid = (np.arange(NT)[None, :] * P + i[:, None] < T).astype(np.float32)
    parts = [strict, row * np.arange(EG), row * np.arange(E), valid, row * np.arange(NMAX) * BLK,
             row * np.arange(NBLK // 2) * 2, i[:, None]]
    return np.concatenate([p.astype(np.float32) for p in parts], axis=1)


NMAX = -(-T // BLK)
FAR = 1e30
RC_STRICT, RC_I8, RC_I64 = 0, P, P + EG
RC_VALID = RC_I64 + E
RC_START = RC_VALID + NT
RC_PAIR = RC_START + NMAX
RC_PART = RC_PAIR + NBLK // 2
RC_ALL = RC_PART + 1


class Persistent:
    pass


def phase_a(nc, A, O, M):
    with ExitStack() as ctx:
        def sb(name, shape, dt=F32):
            return ctx.enter_context(nc.sbuf_tensor(name, shape, dt))

        def sem(name):
            return ctx.enter_context(nc.semaphore(name))

        bank = [ctx.enter_context(nc.psum_tensor(f"a_bank{i}", [P, 512], F32)) for i in range(8)]
        rowbuf = sb("rowbuf", [P, 2, D])
        memT = sb("memT", [P, KC, MEM])
        wckv = sb("wckv", [P, KC, D])
        kvrow = sb("kvrow", [P, 2, D])
        wab = sb("wab", [P, KC, 2 * H])
        ab = sb("ab", [P, NT, 2 * H])
        dtb = sb("dtb", [P, H])
        alog = sb("alog", [P, H])
        u = sb("u", [P, NT, H])
        u2 = sb("u2", [P, NT, H])
        gtm = sb("gtm", [P, NT, H])
        gseq = sb("gseq", [NS, NB, H])
        gl = sb("gl", [P, NT, H])
        prow = sb("prow", [R_ALL, P])
        sprow = sb("sprow", [(PM - 1) * NB, D])
        wp = sb("wp", [P, KC, PG])
        wg = sb("wg", [P, KC, PG])
        wpool = sb("wpool", [P, 2, PG])
        praw = sb("praw", [P, 2, PM - 1 + SEQ])
        psam = sb("psam", [P, 2, NB, PM - 1 + DS])
        statep = sb("statep", [P, KC, NB * (PM - 1)])
        pw_a = sb("pw_a", [P, 2, PM - 1 + SEQ])
        pw_as = sb("pw_as", [P, 2, NB, PM - 1 + DS])
        pw_bs = sb("pw_bs", [P, 2, NB, PM - 1 + DS])
        pooled_gate = sb("pooled_gate", [P, 2, 2, T])
        pooled, gate = pooled_gate[:, 0], pooled_gate[:, 1]
        scrow = pooled_gate[:, :, :, :].rearrange("p a c t -> p (a c t)")[0:(CW - 1) * NB, 0:QKV]
        ptok = sb("ptok", [NS, D])
        ptail = sprow[0:PM - 1, :]

        row_in = [sem(f"row_in{i}") for i in range(2)]
        const_in = sem("const_in")
        param_in = sem("param_in")
        wab_in = sem("wab_in")
        state_in = sem("state_in")
        wkv_in = sem("wkv_in")
        wpool_in = [sem(f"wpool_in{i}") for i in range(3)]
        unit_ready = sem("unit_ready")
        unit_out = sem("unit_out")
        act_step = sem("act_step")
        dve_step = sem("dve_step")
        pooled_ready = sem("pooled_ready")
        merged_ready = sem("merged_ready")
        zeroed = sem("zeroed")
        out_done = sem("a_out_done")
        kv_out = [sem(f"kv_out{i}") for i in range(2)]

        U_X = 0
        U_PAR = U_X + 2 * (NT + 2)
        U_SC = U_PAR + 1
        U_SP = U_SC + 2
        U_AB = U_SP + 2
        U_GC = U_AB + 1
        U_KV = U_GC + 1
        U_POOL = U_KV + 8
        PER_G = 6 + 1 + 6 + 6
        src = [A["x_prompt"][0, t * P:(t + 1) * P, :] for t in range(NT - 1)]
        src += [A["x_sample"].rearrange("b l d -> (b l) d")]
        src += [A["mem_prompt"][0, t * P:(t + 1) * P, :] for t in range(2)]

        def nrow(t):
            return NS if t == NT - 1 else P

        DVE_ABS, DVE_G, DVE_ALL = 1, 2, 3

        def load_pool(sp, g):
            base = U_POOL + (g - 1) * PER_G
            if g:
                sp.wait_ge(unit_ready, base + 6)
            sp.dma_start(wp[:, :, :], A["w_in"][0, :, O_P + g * PG:O_P + (g + 1) * PG]
                         .rearrange("(c p) n -> p c n", p=P)).then_inc(wpool_in[0], 16)
            if g:
                sp.wait_ge(unit_ready, base + 13)
            sp.dma_start(wg[:, :, :], A["w_in"][0, :, O_GB + g * PG:O_GB + (g + 1) * PG]
                         .rearrange("(c p) n -> p c n", p=P)).then_inc(wpool_in[1], 16)
            if g:
                sp.wait_ge(unit_ready, base + PER_G)
            sp.dma_start(wpool[:, :, :], A["w_pool"][0, g].rearrange("(c p) n -> p c n", p=P)).then_inc(wpool_in[2], 16)

        block = ctx.enter_context(nc.Block())

        @block.sync
        def _(sp):
            sp.dma_start(M.const[:, :], A["const"]).then_inc(const_in, 16)
            for t in range(NT + 2):
                if t >= 2:
                    sp.wait_ge(unit_ready, 2 * (t - 1))
                sp.dma_start(rowbuf[0:nrow(t), t % 2, :], src[t]).then_inc(row_in[t % 2], 16)
                if t == 1:
                    wv = A["w_conv"][0].rearrange("i (j h p) -> (i j h) p", j=3, p=P)
                    sp.dma_start(prow[0:R_PS, :], wv).then_inc(param_in, 16)
                    sp.dma_start(prow[R_PS:R_ON, :], A["pool_scale"].rearrange("o (c p) -> (o c) p", p=P)).then_inc(param_in, 16)
                    sp.dma_start(prow[R_ON:R_ALL, :], A["w_onorm"]).then_inc(param_in, 16)
                    sp.dma_start(scrow, A["state_conv"].rearrange("o b j c -> (o b j) c")).then_inc(state_in, 16)
                    sp.dma_start(sprow[:, :], A["state_pool"].rearrange("o b j c -> (o b j) c")).then_inc(state_in, 16)
                    sp.dma_start(wab[:, :, :], A["w_in"][0, :, O_A:O_P].rearrange("(c p) n -> p c n", p=P)).then_inc(wab_in, 16)
                    sp.dma_start(dtb[:, :], A["dt_bias"].to_broadcast((P, H))).then_inc(wab_in, 16)
                    sp.dma_start(alog[:, :], A["a_log"].to_broadcast((P, H))).then_inc(wab_in, 16)
            sp.dma_start(wckv[:, :, :], A["w_ck"][0].rearrange("(c p) n -> p c n", p=P)).then_inc(wkv_in, 16)
            for g in range(2):
                load_pool(sp, g)
                if g == 0:
                    sp.wait_ge(unit_ready, U_KV + 4)
                    sp.dma_start(wckv[:, :, :], A["w_cv"][0].rearrange("(c p) n -> p c n", p=P)).then_inc(wkv_in, 16)
            for g in range(2, 4):
                load_pool(sp, g)
            sp.dma_start(O["pool_sample"][0, :, 0:PM - 1 - DS, :], A["state_pool"][0, :, DS:PM - 1, :]).then_inc(out_done, 16)
            sp.wait_ge(unit_out, U_POOL + 3 * PER_G + 7)
            for b in range(NB):
                sp.dma_start(O["pool_sample"][0, b, PM - 1 - DS:PM - 1, :], ptok[b * DS:(b + 1) * DS, :]).then_inc(out_done, 16)
            sp.dma_start(O["pool_prompt"][0, 0], ptail[:, :]).then_inc(out_done, 16)
            sp.wait_ge(out_done, 16 * (NB + 2))
            sp.wait_ge(kv_out[0], 32)
            sp.wait_ge(kv_out[1], 32)

        @block.tensor
        def _(pe):
            def begin(unit):
                if unit >= 8:
                    pe.wait_ge(unit_out, unit - 7)
                return bank[unit % 8]

            pe.wait_ge(const_in, 16)
            for t in range(NT + 2):
                pe.wait_ge(row_in[t % 2], 16 * (t // 2 + 1))
                n = nrow(t)
                for half in range(2):
                    b = begin(U_X + 2 * t + half)
                    for c in range(4):
                        k = 4 * half + c
                        mm = nc.tensor.transpose(b[:, c * P:c * P + n], rowbuf[0:n, t % 2, k * P:(k + 1) * P], M.ident[0:n, 0:n])
                    mm.then_inc(unit_ready, 1)
            b = begin(U_PAR)
            pe.wait_ge(param_in, 48)
            nc.tensor.transpose(b[:, 0:R_ALL], prow[:, :], M.ident[0:R_ALL, 0:R_ALL]).then_inc(unit_ready, 1)
            pe.wait_ge(state_in, 32)
            n = (CW - 1) * NB
            for half in range(2):
                b = begin(U_SC + half)
                for c in range(12):
                    k = 12 * half + c
                    mm = nc.tensor.transpose(b[:, c * n:(c + 1) * n], scrow[:, k * P:(k + 1) * P], M.ident[0:n, 0:n])
                mm.then_inc(unit_ready, 1)
            n = (PM - 1) * NB
            for half in range(2):
                b = begin(U_SP + half)
                for c in range(4):
                    k = 4 * half + c
                    mm = nc.tensor.transpose(b[:, c * n:(c + 1) * n], sprow[:, k * P:(k + 1) * P], M.ident[0:n, 0:n])
                mm.then_inc(unit_ready, 1)
            b = begin(U_AB)
            pe.wait_ge(wab_in, 48)
            pe.wait_ge(unit_out, U_X + 2 * NT)
            for t in range(NT):
                n = rows_of(t)
                for k in range(KC):
                    mm = nc.tensor.matmul(b[0:n, t * 2 * H:(t + 1) * 2 * H], M.xT[:, k, t * P:t * P + n], wab[:, k, :],
                                          start=(k == 0), stop=(k == KC - 1))
            mm.then_inc(unit_ready, 1)
            b = begin(U_GC)
            pe.wait_ge(dve_step, DVE_G)
            np_ = (NT - 1) * H
            gp = gtm[:, 0:NT - 1, :].rearrange("p t h -> p (t h)")
            nc.tensor.matmul(b[:, 0:np_], M.upper, gp, start=True, stop=True)
            nc.tensor.matmul(b[:, 64:64 + np_], M.ones, gp, start=True, stop=True)
            nc.tensor.matmul(b[0:NS, 128:128 + H], M.upper8[0:NS, 0:NS], gtm[0:NS, NT - 1, :], start=True, stop=True)
            nc.tensor.matmul(b[0:NS, 136:136 + H], M.block8[0:NS, 0:NS], gtm[0:NS, NT - 1, :], start=True, stop=True)
            nc.tensor.matmul(b[:, 192:256], M.ones[0:NS, :], gseq[:, :, :].rearrange("p b h -> p (b h)"),
                             start=True, stop=True).then_inc(unit_ready, 1)

            def memory(i):
                pe.wait_ge(wkv_in, 16 * (i // 2 + 1))
                pe.wait_ge(unit_out, U_X + 2 * (NT + 2))
                for half in range(2):
                    b = begin(U_KV + 2 * i + half)
                    for k in range(KC):
                        mm = nc.tensor.matmul(b[:, :], memT[:, k, (i % 2) * P:(i % 2 + 1) * P],
                                              wckv[:, k, half * 512:(half + 1) * 512], start=(k == 0), stop=(k == KC - 1))
                    mm.then_inc(unit_ready, 1)

            for i in range(4):
                memory(i)
            for g in range(4):
                base = U_POOL + g * PER_G

                def project(w, first):
                    for c in range(2):
                        for s, (at, n) in enumerate(SEGS):
                            b = begin(first + 3 * c + s)
                            for k in range(KC):
                                mm = nc.tensor.matmul(b[:, 0:n], w[:, k, c * P:(c + 1) * P], M.xT[:, k, at:at + n],
                                                      start=(k == 0), stop=(k == KC - 1))
                            mm.then_inc(unit_ready, 1)

                pe.wait_ge(wpool_in[0], 16 * (g + 1))
                project(wp, base)
                b = begin(base + 6)
                pe.wait_ge(unit_out, base + 6)
                pe.wait_ge(dve_step, DVE_ALL + g + 1)
                for c in range(2):
                    nc.tensor.transpose(b[0:NS, c * P:(c + 1) * P], pooled[:, c, SEQ:T], M.ident)
                    mm = nc.tensor.transpose(b[0:PM - 1, (2 + c) * P:(3 + c) * P], praw[:, c, SEQ:SEQ + PM - 1], M.ident)
                mm.then_inc(unit_ready, 1)
                pe.wait_ge(wpool_in[1], 16 * (g + 1))
                project(wg, base + 7)
                pe.wait_ge(wpool_in[2], 16 * (g + 1))
                pe.wait_ge(pooled_ready, g + 1)
                for c in range(2):
                    for s, (at, n) in enumerate(SEGS):
                        b = begin(base + 13 + 3 * c + s)
                        for k in range(2):
                            mm = nc.tensor.matmul(b[:, 0:n], wpool[:, k, c * P:(c + 1) * P], pooled[:, k, at:at + n],
                                                  start=(k == 0), stop=(k == 1))
                        mm.then_inc(unit_ready, 1)

        @block.scalar
        def _(act):
            def leave(unit):
                act.wait_ge(unit_ready, unit + 1)
                return bank[unit % 8]

            for t in range(NT + 2):
                n = nrow(t)
                for half in range(2):
                    b = leave(U_X + 2 * t + half)
                    v = b[:, :].rearrange("p (c n) -> p c n", n=P)[:, :, 0:n]
                    if t < NT:
                        dst = M.xT[:, 4 * half:4 * half + 4, t * P:t * P + n]
                    else:
                        dst = memT[:, 4 * half:4 * half + 4, (t - NT) * P:(t - NT + 1) * P]
                    nc.scalar.copy(dst, v).then_inc(unit_out, 1)
            b = leave(U_PAR)
            nc.scalar.copy(M.par[:, :], b[:, 0:R_ALL]).then_inc(unit_out, 1)
            for half in range(2):
                b = leave(U_SC + half)
                n = (CW - 1) * NB
                nc.scalar.copy(M.stateT[:, 12 * half:12 * half + 12, :], b[:, 0:12 * n].rearrange("p (c n) -> p c n", n=n)
                               ).then_inc(unit_out, 1)
            for half in range(2):
                b = leave(U_SP + half)
                n = (PM - 1) * NB
                nc.scalar.copy(statep[:, 4 * half:4 * half + 4, :], b[:, 0:4 * n].rearrange("p (c n) -> p c n", n=n)
                               ).then_inc(unit_out, 1)
            b = leave(U_AB)
            act.wait_ge(zeroed, 4)
            np_ = (NT - 1) * 2 * H
            nc.scalar.copy(ab[:, 0:NT - 1, :], b[:, 0:np_].rearrange("p (t n) -> p t n", n=2 * H))
            nc.scalar.copy(ab[0:NS, NT - 1, :], b[0:NS, np_:np_ + 2 * H]).then_inc(unit_out, 1)
            act.wait_ge(wab_in, 48)
            nc.scalar.activation(alog[:, :], alog[:, :], ACT.Exp).then_inc(act_step, 1)
            act.wait_ge(dve_step, DVE_ABS)
            nc.scalar.activation(u2[:, :, :], u2[:, :, :], ACT.Exp, scale=-1.0).then_inc(act_step, 1)
            act.wait_ge(act_step, 2)
            nc.scalar.activation(u2[:, :, :], u2[:, :, :], ACT.Ln, bias=1.0).then_inc(act_step, 1)
            act.wait_ge(unit_out, U_AB + 1)
            nc.scalar.activation(ab[:, :, H:2 * H], ab[:, :, H:2 * H], ACT.Tanh, scale=0.5).then_inc(act_step, 1)
            b = leave(U_GC)
            np_ = (NT - 1) * H
            nc.scalar.copy(M.scal[:, :, S_GC:S_GC + 8], b[:, 0:np_].rearrange("p (t h) -> p h t", h=H))
            nc.scalar.copy(M.scal[0:NS, :, S_GC + 8], b[0:NS, 128:128 + H])
            nc.scalar.copy(gl[:, 0:NT - 1, :], b[:, 64:64 + np_].rearrange("p (t h) -> p t h", h=H))
            nc.scalar.activation(M.scal[:, :, S_EGLS:S_EGLS + 8], b[:, 192:256].rearrange("p (b h) -> p h b", h=H), ACT.Exp)
            nc.scalar.activation(M.scal[:, :, S_EGL:S_EGL + 8], b[:, 64:64 + np_].rearrange("p (t h) -> p h t", h=H), ACT.Exp)
            nc.scalar.copy(gl[0:NS, NT - 1, :], b[0:NS, 136:136 + H]).then_inc(unit_out, 1)
            act.wait_ge(dve_step, DVE_ALL)
            nc.scalar.activation(M.scal[:, :, S_KG:S_KG + 9], M.scal[:, :, S_KG:S_KG + 9], ACT.Exp).then_inc(act_step, 1)
            nc.scalar.activation(M.scal[:, :, S_KBE:S_KBE + 9], M.scal[:, :, S_GC:S_GC + 9], ACT.Exp).then_inc(act_step, 1)
            for i in range(4):
                if i >= 2:
                    act.wait_ge(kv_out[i % 2], 16)
                for half in range(2):
                    b = leave(U_KV + 2 * i + half)
                    nc.scalar.copy(kvrow[:, i % 2, half * 512:(half + 1) * 512], b[:, :]).then_inc(unit_out, 1)
                out = O["mem_k"] if i < 2 else O["mem_v"]
                act.wait_ge(unit_out, U_KV + 2 * i + 2)
                act.dma_start(out[0, 0, (i % 2) * P:(i % 2 + 1) * P, :, :].rearrange("m h d -> m (h d)"),
                              kvrow[:, i % 2, :]).then_inc(kv_out[i % 2], 16)
            for g in range(4):
                base = U_POOL + g * PER_G
                if g:
                    act.wait_ge(pooled_ready, g)
                for c in range(2):
                    for s, (at, n) in enumerate(SEGS):
                        b = leave(base + 3 * c + s)
                        if at < SEQ:
                            nc.scalar.copy(praw[:, c, PM - 1 + at:PM - 1 + at + n], b[:, 0:n]).then_inc(unit_out, 1)
                        else:
                            nc.scalar.copy(psam[:, c, :, PM - 1:], b[:, 0:n].rearrange("p (b l) -> p b l", b=NB)
                                           ).then_inc(unit_out, 1)
                b = leave(base + 6)
                nc.scalar.copy(ptok[:, g * PG:(g + 1) * PG], b[0:NS, 0:PG])
                nc.scalar.copy(ptail[:, g * PG:(g + 1) * PG], b[0:PM - 1, PG:2 * PG]).then_inc(unit_out, 1)
                if g:
                    act.wait_ge(merged_ready, g)
                for c in range(2):
                    for s, (at, n) in enumerate(SEGS):
                        b = leave(base + 7 + 3 * c + s)
                        nc.scalar.activation(gate[:, c, at:at + n], b[:, 0:n], ACT.Tanh, scale=0.5).then_inc(unit_out, 1)
                act.wait_ge(dve_step, DVE_ALL + 1)
                for c in range(2):
                    for s, (at, n) in enumerate(SEGS):
                        b = leave(base + 13 + 3 * c + s)
                        nc.scalar.activation(M.mT[:, 2 * g + c, at:at + n], b[:, 0:n], ACT.Copy,
                                             scale=M.par[:, R_PS + 2 * g + c:R_PS + 2 * g + c + 1]).then_inc(unit_out, 1)

        @block.gpsimd
        def _(pool):
            nc.gpsimd.memset(ab[:, :, :], 0.0).then_inc(zeroed, 1)
            nc.gpsimd.memset(praw[:, :, 0:PM - 1], 0.0).then_inc(zeroed, 1)
            nc.gpsimd.memset(gl[:, :, :], 0.0).then_inc(zeroed, 1)
            nc.gpsimd.memset(M.scal[:, :, :], 0.0).then_inc(zeroed, 1)

        @block.vector
        def _(dve):
            link_sem = ctx.enter_context(nc.semaphore("a_link"))
            link_n = [0]

            def link(ins):
                link_n[0] += 1
                ins.then_inc(link_sem, 1)
                dve.wait_ge(link_sem, link_n[0])

            v = nc.vector
            dve.wait_ge(wab_in, 48)
            dve.wait_ge(unit_out, U_AB + 1)
            link(v.tensor_tensor(u[:, :, :], ab[:, :, 0:H], dtb[:, :].unsqueeze(1).to_broadcast((P, NT, H)), ALU.add))
            v.scalar_tensor_tensor(u2[:, :, :], u[:, :, :], -1.0, u[:, :, :], ALU.mult, ALU.max).then_inc(dve_step, 1)
            link(v.tensor_scalar(u[:, :, :], u[:, :, :], 0.0, None, ALU.max))
            dve.wait_ge(act_step, 3)
            link(v.tensor_tensor(u[:, :, :], u[:, :, :], u2[:, :, :], ALU.add))
            link(v.scalar_tensor_tensor(gtm[:, :, :], u[:, :, :], -1.0, alog[:, :].unsqueeze(1).to_broadcast((P, NT, H)),
                                        ALU.mult, ALU.mult))
            v.tensor_tensor(gseq[:, :, :], gtm[0:NS, NT - 1, :].unsqueeze(1).to_broadcast((NS, NB, H)),
                            M.inseq[0:NS, :].unsqueeze(2).to_broadcast((NS, NB, H)), ALU.mult).then_inc(dve_step, 1)
            dve.wait_ge(zeroed, 4)
            dve.wait_ge(act_step, 4)
            link(v.tensor_scalar(M.scal[:, :, S_BETA:S_BETA + 9], ab[:, :, H:2 * H].rearrange("p t h -> p h t"),
                                 0.5, 0.5, ALU.mult, ALU.add))
            dve.wait_ge(dve_step, DVE_G)
            v.tensor_copy(M.scal[:, :, S_G:S_G + 9], gtm[:, :, :].rearrange("p t h -> p h t"))
            dve.wait_ge(unit_out, U_GC + 1)
            v.tensor_tensor(M.scal[:, :, S_KG:S_KG + 9], gl[:, :, :].rearrange("p t h -> p h t"),
                            M.scal[:, :, S_GC:S_GC + 9], ALU.subtract).then_inc(dve_step, 1)
            dve.wait_ge(act_step, 6)
            link(v.tensor_tensor(M.scal[:, :, S_KBE:S_KBE + 9], M.scal[:, :, S_KBE:S_KBE + 9],
                                 M.scal[:, :, S_BETA:S_BETA + 9], ALU.mult))
            link(v.tensor_scalar(M.par[:, R_PS:R_ON], M.par[:, R_PS:R_ON], 0.5, None, ALU.mult))
            link(v.tensor_scalar(M.par[:, R_CONV:R_PS], M.par[:, R_CONV:R_PS], 0.5, None, ALU.mult))
            link(v.tensor_scalar(M.par[:, R_ON:R_ALL], M.par[:, R_ON:R_ALL], 0.25 * float(HD) ** 0.5, None, ALU.mult))
            for g in range(4):
                base = U_POOL + g * PER_G
                w = POOLW[g]
                v.tensor_copy(psam[:, :, :, 0:PM - 1], statep[:, 2 * g:2 * g + 2, :].rearrange("p c (b j) -> p c b j", b=NB))
                if g:
                    dve.wait_ge(unit_ready, base)
                dve.wait_ge(unit_out, base + 6)
                v.tensor_copy(pooled[:, :, SEQ:T].rearrange("p c (b l) -> p c b l", b=NB),
                              psam[:, :, :, PM - 1:]).then_inc(dve_step, 1)
                dve.wait_ge(dve_step, DVE_ALL + g + 1)
                a, s = praw, psam
                for lev in range(g + 1):
                    d = 1 << lev
                    lo = 2 * d - 1
                    for c in range(2):
                        dst = pw_a if lev % 2 == 0 else pooled
                        dc = dst[:, c, 0:PM - 1 + SEQ] if dst is pw_a else pooled[:, c, 0:PM - 1 + SEQ]
                        if c == 0 and lev % 2 == 1:
                            dve.wait_ge(unit_ready, base + 7)
                        v.tensor_tensor(dc[:, lo:], a[:, c, lo:PM - 1 + SEQ], a[:, c, lo - d:PM - 1 + SEQ - d], ALU.add)
                    sd = pw_as if lev % 2 == 0 else pw_bs
                    link(v.tensor_tensor(sd[:, :, :, lo:], s[:, :, :, lo:], s[:, :, :, lo - d:PM - 1 + DS - d], ALU.add))
                    a, s = dst, sd
                link(v.tensor_tensor(a[:, :, PM - 1:PM - 1 + w], a[:, :, PM - 1:PM - 1 + w],
                                     M.early[:, g, 0:w].unsqueeze(1).to_broadcast((P, 2, w)), ALU.mult))
                if a is pooled:
                    for c in range(2):
                        v.tensor_copy(pw_a[:, c, PM - 1:], pooled[:, c, PM - 1:PM - 1 + SEQ])
                    link(v.tensor_copy(pw_as[:, :, :, PM - 1:], s[:, :, :, PM - 1:]))
                dve.wait_ge(unit_ready, base + 7)
                for c in range(2):
                    v.scalar_tensor_tensor(pooled[:, c, 0:SEQ], pw_a[:, c, PM - 1:], 1.0 / w, praw[:, c, PM - 1:],
                                           ALU.mult, ALU.subtract)
                for c in range(2):
                    last = v.scalar_tensor_tensor(pooled[:, c, SEQ:T].rearrange("p (b l) -> p b l", b=NB), pw_as[:, c, :, PM - 1:],
                                                  1.0 / w, psam[:, c, :, PM - 1:], ALU.mult, ALU.subtract)
                last.then_inc(pooled_ready, 1)
                dve.wait_ge(pooled_ready, g + 1)
                dve.wait_ge(unit_out, base + PER_G)
                v.scalar_tensor_tensor(M.mT[:, 2 * g:2 * g + 2, :], gate[:, :, :], 1.0, M.mT[:, 2 * g:2 * g + 2, :],
                                       ALU.add, ALU.mult).then_inc(merged_ready, 1)
            dve.wait_ge(merged_ready, 4)


GROUPS = (("0", 4, LEVELS), ("1", 4, LEVELS), ("s", 1, SLEVELS))


def steps_b():
    pe, dv, ac, pl = [], [], [], []
    dv += ["head", "pack", "conv0", "conv1", "conv2", "silu1", "silu0", "silu2", "z", "nk", "nq"]
    ac += ["tanh1", "tanh0", "sqk", "sqq", "tanh2", "tz", "tga", "cst", "rk", "rq"]
    for g, c, levels in GROUPS:
        pe += ["T" + g, "M" + g]
        dv += ["row" + g, "dec" + g, "A" + g, "PT" + g]
        ac += ["eA" + g, "eT" + g, "eR" + g]
        pl += ["tri" + g, "eB" + g, "eM" + g, "qg" + g]
        for n in range(levels):
            pe += [f"Z{g}{n}"] + ([f"W{g}{n}"] if n else [])
            dv += [f"X{g}{n}"]
            ac += [f"Z{g}{n}"] if n else []
            pl += [f"off{g}{n}"]
        pe += ["w" + g]
        ac += ["w" + g]
        if g == "s":
            pe += ["us", "vs", "vt", "os", "kvs"]
            ac += ["ut", "vn"]
            dv += ["vnT", "vexp", "oTs", "Ss"]
            pl += ["sdec"]
        else:
            for i in range(c):
                pe += [f"v{g}{i}", f"kv{g}{i}", f"o{g}{i}"]
                ac += [f"v{g}{i}"]
                dv += [f"S{g}{i}"]
            ac += ["o" + g]
    ac += ["sqo", "ro"]
    dv += ["final"]
    return pe, dv, ac, pl


class Steps:

    def __init__(self, names, start=0):
        assert len(set(names)) == len(names)
        self.names = names
        self.per_head = len(names)
        self.start = start

    def before(self, h):
        return h * self.per_head + self.start

    def __call__(self, h, name):
        return h * self.per_head + (self.start + self.names.index(name) + 1)


FILL = {"T": 1, "M": 7, "Z0": 2, "Z": 1, "W": 2, "w": 1, "v": 1, "kv": 1,
        "sM": 6, "sZ0": 1, "sZ": 1, "sW": 1, "sw": 1, "sv": 1, "svt": 2, "end": 99}
U_FIRST = 15
U_PER = 24
NP_UNITS = 5 * len(SEGS)


def phase_b(nc, A, O, M):
    with ExitStack() as ctx:
        def sb(name, shape, dt=F32):
            return ctx.enter_context(nc.sbuf_tensor(name, shape, dt))

        def sem(name):
            return ctx.enter_context(nc.semaphore(name))

        ring = [ctx.enter_context(nc.psum_tensor(f"b_ring{i}", [P, 512], F32)) for i in range(2)]
        b2, b3, b4, b5, b6, b7 = (ctx.enter_context(nc.psum_tensor(f"b_bank{i}", [P, 512], F32)) for i in range(2, 8))
        win = sb("win", [P, 5, KC, P])
        raw = sb("raw", [P, 3, CW - 1 + SEQ])
        raws = sb("raws", [P, 3, NB, CW - 1 + DS])
        zraw = sb("zraw", [P, T])
        garaw = sb("garaw", [P, T])
        cur = sb("cur", [P, 3, T])
        zc = sb("zc", [P, T])
        gc = sb("gc", [P, T])
        tmp = sb("tmp", [P, 2, T])
        oT = sb("oT", [P, T])
        ssq = sb("ssq", [P, T])
        wch = sb("wch", [P, CW, 3])
        sch = sb("sch", [P, S_ALL])
        pack = sb("pack", [P, 3, 27])
        cst = sb("cst", [27, 3, P])
        kbe, kg, vb, ET, PT, qg, nw, Zs, X, XT, tri = (sb(n, [P, 4, P]) for n in
                                                      ("kbe", "kg", "vb", "ET", "PT", "qg", "nw", "Zs", "X", "XT", "tri"))
        ea_a = sb("ea_a", [P, 2, 4, P])
        EA, Am = ea_a[:, 0], ea_a[:, 1]
        vexp = ea_a[0:NS].rearrange("p a c n -> p (a c) n")
        off = sb("off", [P, 2, 4, P])
        nwq = sb("nwq", [P, NB, 2 * DS])
        ut = sb("ut", [P, NS])
        vnT = sb("vnT", [P, P])
        qS = sb("qS", [P, NS])
        vnew = sb("vnew", [P, 2, P])
        S = sb("S", [P, 2, P])
        Sb = sb("Sb", [P, NB, P])

        w_in = [sem(f"w_in{f}") for f in range(5)]
        sb_in = sem("sb_in")
        filled = sem("filled")
        pe_s, dv_s, ac_s, pl_s = sem("pe_step"), sem("dve_step_b"), sem("act_step_b"), sem("pool_step")
        unit_ready, unit_out = sem("b_unit_ready"), sem("b_unit_out")
        pre = sem("b_zeroed")
        conv_out, dp_out, ds_out = sem("conv_out"), sem("dp_out"), sem("ds_out")
        link_s = sem("b_link")
        plink_s = sem("b_plink")
        PE, DV, AC, PL = (Steps(x, 1) for x in steps_b())

        w_feat = [j * H * HD for j in range(3)] + [O_Z, O_GA]

        def w_src(f, j):
            v = A["w_in"][0, :, w_feat[f]:w_feat[f] + H * HD].rearrange("(c p) (h n) -> p c h n", p=P, n=P)
            return v[:, :, j, :]

        block = ctx.enter_context(nc.Block())

        @block.sync
        def _(sp):
            for j in range(1):
                for f in range(5):
                    sp.dma_start(win[:, f, :, :], w_src(f, 0)).then_inc(w_in[f], 16)
            for f in range(5):
                sp.wait_ge(unit_ready, 3 * f + 3)
                sp.dma_start(win[:, f, :, :], w_src(f, 1)).then_inc(w_in[f], 16)

            def body(h, load):
                sp.wait_ge(ds_out, 16 * h + 16)
                sp.dma_start(Sb[:, :, :], A["state_delta"][0].rearrange("b h k v -> k b h v")[:, :, h, :]).then_inc(sb_in, 16)
                sp.wait_ge(ac_s, AC(h, "cst"))
                cs = O["conv_sample"].rearrange("o b i (j h p) -> (o b i) j h p", j=3, p=P)
                cp = O["conv_prompt"].rearrange("o b i (j h p) -> (o b i) j h p", j=3, p=P)
                sp.dma_start(cs[:, :, h, :], cst[0:24, :, :]).then_inc(conv_out, 16)
                sp.dma_start(cp[:, :, h, :], cst[24:27, :, :]).then_inc(conv_out, 16)

                def load_w(f):
                    if load:
                        done = {0: 4, 1: 12, 2: 15, 3: 18, 4: 21}[f]
                        sp.wait_ge(unit_ready, h * U_PER + (U_FIRST + done))
                        sp.dma_start(win[:, f, :, :], w_src(f, h + 2)).then_inc(w_in[f], 16)

                load_w(0)
                load_w(1)
                load_w(2)
                sp.wait_ge(dv_s, DV(h, "S13"))
                sp.dma_start(O["delta_prompt"][0, 0, h, :, :], S[:, 0, :]).then_inc(dp_out, 16)
                load_w(3)
                load_w(4)
                rows = M.y_rows[bass.ds(h * FILL_ROWS + MIN_SLOTS, FILL_ROWS), :].rearrange("(c p) d -> p c d", p=P)
                src = M.const[:, 4:4 + D].unsqueeze(1).to_broadcast((P, FILL_ROWS // P, D))
                sp.dma_start(rows, src).then_inc(filled, 16)
                sp.wait_ge(dv_s, DV(h, "Ss"))
                sp.dma_start(O["delta_sample"][0].rearrange("b h k v -> k b h v")[:, :, h, :], Sb[:, :, :]).then_inc(ds_out, 16)

            for out, n in ((conv_out, 32), (dp_out, 16), (ds_out, 16)):
                sp.sem_inc(out, n)
            with sp.Fori(0, H - 2) as h:
                body(h, True)
            body(H - 2, False)
            body(H - 1, False)
            sp.wait_ge(conv_out, 32 * H + 32)
            sp.wait_ge(dp_out, 16 * H + 16)
            sp.wait_ge(ds_out, 16 * H + 16)
            sp.wait_ge(filled, 16 * H)

        @block.tensor
        def _(pe):
            mm = nc.tensor.matmul
            tr = nc.tensor.transpose
            pe.sem_inc(pe_s, 1)

            def proj_step(j, i, base, pos):
                unit, k = divmod(i, KC)
                f, s = divmod(unit, len(SEGS))
                at, n = SEGS[s]
                if k == 0:
                    if s == 0:
                        pe.wait_ge(w_in[f], (j + 1) * 16)
                    if isinstance(base, int) and base + pos < 2:
                        pass
                    else:
                        pe.wait_ge(unit_out, base + (pos - 1))
                m = mm(ring[pos % 2][:, 0:n], win[:, f, k, :], M.xT[:, k, at:at + n], start=(k == 0), stop=(k == KC - 1))
                if k == KC - 1:
                    m.then_inc(unit_ready, 1)

            for i in range(NP_UNITS * KC):
                proj_step(0, i, 0, i // KC)

            def body(h, more):
                base = h * U_PER
                pos = [U_FIRST]
                nxt = [0]

                def fill(n):
                    if not more:
                        return
                    for _ in range(n):
                        if nxt[0] == NP_UNITS * KC:
                            return
                        proj_step(h + 1, nxt[0], base, pos[0])
                        nxt[0] += 1
                        if nxt[0] % KC == 0:
                            pos[0] += 1

                def ring_bank():
                    pe.wait_ge(unit_out, base + (pos[0] - 1))
                    b = ring[pos[0] % 2]
                    pos[0] += 1
                    return b

                pe.wait_ge(dv_s, DV(h, "pack"))
                b = ring_bank()
                for j in range(3):
                    m = tr(b[0:27, j * P:(j + 1) * P], pack[:, j, :], M.ident)
                m.then_inc(unit_ready, 1)
                fill(3 * KC)
                pe.wait_ge(ac_s, AC(h, "sqk"))
                for half in range(2):
                    mm(ring_bank()[:, :], M.ones, tmp[:, 0, half * 512:half * 512 + 512], start=True, stop=True).then_inc(unit_ready, 1)
                pe.wait_ge(ac_s, AC(h, "sqq"))
                for half in range(2):
                    mm(ring_bank()[:, :], M.ones, tmp[:, 1, half * 512:half * 512 + 512], start=True, stop=True).then_inc(unit_ready, 1)
                mm(ring_bank()[:, 0:2 * NS].rearrange("p (a n) -> p a n", a=2), M.ones, tmp[:, :, SEQ:T],
                   start=True, stop=True).then_inc(unit_ready, 1)
                fill(3 * KC)

                for g, nch, levels in GROUPS:
                    smp = g == "s"
                    n = NS if smp else P
                    at = [SEQ] if smp else [(4 * int(g) + c) * P for c in range(4)]
                    f_ = (lambda key: FILL.get("s" + key, 0)) if smp else (lambda key: FILL.get(key, 0))
                    if g == "0":
                        pe.wait_ge(dv_s, DV(h, "nq"))
                    elif g == "1":
                        pe.wait_ge(dv_s, DV(h, "S03"))
                    else:
                        pe.wait_ge(dv_s, DV(h, "S13"))
                    for c in range(nch):
                        tr(b2[:, c * P:(c + 1) * P], cur[:, 1:3, :].rearrange("p j t -> p (j t)")[:, at[c]:at[c] + P], M.ident)
                    for c in range(nch):
                        m = tr(b3[0:n, c * P:(c + 1) * P], cur[:, 2, at[c]:at[c] + n], M.ident)
                    m.then_inc(pe_s, 1)
                    fill(f_("T"))
                    if g != "0":
                        pe.wait_ge(ac_s, AC(h, "o" + {"1": "0", "s": "1"}[g]))
                    for c in range(nch):
                        mm(b4[0:n, c * P:c * P + n], cur[:, 1, at[c]:at[c] + n], cur[:, 1, at[c]:at[c] + n], start=True, stop=True)
                        mm(b5[0:n, c * P:c * P + n], cur[:, 1, at[c]:at[c] + n], cur[:, 0, at[c]:at[c] + n], start=True, stop=True)
                    pe.wait_ge(pl_s, PL(h, "tri" + g))
                    for c in range(nch):
                        m = mm(b6[:, c * P:c * P + n], M.ones[0:n, :], tri[0:n, c, 0:n], start=True, stop=True)
                    m.then_inc(pe_s, 1)
                    fill(f_("M"))
                    pe.wait_ge(dv_s, DV(h, "row" + g))
                    for lev in range(levels):
                        pe.wait_ge(pl_s, PL(h, f"off{g}{lev}"))
                        if lev:
                            pe.wait_ge(dv_s, DV(h, f"X{g}{lev - 1}"))
                        for c in range(nch):
                            rhs = XT[0:n, c, 0:n] if lev else M.ident[0:n, 0:n]
                            m = mm(b2[:, c * P:c * P + n], off[0:n, lev % 2, c, :], rhs, start=True, stop=True)
                        m.then_inc(pe_s, 1)
                        if lev == 0:
                            fill(f_("Z0"))
                            continue
                        fill(f_("Z"))
                        pe.wait_ge(ac_s, AC(h, f"Z{g}{lev}"))
                        for c in range(nch):
                            m = mm(b3[:, c * P:c * P + n], X[0:n, c, :], Zs[0:n, c, 0:n], start=True, stop=True)
                        if lev < levels - 1:
                            for c in range(nch):
                                m = mm(b7[0:n, c * P:c * P + n], Zs[0:n, c, 0:n], X[0:n, c, 0:n], start=True, stop=True)
                        m.then_inc(pe_s, 1)
                        fill(f_("W"))
                    pe.wait_ge(dv_s, DV(h, f"X{g}{levels - 1}"))
                    for c in range(nch):
                        m = mm(b4[:, c * P:c * P + n], kbe[0:n, c, :], XT[0:n, c, 0:n], start=True, stop=True)
                    m.then_inc(pe_s, 1)
                    fill(f_("w"))
                    if smp:
                        break
                    for c in range(4):
                        cc = 4 * int(g) + c
                        if c == 0:
                            pe.wait_ge(dv_s, DV(h, "PT" + g))
                        mm(b5[:, 0:P], XT[:, c, :], vb[:, c, :], start=True, stop=False)
                        if c == 0:
                            pe.wait_ge(ac_s, AC(h, "w" + g))
                            pe.wait_ge(pl_s, PL(h, "qg" + g))
                        elif c or g == "1":
                            prev = f"S{g}{c - 1}"
                            pe.wait_ge(dv_s, DV(h, prev))
                        mm(b5[:, 0:P], nw[:, c, :], S[:, cc % 2, :], start=False, stop=True).then_inc(pe_s, 1)
                        mm(b6[:, c * P:(c + 1) * P], S[:, cc % 2, :], qg[:, c, :], start=True, stop=False)
                        fill(f_("v"))
                        pe.wait_ge(ac_s, AC(h, f"v{g}{c}"))
                        mm(b3[:, 0:P], kg[:, c, :], vnew[:, c % 2, :], start=True, stop=True).then_inc(pe_s, 1)
                        mm(b6[:, c * P:(c + 1) * P], vnew[:, c % 2, :], PT[:, c, :], start=False, stop=True).then_inc(pe_s, 1)
                        fill(f_("kv"))
                mm(b3[:, 0:NS], vb[0:NS, 0, :], XT[0:NS, 0, 0:NS], start=True, stop=True).then_inc(pe_s, 1)
                pe.wait_ge(sb_in, (h + 1) * 16)
                pe.wait_ge(ac_s, AC(h, "ws"))
                pe.wait_ge(pl_s, PL(h, "qgs"))
                pe.wait_ge(dv_s, DV(h, "PTs"))
                for b in range(NB):
                    m = mm(b5[:, b * 2 * DS:(b + 1) * 2 * DS], Sb[:, b, :], nwq[:, b, :], start=True, stop=True)
                m.then_inc(pe_s, 1)
                fill(FILL["sv"])
                pe.wait_ge(dv_s, DV(h, "vnT"))
                tr(b2[:, 0:P], vnT[:, :], M.ident).then_inc(pe_s, 1)
                fill(FILL["svt"])
                pe.wait_ge(ac_s, AC(h, "vn"))
                pe.wait_ge(ac_s, AC(h, "eRs"))
                mm(b6[:, 0:NS], vnew[0:NS, 0, :], PT[0:NS, 0, 0:NS], start=True, stop=True).then_inc(pe_s, 1)
                pe.wait_ge(dv_s, DV(h, "vexp"))
                mm(b3[:, :], kg[0:NS, 0, :], vexp[:, 0:4, :], start=True, stop=True)
                mm(b7[:, :], kg[0:NS, 0, :], vexp[:, 4:8, :], start=True, stop=True).then_inc(pe_s, 1)
                fill(FILL["end"])
                pe.wait_ge(ac_s, AC(h, "sqo"))
                for at, n in SEGS:
                    mm(ring_bank()[:, 0:n], M.ones, tmp[:, 0, at:at + n], start=True, stop=True).then_inc(unit_ready, 1)

            with pe.Fori(0, H - 1) as h:
                body(h, True)
            body(H - 1, False)

        @block.scalar
        def _(act):
            a = nc.scalar
            act.sem_inc(ac_s, 1)

            def proj_out(j, unit, base, pos):
                f, s = divmod(unit, len(SEGS))
                at, n = SEGS[s]
                act.wait_ge(unit_ready, base + (pos + 1))
                b = ring[pos % 2]
                if f < 3 and s < 2:
                    dst, src = raw[:, f, CW - 1 + at:CW - 1 + at + n], b[:, 0:n]
                elif f < 3:
                    dst, src = raws[:, f, :, CW - 1:], b[:, 0:n].rearrange("p (b l) -> p b l", b=NB)
                else:
                    dst, src = (zraw, garaw)[f - 3][:, at:at + n], b[:, 0:n]
                a.copy(dst, src).then_inc(unit_out, 1)

            act.wait_ge(pre, 2)
            for unit in range(NP_UNITS):
                proj_out(0, unit, 0, unit)

            def body(h, more):
                base = h * U_PER
                pos = [U_FIRST]
                nxt = [0]

                def fill(n):
                    if not more:
                        return
                    for _ in range(n):
                        if nxt[0] == NP_UNITS * KC:
                            return
                        nxt[0] += 1
                        if nxt[0] % KC == 0:
                            unit = nxt[0] // KC - 1
                            if unit % 3 == 0:
                                need = {0: "conv0", 1: "conv1", 2: "conv2", 3: "z"}.get(unit // 3)
                                if need:
                                    act.wait_ge(dv_s, DV(h, need))
                                else:
                                    act.wait_ge(ac_s, AC(h, "tga"))
                            proj_out(h + 1, unit, base, pos[0])
                            pos[0] += 1

                def leave():
                    act.wait_ge(unit_ready, base + (pos[0] + 1))
                    b = ring[pos[0] % 2]
                    pos[0] += 1
                    return b

                act.wait_ge(dv_s, DV(h, "conv1"))
                act.wait_ge(unit_out, base + U_FIRST)
                a.activation(tmp[:, 0, :], cur[:, 1, :], ACT.Tanh).then_inc(ac_s, 1)
                act.wait_ge(dv_s, DV(h, "conv0"))
                a.activation(tmp[:, 1, :], cur[:, 0, :], ACT.Tanh).then_inc(ac_s, 1)
                act.wait_ge(dv_s, DV(h, "silu1"))
                a.activation(tmp[:, 0, :], cur[:, 1, :], ACT.Square).then_inc(ac_s, 1)
                act.wait_ge(dv_s, DV(h, "silu0"))
                a.activation(tmp[:, 1, :], cur[:, 0, :], ACT.Square, scale=float(HD) ** 0.5).then_inc(ac_s, 1)
                act.wait_ge(dv_s, DV(h, "conv2"))
                a.activation(ssq[:, :], cur[:, 2, :], ACT.Tanh).then_inc(ac_s, 1)
                a.activation(zc[:, :], zraw[:, :], ACT.Tanh, scale=0.5).then_inc(ac_s, 1)
                a.activation(gc[:, :], garaw[:, :], ACT.Tanh, scale=0.5).then_inc(ac_s, 1)
                act.wait_ge(conv_out, 32 * h + 32)
                b = leave()
                a.copy(cst[:, :, :], b[0:27, 0:3 * P].rearrange("p (j n) -> p j n", j=3)).then_inc(unit_out, 1)
                act.wait_ge(unit_out, base + pos[0])
                a.nop().then_inc(ac_s, 1)
                fill(3 * KC)
                for half in range(2):
                    a.activation(oT[:, half * 512:half * 512 + 512], leave()[:, :], ACT.Ln, bias=M.eps).then_inc(unit_out, 1)
                act.wait_ge(dv_s, DV(h, "silu2"))
                for half in range(2):
                    a.activation(ssq[:, half * 512:half * 512 + 512], leave()[:, :], ACT.Ln, bias=M.epshd).then_inc(unit_out, 1)
                b = leave()
                a.activation(oT[:, SEQ:T], b[:, 0:NS], ACT.Ln, bias=M.eps)
                a.activation(ssq[:, SEQ:T], b[:, NS:2 * NS], ACT.Ln, bias=M.epshd).then_inc(unit_out, 1)
                act.wait_ge(unit_out, base + pos[0])
                a.activation(oT[:, :], oT[:, :], ACT.Exp, scale=-0.5).then_inc(ac_s, 1)
                a.activation(ssq[:, :], ssq[:, :], ACT.Exp, scale=-0.5).then_inc(ac_s, 1)
                fill(3 * KC)

                for g, nch, levels in GROUPS:
                    smp = g == "s"
                    n = NS if smp else P
                    f_ = (lambda key: FILL.get("s" + key, 0)) if smp else (lambda key: FILL.get(key, 0))
                    fill(f_("T"))

                    def grid(b, rows=n):
                        return b[0:rows, 0:nch * P].rearrange("p (c n) -> p c n", n=P)[:, :, 0:n]

                    act.wait_ge(dv_s, DV(h, "dec" + g))
                    a.activation(EA[0:n, 0:nch, 0:n], EA[0:n, 0:nch, 0:n], ACT.Exp).then_inc(ac_s, 1)
                    a.activation(ET[0:n, 0:nch, 0:n], ET[0:n, 0:nch, 0:n], ACT.Exp).then_inc(ac_s, 1)
                    a.activation(qg[:, 0:nch, 0:n], grid(b6, P), ACT.Exp).then_inc(ac_s, 1)
                    fill(f_("M"))
                    for lev in range(levels):
                        if lev == 0:
                            fill(f_("Z0"))
                            continue
                        act.wait_ge(pe_s, PE(h, f"Z{g}{lev}"))
                        a.copy(Zs[0:n, 0:nch, 0:n], grid(b2)).then_inc(ac_s, 1)
                        fill(f_("Z"))
                        fill(f_("W"))
                    act.wait_ge(pe_s, PE(h, "w" + g))
                    if smp:
                        a.mul(nwq[:, :, 0:DS], b4[:, 0:NS].rearrange("p (b l) -> p b l", b=NB), -1.0).then_inc(ac_s, 1)
                        fill(f_("w"))
                        break
                    a.mul(nw[:, :, :], grid(b4), -1.0).then_inc(ac_s, 1)
                    fill(f_("w"))
                    for c in range(4):
                        act.wait_ge(pe_s, PE(h, f"v{g}{c}"))
                        a.copy(vnew[:, c % 2, :], b5[:, 0:P]).then_inc(ac_s, 1)
                        fill(f_("v"))
                        fill(f_("kv"))
                    act.wait_ge(pe_s, PE(h, f"o{g}3"))
                    a.copy(oT[:, int(g) * 512:int(g) * 512 + 512], b6[:, :]).then_inc(ac_s, 1)
                act.wait_ge(pe_s, PE(h, "us"))
                a.copy(ut[:, :], b3[:, 0:NS]).then_inc(ac_s, 1)
                fill(FILL["sv"])
                act.wait_ge(pe_s, PE(h, "vt"))
                a.copy(vnew[0:NS, 0, :], b2[0:NS, 0:P]).then_inc(ac_s, 1)
                fill(FILL["svt"])
                fill(FILL["end"])
                act.wait_ge(dv_s, DV(h, "oTs"))
                a.activation(tmp[:, 0, :], oT[:, :], ACT.Square).then_inc(ac_s, 1)
                for at, n in SEGS:
                    a.activation(ssq[:, at:at + n], leave()[:, 0:n], ACT.Ln, bias=M.epshd).then_inc(unit_out, 1)
                act.wait_ge(unit_out, base + pos[0])
                a.activation(ssq[:, :], ssq[:, :], ACT.Exp, scale=-0.5).then_inc(ac_s, 1)

            with act.Fori(0, H - 1) as h:
                body(h, True)
            body(H - 1, False)

        @block.gpsimd
        def _(pool):
            g_ = nc.gpsimd
            pool.sem_inc(pl_s, 1)
            g_.memset(vnT[:, :], 0.0).then_inc(pre, 1)
            g_.memset(raw[:, :, 0:CW - 1], 0.0).then_inc(pre, 1)

            def body(h):
                for g, nch, levels in GROUPS:
                    smp = g == "s"
                    n = NS if smp else P
                    t0 = 8 if smp else 4 * int(g)
                    causal = M.upper8 if smp else M.upper

                    def col(base):
                        return sch[0:n, base + t0:base + t0 + nch].unsqueeze(2).to_broadcast((n, nch, n))

                    def cols(m):
                        return m[0:n, 0:n].unsqueeze(1).to_broadcast((n, nch, n))

                    pool.wait_ge(dv_s, DV(h, "head"))
                    if g != "0":
                        pool.wait_ge(pe_s, PE(h, "M" + {"1": "0", "s": "1"}[g]))
                    g_.tensor_tensor(tri[0:n, 0:nch, 0:n], cols(causal), col(S_G), ALU.mult).then_inc(pl_s, 1)
                    pool.wait_ge(ac_s, AC(h, "eA" + g))
                    g_.tensor_tensor(EA[0:n, 0:nch, 0:n], EA[0:n, 0:nch, 0:n], col(S_BETA), ALU.mult).then_inc(pl_s, 1)
                    pool.wait_ge(ac_s, AC(h, "eT" + g))
                    g_.tensor_tensor(ET[0:n, 0:nch, 0:n], ET[0:n, 0:nch, 0:n], cols(causal), ALU.mult).then_inc(pl_s, 1)
                    pool.wait_ge(ac_s, AC(h, "eR" + g))
                    if smp:
                        g_.tensor_tensor(nwq[:, :, DS:], qg[:, 0, 0:NS].rearrange("p (b l) -> p b l", b=NB),
                                         cur[:, 0, SEQ:T].rearrange("p (b l) -> p b l", b=NB), ALU.mult).then_inc(pl_s, 1)
                    else:
                        g_.tensor_tensor(qg[:, :, :], qg[:, :, :], cur[:, 0, int(g) * 512:int(g) * 512 + 512]
                                         .rearrange("p (c n) -> p c n", n=P), ALU.mult).then_inc(pl_s, 1)
                    for lev in range(levels):
                        if lev == 0:
                            pool.wait_ge(dv_s, DV(h, "A" + g))
                        if lev == 2:
                            pool.wait_ge(dv_s, DV(h, f"X{g}0"))
                        elif lev > 2:
                            pool.wait_ge(pe_s, PE(h, f"Z{g}{lev - 2}"))
                        g_.tensor_tensor(off[0:n, lev % 2, 0:nch, 0:n], Am[0:n, 0:nch, 0:n], cols(M.level[:, lev, :]),
                                         ALU.mult).then_inc(pl_s, 1)
                pool.wait_ge(pe_s, PE(h, "vs"))
                g_.tensor_tensor(Sb[:, :, :], Sb[:, :, :], sch[:, S_EGLS:S_EGLS + NB].unsqueeze(2).to_broadcast((P, NB, P)),
                                 ALU.mult).then_inc(pl_s, 1)

            with pool.Fori(0, H) as h:
                body(h)

        @block.vector
        def _(dve):
            v = nc.vector
            dve.sem_inc(dv_s, 1)

            def body(h):
                n_link = [0]

                def link(ins):
                    n_link[0] += 1
                    ins.then_inc(link_s, 1)
                    dve.wait_ge(link_s, n_link[0])

                dve.sem_clear(link_s)
                dve.wait_ge(pl_s, PL.before(h))
                dve.wait_ge(unit_out, h * U_PER + U_FIRST)
                v.tensor_copy(wch[:, :, :], M.par[:, R_CONV:R_PS].rearrange("p (i j h) -> p i j h", i=CW, j=3)[:, :, :, h])
                v.tensor_copy(raws[:, :, :, 0:CW - 1], M.stateT.rearrange("p (j h) n -> p j h n", j=3)[:, :, h, :]
                              .rearrange("p j (b i) -> p j b i", b=NB))
                v.tensor_copy(sch[:, :], M.scal[:, h, :]).then_inc(dv_s, 1)
                dve.wait_ge(dv_s, DV(h, "head"))
                v.tensor_copy(pack[:, :, 0:24].rearrange("p j (b i) -> p j b i", b=NB), raws[:, :, :, DS:])
                v.tensor_copy(pack[:, :, 24:27], raw[:, :, SEQ:]).then_inc(dv_s, 1)
                dve.wait_ge(pe_s, PE.before(h))
                dve.wait_ge(dp_out, 16 * h + 16)
                link(v.memset(S[:, 0, :], 0.0))
                for j in range(3):
                    cs = cur[:, j, SEQ:T].rearrange("p (b l) -> p b l", b=NB)
                    v.tensor_scalar(cur[:, j, 0:SEQ], raw[:, j, 0:SEQ], wch[:, 0, j:j + 1], None, ALU.mult)
                    link(v.tensor_scalar(cs, raws[:, j, :, 0:DS], wch[:, 0, j:j + 1], None, ALU.mult))
                    for i in range(1, CW):
                        v.scalar_tensor_tensor(cur[:, j, 0:SEQ], raw[:, j, i:i + SEQ], wch[:, i, j:j + 1],
                                               cur[:, j, 0:SEQ], ALU.mult, ALU.add)
                        ins = v.scalar_tensor_tensor(cs, raws[:, j, :, i:i + DS], wch[:, i, j:j + 1], cs, ALU.mult, ALU.add)
                        if i < CW - 1:
                            link(ins)
                    ins.then_inc(dv_s, 1)
                for j, name in ((1, "tanh1"), (0, "tanh0"), (2, "tanh2")):
                    dve.wait_ge(ac_s, AC(h, name))
                    src = ssq if j == 2 else tmp[:, 1 - j, :]
                    v.scalar_tensor_tensor(cur[:, j, :], src[:, :] if j == 2 else src, 1.0, cur[:, j, :],
                                           ALU.add, ALU.mult).then_inc(dv_s, 1)
                dve.wait_ge(ac_s, AC(h, "tz"))
                v.scalar_tensor_tensor(zc[:, :], zc[:, :], 1.0, zraw[:, :], ALU.add, ALU.mult).then_inc(dv_s, 1)
                dve.wait_ge(ac_s, AC(h, "rk"))
                v.tensor_tensor(cur[:, 1, :], cur[:, 1, :], oT[:, :], ALU.mult).then_inc(dv_s, 1)
                dve.wait_ge(ac_s, AC(h, "rq"))
                v.tensor_tensor(cur[:, 0, :], cur[:, 0, :], ssq[:, :], ALU.mult).then_inc(dv_s, 1)
                for g, nch, levels in GROUPS:
                    smp = g == "s"
                    n = NS if smp else P
                    t0 = 8 if smp else 4 * int(g)

                    def col(base, m):
                        return sch[0:n, base + t0:base + t0 + nch].unsqueeze(2).to_broadcast((n, nch, m))

                    def grid(b, m=n):
                        return b[0:n, 0:nch * P].rearrange("p (c n) -> p c n", n=P)[:, :, 0:m]

                    dve.wait_ge(pe_s, PE(h, "T" + g))
                    v.tensor_tensor(kbe[0:n, 0:nch, :], grid(b2, P), col(S_KBE, P), ALU.mult)
                    v.tensor_tensor(kg[0:n, 0:nch, :], grid(b2, P), col(S_KG, P), ALU.mult)
                    v.tensor_tensor(vb[0:n, 0:nch, :], grid(b3, P), col(S_BETA, P), ALU.mult).then_inc(dv_s, 1)
                    dve.wait_ge(pe_s, PE(h, "M" + g))
                    link(v.tensor_tensor(EA[0:n, 0:nch, 0:n], grid(b6), col(S_GC, n), ALU.subtract))
                    link(v.tensor_scalar(ET[0:n, 0:nch, 0:n], EA[0:n, 0:nch, 0:n], 0.0, None, ALU.min))
                    v.tensor_scalar(EA[0:n, 0:nch, 0:n], EA[0:n, 0:nch, 0:n], -1.0, 0.0, ALU.mult, ALU.min).then_inc(dv_s, 1)
                    dve.wait_ge(pl_s, PL(h, "eB" + g))
                    v.tensor_tensor(Am[0:n, 0:nch, 0:n], grid(b4), EA[0:n, 0:nch, 0:n], ALU.mult).then_inc(dv_s, 1)
                    dve.wait_ge(pl_s, PL(h, "eM" + g))
                    v.tensor_tensor(PT[0:n, 0:nch, 0:n], grid(b5), ET[0:n, 0:nch, 0:n], ALU.mult).then_inc(dv_s, 1)
                    ident = M.ident[0:n, 0:n].unsqueeze(1).to_broadcast((n, nch, n))
                    for lev in range(levels):
                        if lev == 0:
                            dve.wait_ge(pe_s, PE(h, f"Z{g}0"))
                            v.tensor_tensor(XT[0:n, 0:nch, 0:n], ident, grid(b2), ALU.subtract)
                            v.tensor_tensor(X[0:n, 0:nch, 0:n], ident, off[0:n, 0, 0:nch, 0:n], ALU.subtract).then_inc(dv_s, 1)
                            continue
                        dve.wait_ge(dv_s, DV(h, f"X{g}{lev - 1}"))
                        dve.wait_ge(pe_s, PE(h, f"W{g}{lev}"))
                        ins = v.tensor_tensor(XT[0:n, 0:nch, 0:n], XT[0:n, 0:nch, 0:n], grid(b3), ALU.subtract)
                        if lev < levels - 1:
                            ins = v.tensor_tensor(X[0:n, 0:nch, 0:n], X[0:n, 0:nch, 0:n], grid(b7), ALU.subtract)
                        ins.then_inc(dv_s, 1)
                    if smp:
                        break
                    for c in range(4):
                        cc = 4 * int(g) + c
                        if c or g == "1":
                            prev = f"S{g}{c - 1}" if c else "S03"
                            dve.wait_ge(dv_s, DV(h, prev))
                        dve.wait_ge(pe_s, PE(h, f"kv{g}{c}"))
                        v.scalar_tensor_tensor(S[:, (cc + 1) % 2, :], S[:, cc % 2, :], sch[:, S_EGL + cc:S_EGL + cc + 1],
                                               b3[:, 0:P], ALU.mult, ALU.add).then_inc(dv_s, 1)
                dve.wait_ge(ac_s, AC(h, "ut"))
                dve.wait_ge(pe_s, PE(h, "vs"))
                sv = b5[:, 0:2 * NS].rearrange("p (b l) -> p b l", b=NB)
                v.tensor_copy(qS.rearrange("p (b l) -> p b l", b=NB), sv[:, :, DS:])
                v.tensor_tensor(vnT[:, 0:NS].rearrange("p (b l) -> p b l", b=NB), sv[:, :, 0:DS],
                                ut.rearrange("p (b l) -> p b l", b=NB), ALU.add).then_inc(dv_s, 1)
                dve.wait_ge(ac_s, AC(h, "vn"))
                v.tensor_tensor(vexp, vnew[0:NS, 0, :].unsqueeze(1).to_broadcast((NS, NB, P)),
                                M.inseq[0:NS, :].unsqueeze(2).to_broadcast((NS, NB, P)), ALU.mult).then_inc(dv_s, 1)
                dve.wait_ge(pe_s, PE(h, "os"))
                v.tensor_tensor(oT[:, SEQ:T], b6[:, 0:NS], qS[:, :], ALU.add).then_inc(dv_s, 1)
                dve.wait_ge(pe_s, PE(h, "kvs"))
                dve.wait_ge(pl_s, PL(h, "sdec"))
                v.tensor_tensor(Sb[:, 0:4, :], Sb[:, 0:4, :], b3[:, :].rearrange("p (b n) -> p b n", n=P), ALU.add)
                v.tensor_tensor(Sb[:, 4:8, :], Sb[:, 4:8, :], b7[:, :].rearrange("p (b n) -> p b n", n=P), ALU.add).then_inc(dv_s, 1)
                dve.wait_ge(ac_s, AC(h, "ro"))
                link(v.tensor_tensor(oT[:, :], oT[:, :], ssq[:, :], ALU.mult))
                link(v.scalar_tensor_tensor(oT[:, :], oT[:, :], M.par[:, R_ON:R_ALL], zc[:, :], ALU.mult, ALU.mult))
                link(v.scalar_tensor_tensor(oT[:, :], gc[:, :], 1.0, oT[:, :], ALU.add, ALU.mult))
                v.tensor_tensor(M.mT[:, h, :], M.mT[:, h, :], oT[:, :], ALU.add).then_inc(dv_s, 1)
                dve.wait_ge(dv_s, DV(h, "final"))

            with dve.Fori(0, H - 1) as h:
                body(h)
            body(H - 1)


def layer_norm_rows(v, link, r, stats, mv, n):
    v.bn_stats(stats[0:n, 0, :], r[0:n, 0:512])
    link(v.bn_stats(stats[0:n, 1, :], r[0:n, 512:D]))
    return v.bn_aggr(mv[0:n, :], stats[0:n, :, :])


def steps_c():
    pe, dv, ac, pl = [], [], [], []
    for t in range(NT):
        pe += [f"y{t}"]
        dv += [f"r{t}", f"v{t}", f"n{t}"]
        ac += [f"s{t}"]
        pl += [f"x{t}"]
        if t:
            pe += [f"t{t - 1}"]
            ac += [f"t{t - 1}"]
    pe += [f"t{NT - 1}", "kt"]
    ac += [f"t{NT - 1}", "kt"]
    for u in range(KC * len(SEGS)):
        pe += [f"q{u}"]
        ac += [f"q{u}"]
    pl += ["qpad"]
    for t in range(NT - 1):
        pe += [f"S{t}"]
        dv += [f"m{t}"]
        ac += [f"e{t}"]
        dv += [f"p{t}"]
        if t:
            pe += [f"Y{t - 1}"]
            dv += [f"R{t - 1}", f"V{t - 1}", f"N{t - 1}"]
            ac += [f"s_{t - 1}"]
            pl += [f"X{t - 1}"]
        if t > 1:
            pe += [f"T{t - 2}"]
            ac += [f"T{t - 2}"]
            pe += [f"G{t - 2}"]
            ac += [f"G{t - 2}"]
        pe += [f"P{t}", f"O{t}"]
        ac += [f"P{t}", f"O{t}"]
    t = NT - 1
    pe += [f"Y{t - 1}"]
    dv += [f"R{t - 1}", f"V{t - 1}", f"N{t - 1}"]
    ac += [f"s_{t - 1}"]
    pl += [f"X{t - 1}"]
    for b in range(NB):
        pe += [f"K{b}", f"s{b}", f"p{b}", f"o{b}"]
        ac += [f"K{b}", f"e_{b}", f"p{b}", f"o{b}"]
        dv += [f"m_{b}", f"p_{b}"]
    for i in (t - 2, t - 1):
        pe += [f"T{i}", f"G{i}"]
        ac += [f"T{i}", f"G{i}"]
    pe += [f"Y{t}"]
    dv += [f"R{t}", f"V{t}", f"N{t}"]
    ac += [f"s_{t}"]
    pl += [f"X{t}"]
    pe += [f"T{t}", f"G{t}"]
    ac += [f"T{t}", f"G{t}"]
    return pe, dv, ac, pl


def phase_c(nc, A, O, M):
    with ExitStack() as ctx:
        def sb(name, shape, dt=F32):
            return ctx.enter_context(nc.sbuf_tensor(name, shape, dt))

        def sem(name):
            return ctx.enter_context(nc.semaphore(name))

        bank = [ctx.enter_context(nc.psum_tensor(f"c_bank{i}", [P, 512], F32)) for i in range(8)]
        w0 = sb("w0", [P, KC, D])
        w1 = sb("w1", [P, KC, D])
        kvb = w1[:, :, :].rearrange("p (s a m) n -> p s a m n", s=2, a=2)
        lng = sb("lng", [P, D])
        lnb = sb("lnb", [P, D])
        xrow = sb("xrow", [P, 2, D])
        r = sb("r", [P, 2, D])
        xo = sb("xo", [P, 2, D])
        kT = sb("kT", [P, KC, MEM])
        vm = sb("vm", [P, 2, D])
        pr = sb("pr", [P, CAH, MEM])
        prT = sb("prT", [P, 2, CAH, P])
        oTt = sb("oTt", [P, KC, P])
        qs = sb("qs", [P, KC, NS + 32])
        wr = sb("wr", [P, KC, EG + E])
        stats = sb("stats", [P, 2, 6])
        mv = sb("mv", [P, 2])
        rs = sb("rs", [P, 2])
        mx = sb("mx", [P, 2, CAH])
        sm = sb("sm", [P, 2, CAH])
        qT = M.mT

        w0_in, w1_in, ln_in, km_in, wr_in = sem("w0_in"), sem("w1_in"), sem("ln_in"), sem("km_in"), sem("wr_in")
        xr_in = [sem(f"xr_in{i}") for i in range(2)]
        kv_in = [sem(f"kv_in{i}") for i in range(2)]
        x_out = [sem(f"x_out{i}") for i in range(2)]
        pe_s, dv_s, ac_s, pl_s = sem("c_pe"), sem("c_dve"), sem("c_act"), sem("c_pool")
        link_s, alink_s, plink_s = sem("c_link"), sem("c_alink"), sem("c_plink")
        st = [Steps(x) for x in steps_c()]
        PE, DV, AC, PL = ((lambda name, s=s: s(0, name)) for s in st)

        def rows(ap, t):
            return ap[t * P:t * P + rows_of(t), :]

        def src(t):
            return A["x_prompt"][0, t * P:(t + 1) * P, :] if t < NT - 1 else A["x_sample"].rearrange("b l d -> (b l) d")

        def load_kv(sp, b):
            for i, name in enumerate(("cache_mem_k", "cache_mem_v")):
                sp.dma_start(kvb[:, b % 2, i, :, :], A[name][0, b].rearrange("(m p) h d -> p m (h d)", p=P)
                             ).then_inc(kv_in[b % 2], 16)

        block = ctx.enter_context(nc.Block())

        @block.sync
        def _(sp):
            sp.dma_start(w0[:, :, :], A["w_out"][0].rearrange("(c p) n -> p c n", p=P)).then_inc(w0_in, 16)
            sp.dma_start(lng[:, :], A["ln1_g"].to_broadcast((P, D))).then_inc(ln_in, 16)
            sp.dma_start(lnb[:, :], A["ln1_b"].to_broadcast((P, D))).then_inc(ln_in, 16)
            for t in range(NT):
                if t >= 2:
                    sp.wait_ge(dv_s, DV(f"r{t - 2}"))
                sp.dma_start(xrow[0:rows_of(t), t % 2, :], src(t)).then_inc(xr_in[t % 2], 16)
                if t == 0:
                    sp.dma_start(w1[:, :, :], A["w_cq"][0].rearrange("(c p) n -> p c n", p=P)).then_inc(w1_in, 16)
                    sp.dma_start(vm[:, :, :], O["mem_v"][0, 0].rearrange("(m p) h d -> p m (h d)", p=P)).then_inc(km_in, 16)
                    sp.dma_start(oTt[:, :, :].rearrange("p (m a) n -> p m (a n)", m=2),
                                 O["mem_k"][0, 0, :, 0:2].rearrange("(m p) h d -> p m (h d)", p=P)).then_inc(km_in, 16)
                    sp.dma_start(prT[:, :, :, :].rearrange("p m h n -> p m (h n)"),
                                 O["mem_k"][0, 0, :, 2:4].rearrange("(m p) h d -> p m (h d)", p=P)).then_inc(km_in, 16)
                    sp.dma_start(wr[:, :, 0:EG], A["w_router_group"][0].rearrange("(c p) n -> p c n", p=P)).then_inc(wr_in, 16)
                    sp.dma_start(wr[:, :, EG:], A["w_router_expert"][0].rearrange("(c p) n -> p c n", p=P)).then_inc(wr_in, 16)
                if t >= 1:
                    sp.wait_ge(pl_s, PL(f"x{t - 1}"))
                    sp.dma_start(rows(M.x1d, t - 1), xo[0:rows_of(t - 1), (t - 1) % 2, :]).then_inc(x_out[(t - 1) % 2], 16)
            t = NT - 1
            sp.wait_ge(pl_s, PL(f"x{t}"))
            sp.dma_start(rows(M.x1d, t), xo[0:rows_of(t), t % 2, :]).then_inc(x_out[t % 2], 16)
            sp.dma_start(lng[:, :], A["ln2_g"].to_broadcast((P, D))).then_inc(ln_in, 16)
            sp.dma_start(lnb[:, :], A["ln2_b"].to_broadcast((P, D))).then_inc(ln_in, 16)
            sp.wait_ge(pe_s, PE(f"y{t}"))
            sp.dma_start(w0[:, :, :], A["w_co"][0].rearrange("(c p) n -> p c n", p=P)).then_inc(w0_in, 16)
            sp.wait_ge(x_out[0], 16 * 5)
            sp.wait_ge(x_out[1], 16 * 4)
            for t in range(NT):
                i = NT + t
                sp.wait_ge(dv_s, DV(f"r{NT - 2 + t}") if t < 2 else DV(f"R{t - 2}"))
                sp.dma_start(xrow[0:rows_of(t), i % 2, :], rows(M.x1d, t)).then_inc(xr_in[i % 2], 16)
                if t == 1:
                    sp.wait_ge(pe_s, PE(f"q{KC * len(SEGS) - 1}"))
                    for b in range(2):
                        load_kv(sp, b)
                if t >= 1:
                    sp.wait_ge(pl_s, PL(f"X{t - 1}"))
                    sp.dma_start(rows(M.x2d, t - 1), xo[0:rows_of(t - 1), (i - 1) % 2, :]).then_inc(x_out[(i - 1) % 2], 16)
            for b in range(2, NB):
                sp.wait_ge(pe_s, PE(f"o{b - 2}"))
                load_kv(sp, b)
            t = NT - 1
            sp.wait_ge(pl_s, PL(f"X{t}"))
            sp.dma_start(rows(M.x2d, t), xo[0:rows_of(t), (NT + t) % 2, :]).then_inc(x_out[(NT + t) % 2], 16)
            sp.wait_ge(x_out[0], 16 * 9)
            sp.wait_ge(x_out[1], 16 * 9)

        @block.tensor
        def _(pe):
            mm, tr = nc.tensor.matmul, nc.tensor.transpose

            def wide(t, lhs, i, w):
                n = rows_of(t)
                for half in range(2):
                    for k in range(KC):
                        m = mm(bank[2 * (i % 2) + half][0:n, :], lhs(k), w[:, k, half * 512:(half + 1) * 512],
                               start=(k == 0), stop=(k == KC - 1))
                m.then_inc(pe_s, 1)

            def rows_T(t, i):
                n = rows_of(t)
                for k in range(KC):
                    m = tr(bank[4 + k // 4][:, (k % 4) * P:(k % 4) * P + n], xo[0:n, i % 2, k * P:(k + 1) * P], M.ident[0:n, 0:n])
                m.then_inc(pe_s, 1)

            def x1_T(t):
                pe.wait_ge(pl_s, PL(f"x{t}"))
                if t:
                    pe.wait_ge(ac_s, AC(f"t{t - 1}"))
                rows_T(t, t)

            pe.wait_ge(w0_in, 16)
            for t in range(NT):
                if t >= 2:
                    pe.wait_ge(dv_s, DV(f"r{t - 2}"))
                n = rows_of(t)
                wide(t, lambda k: M.mT[:, k, t * P:t * P + n], t, w0)
                if t:
                    x1_T(t - 1)
            x1_T(NT - 1)
            pe.wait_ge(km_in, 48)
            pe.wait_ge(ac_s, AC(f"t{NT - 1}"))
            kr = (oTt[:, :, :].rearrange("p (m a) n -> p m (a n)", m=2), prT[:, :, :, :].rearrange("p m h n -> p m (h n)"))
            for m_ in range(2):
                for k in range(KC):
                    m = tr(bank[4 + k // 2][:, (k % 2) * MEM + m_ * P:(k % 2) * MEM + (m_ + 1) * P],
                           kr[k // 4][:, m_, (k % 4) * P:(k % 4 + 1) * P], M.ident)
            m.then_inc(pe_s, 1)
            pe.wait_ge(w1_in, 16)
            for c in range(KC):
                for s, (at, n) in enumerate(SEGS):
                    u = 3 * c + s
                    if u < 2:
                        pe.wait_ge(ac_s, AC("kt"))
                    else:
                        pe.wait_ge(ac_s, AC(f"q{u - 2}"))
                    for k in range(KC):
                        m = mm(bank[6 + u % 2][:, 0:n], w1[:, k, c * P:(c + 1) * P], M.xT[:, k, at:at + n],
                               start=(k == 0), stop=(k == KC - 1))
                    m.then_inc(pe_s, 1)
            pe.wait_ge(ac_s, AC(f"q{KC * len(SEGS) - 1}"))
            pe.wait_ge(w0_in, 32)

            def out(t):
                if t < 2:
                    pe.wait_ge(dv_s, DV(f"r{NT - 2 + t}"))
                else:
                    pe.wait_ge(dv_s, DV(f"R{t - 2}"))
                pe.wait_ge(ac_s, AC(f"O{t}") if t < NT - 1 else AC(f"o{NB - 1}"))
                wide(t, lambda k: oTt[:, k, 0:rows_of(t)], NT + t, w0)

            def route(t, last):
                pe.wait_ge(pl_s, PL(f"X{t}"))
                pe.wait_ge(ac_s, last)
                rows_T(t, NT + t)
                pe.wait_ge(ac_s, AC(f"T{t}"))
                if t == 0:
                    pe.wait_ge(wr_in, 32)
                n = rows_of(t)
                for k in range(KC):
                    m = mm(bank[6][0:n, 0:EG + E], M.xT[:, k, t * P:t * P + n], wr[:, k, :], start=(k == 0), stop=(k == KC - 1))
                m.then_inc(pe_s, 1)

            for t in range(NT - 1):
                if t:
                    pe.wait_ge(ac_s, AC(f"O{t - 1}"))
                for h in range(CAH):
                    for k in range(2):
                        m = mm(bank[6 + h // 2][:, (h % 2) * MEM:(h % 2 + 1) * MEM], qT[:, 2 * h + k, t * P:(t + 1) * P],
                               kT[:, 2 * h + k, :], start=(k == 0), stop=(k == 1))
                m.then_inc(pe_s, 1)
                if t:
                    out(t - 1)
                pe.wait_ge(ac_s, AC(f"e{t}"))
                if t > 1:
                    route(t - 2, AC(f"P{t - 1}"))
                pe.wait_ge(dv_s, DV(f"p{t}"))
                if t > 1:
                    pe.wait_ge(ac_s, AC(f"G{t - 2}"))
                elif t:
                    pe.wait_ge(ac_s, AC(f"P{t - 1}"))
                for h in range(CAH):
                    for k in range(2):
                        m = tr(bank[4 + k][:, h * P:(h + 1) * P], pr[:, h, k * P:(k + 1) * P], M.ident)
                m.then_inc(pe_s, 1)
                pe.wait_ge(ac_s, AC(f"P{t}"))
                for c in range(KC):
                    for k in range(2):
                        m = mm(bank[6 + c // 4][:, (c % 4) * P:(c % 4 + 1) * P], vm[:, k, c * P:(c + 1) * P],
                               prT[:, k, c // 2, :], start=(k == 0), stop=(k == 1))
                m.then_inc(pe_s, 1)
            out(NT - 2)
            for b in range(NB):
                s = b % 2
                pe.wait_ge(kv_in[s], 32 * (b // 2 + 1))
                if b == 0:
                    pe.wait_ge(ac_s, AC(f"O{NT - 2}"))
                for k in range(KC):
                    for m_ in range(2):
                        m = tr(bank[(4, 5, 6, 7)[k // 2]][:, (k % 2) * MEM + m_ * P:(k % 2) * MEM + (m_ + 1) * P],
                               kvb[:, s, 0, m_, k * P:(k + 1) * P], M.ident)
                m.then_inc(pe_s, 1)
                pe.wait_ge(ac_s, AC(f"K{b}"))
                pe.wait_ge(pl_s, PL("qpad"))
                for h in range(CAH):
                    for k in range(2):
                        m = mm(bank[4][32 * h:32 * h + 32, 0:MEM], qs[:, 2 * h + k, b * DS:b * DS + 32], kT[:, 2 * h + k, :],
                               start=(k == 0), stop=(k == 1))
                m.then_inc(pe_s, 1)
                pe.wait_ge(dv_s, DV(f"p_{b}"))
                for k in range(2):
                    m = tr(bank[5][:, k * P:(k + 1) * P], pr[:, 0, k * P:(k + 1) * P], M.ident)
                m.then_inc(pe_s, 1)
                pe.wait_ge(ac_s, AC(f"p{b}"))
                for c in range(KC):
                    for k in range(2):
                        m = mm(bank[6][:, c * DS:(c + 1) * DS], kvb[:, s, 1, k, c * P:(c + 1) * P],
                               prT[:, k, 0, 32 * (c // 2):32 * (c // 2) + DS], start=(k == 0), stop=(k == 1))
                m.then_inc(pe_s, 1)
                pe.wait_ge(ac_s, AC(f"o{b}"))
            t = NT - 1
            route(t - 2, AC(f"o{NB - 1}"))
            pe.wait_ge(ac_s, AC(f"G{t - 2}"))
            route(t - 1, AC(f"G{t - 2}"))
            out(t)
            pe.wait_ge(ac_s, AC(f"G{t - 1}"))
            route(t, AC(f"G{t - 1}"))

        @block.scalar
        def _(act):
            a = nc.scalar
            n_link = [0]

            def link(ins):
                n_link[0] += 1
                ins.then_inc(alink_s, 1)
                act.wait_ge(alink_s, n_link[0])

            def rstd(t, name):
                n = rows_of(t)
                act.wait_ge(dv_s, DV(name))
                link(a.activation(rs[0:n, 0:1], mv[0:n, 1:2], ACT.Ln, bias=M.lneps[0:n]))
                a.activation(rs[0:n, 1:2], rs[0:n, 0:1], ACT.Exp, scale=-0.5).then_inc(ac_s, 1)

            def rows_T(t, name, before):
                n = rows_of(t)
                act.wait_ge(pe_s, PE(name))
                for half in range(2):
                    ins = a.copy(M.xT[:, 4 * half:4 * half + 4, t * P:t * P + n],
                                 bank[4 + half][:, :].rearrange("p (c n) -> p c n", n=P)[:, :, 0:n])
                ins.then_inc(ac_s, 1)

            for t in range(NT):
                rstd(t, f"v{t}")
                if t:
                    rows_T(t - 1, f"t{t - 1}", None)
            rows_T(NT - 1, f"t{NT - 1}", None)
            act.wait_ge(pe_s, PE("kt"))
            for i in range(4):
                ins = a.copy(kT[:, 2 * i:2 * i + 2, :], bank[4 + i][:, :].rearrange("p (c n) -> p c n", n=MEM))
            ins.then_inc(ac_s, 1)
            for c in range(KC):
                for s, (at, n) in enumerate(SEGS):
                    u = 3 * c + s
                    act.wait_ge(pe_s, PE(f"q{u}"))
                    dst = qT[:, c, at:at + n] if at < SEQ else qs[:, c, 0:n]
                    a.copy(dst, bank[6 + u % 2][:, 0:n]).then_inc(ac_s, 1)

            def route(t):
                rows_T(t, f"T{t}", None)
                n = rows_of(t)
                act.wait_ge(pe_s, PE(f"G{t}"))
                a.copy(M.logits[0:n, t, :], bank[6][0:n, 0:EG + E]).then_inc(ac_s, 1)

            scale = float(CAD) ** -0.5
            for t in range(NT - 1):
                act.wait_ge(dv_s, DV(f"m{t}"))
                for h in range(CAH):
                    ins = a.activation(pr[:, h, :], bank[6 + h // 2][:, (h % 2) * MEM:(h % 2 + 1) * MEM], ACT.Exp,
                                       bias=mx[:, 1, h:h + 1], scale=scale, accum_out=sm[:, 0, h:h + 1])
                ins.then_inc(ac_s, 1)
                if t:
                    rstd(t - 1, f"V{t - 1}")
                if t > 1:
                    route(t - 2)
                act.wait_ge(pe_s, PE(f"P{t}"))
                for k in range(2):
                    ins = a.copy(prT[:, k, :, :], bank[4 + k][:, :].rearrange("p (h n) -> p h n", n=P))
                ins.then_inc(ac_s, 1)
                act.wait_ge(pe_s, PE(f"O{t}"))
                for k in range(2):
                    ins = a.copy(oTt[:, 4 * k:4 * k + 4, :], bank[6 + k][:, :].rearrange("p (h n) -> p h n", n=P))
                ins.then_inc(ac_s, 1)
            rstd(NT - 2, f"V{NT - 2}")
            for b in range(NB):
                act.wait_ge(pe_s, PE(f"K{b}"))
                for i in range(4):
                    ins = a.copy(kT[:, 2 * i:2 * i + 2, :], bank[4 + i][:, :].rearrange("p (c n) -> p c n", n=MEM))
                ins.then_inc(ac_s, 1)
                act.wait_ge(dv_s, DV(f"m_{b}"))
                a.activation(pr[:, 0, :], bank[4][:, 0:MEM], ACT.Exp, bias=mx[:, 1, 0:1], scale=scale,
                             accum_out=sm[:, 0, 0:1]).then_inc(ac_s, 1)
                act.wait_ge(pe_s, PE(f"p{b}"))
                a.copy(prT[:, :, 0, :], bank[5][:, 0:2 * P].rearrange("p (k n) -> p k n", n=P)).then_inc(ac_s, 1)
                act.wait_ge(pe_s, PE(f"o{b}"))
                a.copy(oTt[:, :, b * DS:(b + 1) * DS], bank[6][:, 0:KC * DS].rearrange("p (c l) -> p c l", l=DS)).then_inc(ac_s, 1)
            t = NT - 1
            route(t - 2)
            route(t - 1)
            rstd(t, f"V{t}")
            route(t)

        @block.gpsimd
        def _(pool):
            g_ = nc.gpsimd
            n_link = [0]

            def link(ins):
                n_link[0] += 1
                ins.then_inc(plink_s, 1)
                pool.wait_ge(plink_s, n_link[0])

            def affine(t, i, name, tname):
                n = rows_of(t)
                pool.wait_ge(dv_s, DV(name))
                if i >= 2:
                    pool.wait_ge(x_out[i % 2], 16 * (i // 2))
                if tname:
                    pool.wait_ge(pe_s, PE(tname))
                link(g_.tensor_tensor(xo[0:n, i % 2, :], r[0:n, i % 2, :], lng[0:n, :], ALU.mult))
                g_.tensor_tensor(xo[0:n, i % 2, :], xo[0:n, i % 2, :], lnb[0:n, :], ALU.add).then_inc(pl_s, 1)

            pool.wait_ge(ln_in, 32)
            for t in range(NT):
                affine(t, t, f"n{t}", f"t{t - 2}" if t >= 2 else None)
            g_.memset(qs[:, :, NS:], 0.0).then_inc(pl_s, 1)
            pool.wait_ge(ln_in, 64)
            for t in range(NT):
                affine(t, NT + t, f"N{t}", f"t{NT - 2 + t}" if t < 2 else f"T{t - 2}")

        @block.vector
        def _(dve):
            v = nc.vector
            n_link = [0]

            def link(ins):
                n_link[0] += 1
                ins.then_inc(link_s, 1)
                dve.wait_ge(link_s, n_link[0])

            def norm(t, i, y, s, freed):
                n = rows_of(t)
                dve.wait_ge(pe_s, PE(y))
                dve.wait_ge(xr_in[i % 2], 16 * (i // 2 + 1))
                if freed:
                    dve.wait_ge(pl_s, PL(freed))
                ri = r[0:n, i % 2, :]
                for half in range(2):
                    ins = v.scalar_tensor_tensor(ri[:, half * 512:half * 512 + 512], xrow[0:n, i % 2, half * 512:half * 512 + 512],
                                                 ALPHA, bank[2 * (i % 2) + half][0:n, :], ALU.mult, ALU.add)
                ins.then_inc(dv_s, 1)
                dve.wait_ge(dv_s, n_after[0] + 1)
                layer_norm_rows(v, link, ri, stats, mv, n).then_inc(dv_s, 1)
                dve.wait_ge(ac_s, AC(s))
                v.tensor_scalar(ri, ri, mv[0:n, 0:1], rs[0:n, 1:2], ALU.subtract, ALU.mult).then_inc(dv_s, 1)
                n_after[0] += 3

            n_after = [0]
            for t in range(NT):
                norm(t, t, f"y{t}", f"s{t}", f"x{t - 2}" if t >= 2 else None)

            def soft(maxes, banks, heads, e):
                for lo, b in banks:
                    ins = v.tensor_reduce(mx[:, 0, lo:lo + (2 if heads > 1 else 1)],
                                          b[:, 0:MEM * (2 if heads > 1 else 1)].rearrange("p (h n) -> p h n", n=MEM), AX_X, ALU.max)
                link(ins)
                v.tensor_scalar(mx[:, 1, 0:heads], mx[:, 0, 0:heads], -float(CAD) ** -0.5, None, ALU.mult).then_inc(dv_s, 1)
                dve.wait_ge(ac_s, AC(e))
                link(v.reciprocal(sm[:, 1, 0:heads], sm[:, 0, 0:heads]))
                v.tensor_tensor(pr[:, 0:heads, :], pr[:, 0:heads, :], sm[:, 1, 0:heads].unsqueeze(2).to_broadcast((P, heads, MEM)),
                                ALU.mult).then_inc(dv_s, 1)
                n_after[0] += 2

            for t in range(NT - 1):
                dve.wait_ge(pe_s, PE(f"S{t}"))
                soft(None, ((0, bank[6]), (2, bank[7])), CAH, f"e{t}")
                if t:
                    norm(t - 1, NT + t - 1, f"Y{t - 1}", f"s_{t - 1}", f"x{NT - 3 + t}" if t < 3 else f"X{t - 3}")
            t = NT - 1
            norm(t - 1, NT + t - 1, f"Y{t - 1}", f"s_{t - 1}", f"X{t - 3}")
            for b in range(NB):
                dve.wait_ge(pe_s, PE(f"s{b}"))
                soft(None, ((0, bank[4]),), 1, f"e_{b}")
            norm(t, NT + t, f"Y{t}", f"s_{t}", f"X{t - 2}")


def phase_r(nc, A, O, M):
    with ExitStack() as ctx:
        def sb(name, shape, dt=F32):
            return ctx.enter_context(nc.sbuf_tensor(name, shape, dt))

        def sem(name):
            return ctx.enter_context(nc.semaphore(name))

        bank = [ctx.enter_context(nc.psum_tensor(f"r_bank{i}", [P, 512], F32)) for i in range(4)]
        rc = sb("rc", [P, RC_ALL])
        strict = rc[:, RC_STRICT:RC_STRICT + P]
        iota8 = rc[:, RC_I8:RC_I8 + EG]
        iota64 = rc[:, RC_I64:RC_I64 + E]
        valid = rc[:, RC_VALID:RC_VALID + NT]
        starts = rc[:, RC_START:RC_START + NMAX]
        pairs = rc[:, RC_PAIR:RC_PAIR + NBLK // 2]
        part = rc[:, RC_PART:RC_PART + 1]
        tok = sb("tok", [P, NT], I32)
        g3 = [sb(f"g3_{i}", [P, NT, EG]) for i in range(2)]
        e3 = [sb(f"e3_{i}", [P, NT, E]) for i in range(2)]
        em = sb("em", [P, NT, E])
        oh = sb("oh", [P, 2, NT, E])
        before = sb("before", [P, NT, E])
        both = sb("both", [P, NT, E])
        s1 = [sb(f"s1_{i}", [P, NT]) for i in range(8)]
        cnt = sb("cnt", [P, E])
        big = sb("big", [P, E, NMAX])
        nb = sb("nb", [P, E])
        bend = sb("bend", [P, E])
        base = sb("base", [P, E])
        one = sb("one", [P, E])
        destf = sb("destf", [P, 2, NT])
        bexp = sb("bexp", [P, 1])
        bexpi = sb("bexpi", [P, 1], I32)
        npf = sb("npf", [P, NBLK // 2])
        npi = sb("npi", [P, 1], I32)
        zero = sb("zero", [P, SLOTS // P], I32)
        rowsf = sb("rowsf", [NBLK, BLK])
        rowsi = sb("rowsi", [NBLK, BLK], I32)

        rc_in, tok_in, zeroed = sem("rc_in"), sem("tok_in"), sem("r_zeroed")
        table_zero, scat, rows_in, tab_out = sem("table_zero"), sem("scattered"), sem("rows_in"), sem("tab_out")
        link_s = sem("r_link")
        to_act, from_act, to_pe, from_pe, dest_ready, tab_ready = (sem(n) for n in
            ("to_act", "from_act", "to_pe", "from_pe", "dest_ready", "tab_ready"))
        block = ctx.enter_context(nc.Block())

        @block.sync
        def _(sp):
            sp.dma_start(rc[:, :], A["rconst"]).then_inc(rc_in, 16)
            sp.dma_start(tok[:, :], A["tokens"]).then_inc(tok_in, 16)
            sp.wait_ge(zeroed, 1)
            sp.dma_start(M.row_tok.rearrange("(p n) o -> p (n o)", p=P), zero[:, :]).then_inc(table_zero, 16)
            sp.wait_ge(tab_ready, 1)
            sp.dma_start(M.blk_d[0:NBLK, :], bexpi[0:NBLK, :]).then_inc(tab_out, 16)
            sp.dma_start(M.blk_d[NBLK:NBLK + 1, :], npi[0:1, :]).then_inc(tab_out, 16)
            sp.wait_ge(scat, 16 * 2 * NT)
            sp.dma_start(rowsi[:, :], M.row_tok.rearrange("(b n) o -> b (n o)", n=BLK)).then_inc(rows_in, 16)
            sp.wait_ge(tab_out, 32)

        @block.gpsimd
        def _(pool):
            nc.gpsimd.memset(zero[:, :], 0).then_inc(zeroed, 1)
            pool.wait_ge(table_zero, 16)
            pool.wait_ge(tok_in, 16)
            pool.wait_ge(dest_ready, 1)
            for t in range(NT):
                for i in range(2):
                    n = rows_of(t)
                    nc.gpsimd.indirect_dma_start(
                        out=M.row_tok, out_offset=bass.IndirectOffsetOnAxis(ap=M.dest[0:n, i, t:t + 1], axis=0),
                        in_=tok[0:n, t:t + 1], in_offset=None).then_inc(scat, 16)

        @block.scalar
        def _(act):
            act.wait_ge(to_act, 1)
            nc.scalar.activation(g3[0][:, :, :], g3[0][:, :, :], ACT.Exp).then_inc(from_act, 1)
            act.wait_ge(to_act, 2)
            nc.scalar.activation(s1[4][:, :], s1[4][:, :], ACT.Exp).then_inc(from_act, 1)

        @block.tensor
        def _(pe):
            mm = nc.tensor.matmul
            pe.wait_ge(to_pe, 1)
            flat = both[:, :, :].rearrange("p t e -> p (t e)")
            bef = before[:, :, :].rearrange("p t e -> p (t e)")
            for b, (at, n) in enumerate(((0, 512), (512, E))):
                mm(bank[b][:, 0:n], strict, flat[:, at:at + n], start=True, stop=False)
                mm(bank[b][:, 0:n], M.ones, bef[:, at:at + n], start=False, stop=True)
            mm(bank[2][:, 0:E], M.ones, before[:, NT - 1, :], start=True, stop=False)
            mm(bank[2][:, 0:E], M.ones, both[:, NT - 1, :], start=False, stop=True).then_inc(from_pe, 1)
            pe.wait_ge(to_pe, 2)
            nc.tensor.transpose(bank[3][0:BLK, 0:NBLK], rowsf[:, :], M.ident[0:NBLK, 0:NBLK]).then_inc(from_pe, 1)

        @block.vector
        def _(dve):
            v = nc.vector
            n_link = [0]

            def link(ins):
                n_link[0] += 1
                ins.then_inc(link_s, 1)
                dve.wait_ge(link_s, n_link[0])

            def wide(a, m):
                return a.unsqueeze(2).to_broadcast((P, NT, m))

            def first_hot(out, x, best, iota, m, scratch, idx):
                over = iota.unsqueeze(1).to_broadcast((P, NT, m))
                link(v.tensor_tensor(scratch, x, wide(best, m), ALU.is_equal))
                link(v.scalar_tensor_tensor(scratch, scratch, -float(m), over, ALU.mult, ALU.add))
                link(v.tensor_reduce(idx, scratch, AX_X, ALU.min))
                link(v.tensor_scalar(idx, idx, float(m), None, ALU.add))
                link(v.tensor_tensor(out, over, wide(idx, m), ALU.is_equal))

            v.memset(M.logits[NS:P, NT - 1, :], 0.0).then_inc(link_s, 1)
            n_link[0] += 1
            dve.wait_ge(link_s, 1)
            dve.wait_ge(rc_in, 16)
            gl, el = M.logits[:, :, 0:EG], M.logits[:, :, EG:]
            link(v.memset(one[:, :], 1.0))
            link(v.tensor_reduce(s1[0][:, :], gl, AX_X, ALU.max))
            v.tensor_tensor(g3[0][:, :, :], gl, wide(s1[0][:, :], EG), ALU.subtract).then_inc(to_act, 1)
            first_hot(g3[1][:, :, :], gl, s1[0][:, :], iota8, EG, e3[0][:, :, 0:EG], s1[1][:, :])
            link(v.tensor_scalar(g3[1][:, :, :], g3[1][:, :, :], -1.0, FAR, ALU.add, ALU.mult))
            link(v.tensor_copy(e3[0][:, :, :].rearrange("p t (g e) -> p t g e", g=EG),
                               g3[1][:, :, :].unsqueeze(3).to_broadcast((P, NT, EG, EPG))))
            link(v.tensor_tensor(em[:, :, :], el, e3[0][:, :, :], ALU.add))
            link(v.tensor_reduce(s1[2][:, :], em[:, :, :], AX_X, ALU.max))
            first_hot(oh[:, 0], em[:, :, :], s1[2][:, :], iota64, E, e3[1][:, :, :], s1[1][:, :])
            link(v.scalar_tensor_tensor(em[:, :, :], oh[:, 0], -2.0 * FAR, em[:, :, :], ALU.mult, ALU.add))
            link(v.tensor_reduce(s1[3][:, :], em[:, :, :], AX_X, ALU.max))
            first_hot(oh[:, 1], em[:, :, :], s1[3][:, :], iota64, E, e3[1][:, :, :], s1[1][:, :])
            v.tensor_tensor(s1[4][:, :], s1[3][:, :], s1[2][:, :], ALU.subtract).then_inc(to_act, 1)
            link(v.tensor_tensor(both[:, :, :], oh[:, 0], oh[:, 1], ALU.add))
            link(v.tensor_tensor(both[:, :, :], both[:, :, :], wide(valid, E), ALU.mult))
            link(v.memset(before[:, 0, :], 0.0))
            for t in range(1, NT):
                link(v.tensor_tensor(before[:, t, :], before[:, t - 1, :], both[:, t - 1, :], ALU.add))
            v.tensor_copy(s1[7][:, 0:1], part).then_inc(to_pe, 1)
            dve.wait_ge(from_act, 1)
            link(v.tensor_reduce(s1[5][:, :], g3[0][:, :, :], AX_X, ALU.add))
            dve.wait_ge(from_act, 2)
            link(v.scalar_tensor_tensor(s1[6][:, :], s1[4][:, :], 1.0, s1[5][:, :], ALU.add, ALU.mult))
            link(v.reciprocal(M.w12[:, 0, :], s1[6][:, :]))
            link(v.tensor_tensor(M.w12[:, 1, :], s1[4][:, :], M.w12[:, 0, :], ALU.mult))
            dve.wait_ge(from_pe, 1)
            link(v.tensor_copy(cnt[:, :], bank[2][:, 0:E]))
            link(v.tensor_tensor(big[:, :, :], cnt[:, :].unsqueeze(2).to_broadcast((P, E, NMAX)),
                                 starts.unsqueeze(1).to_broadcast((P, E, NMAX)), ALU.is_gt))
            link(v.tensor_reduce(nb[:, :], big[:, :, :], AX_X, ALU.add))
            link(v.tensor_tensor_scan(bend[:, :], one[:, :], nb[:, :], 0.0, ALU.mult, ALU.add))
            link(v.tensor_tensor(base[:, :], bend[:, :], nb[:, :], ALU.subtract))
            link(v.tensor_scalar(base[:, :], base[:, :], float(BLK), None, ALU.mult))
            v.tensor_tensor(em[:, 0:8, :], bank[0][:, :].rearrange("p (t e) -> p t e", e=E),
                            base[:, :].unsqueeze(1).to_broadcast((P, 8, E)), ALU.add)
            link(v.tensor_tensor(em[:, 8, :], bank[1][:, 0:E], base[:, :], ALU.add))
            for i in range(2):
                link(v.tensor_tensor(e3[i][:, :, :], em[:, :, :], oh[:, i], ALU.mult))
                link(v.tensor_reduce(destf[:, i, :], e3[i][:, :, :], AX_X, ALU.add))
            v.tensor_copy(M.dest[:, :, :], destf[:, :, :]).then_inc(dest_ready, 1)
            link(v.tensor_scalar(e3[0][:, 0, :], bend[:, :], part, None, ALU.is_le))
            link(v.tensor_reduce(bexp[:, :], e3[0][:, 0, :], AX_X, ALU.add))
            link(v.tensor_scalar(bexp[:, :], bexp[:, :], float(E - 1), None, ALU.min))
            link(v.tensor_copy(bexpi[:, :], bexp[:, :]))
            link(v.tensor_scalar(npf[:, :], pairs, bend[:, E - 1:E], None, ALU.is_lt))
            link(v.tensor_reduce(bexp[:, :], npf[:, :], AX_X, ALU.add))
            v.tensor_copy(npi[:, :], bexp[:, :]).then_inc(tab_ready, 1)
            dve.wait_ge(rows_in, 16)
            v.tensor_copy(rowsf[:, :], rowsi[:, :]).then_inc(to_pe, 1)
            dve.wait_ge(from_pe, 2)
            link(v.tensor_copy(M.idx_all[:, :], bank[3][0:BLK, 0:NBLK]))


def steps_d():
    pe, dv, ac = [], [], []
    pe += ["T0", "G0", "U0", "T1", "D0", "G1", "U1", "D1"]
    ac += ["x0", "t0", "x1", "y0", "t1", "y1"]
    dv += ["h0", "z0", "h1", "z1"]
    return pe, dv, ac


def phase_d(nc, A, O, M):
    with ExitStack() as ctx:
        def sb(name, shape, dt=F32):
            return ctx.enter_context(nc.sbuf_tensor(name, shape, dt))

        def sem(name):
            return ctx.enter_context(nc.semaphore(name))

        bT = [ctx.enter_context(nc.psum_tensor(f"d_t{i}", [P, 512], F32)) for i in range(2)]
        bH = [ctx.enter_context(nc.psum_tensor(f"d_h{i}", [P, 512], F32)) for i in range(2)]
        bY = [ctx.enter_context(nc.psum_tensor(f"d_y{i}", [P, 2, 512], F32)) for i in range(2)]
        wg = sb("wg_e", [P, 2, KC, FF])
        wu = sb("wu_e", [P, 2, KC, FF])
        wd = sb("wd_e", [P, 2, 2, D])
        idx = sb("idx", [BLK, 2], I32)
        xg = sb("xg", [BLK, 2, D])
        xT = sb("xT_e", [P, 2, KC, BLK])
        th = sb("th", [P, 2, 2, BLK])
        hh = sb("hh", [P, 2, 2, BLK])
        yb = sb("yb", [BLK, 2, D])
        wg_in, wu_in, wd_in, xg_in, idx_set, y_out = ([sem(f"{n}{j}") for j in range(2)] for n in
                                                      ("wg_in", "wu_in", "wd_in", "xg_in", "idx_set", "y_out"))
        pe_s, dv_s, ac_s = sem("d_pe"), sem("d_dve"), sem("d_act")
        link_s = sem("d_link")
        PE, DV, AC = (Steps(x) for x in steps_d())
        most = NBLK // 2

        def rounds(eng):
            return eng.value_load(M.blk_d[NBLK:NBLK + 1, 0:1], min_val=1, max_val=most)

        block = ctx.enter_context(nc.Block())

        @block.sync
        def _(sp):
            with sp.Fori(0, rounds(sp)) as i:
                es = [sp.value_load(M.blk_d[bass.ds(2 * i + j, 1), 0:1], min_val=0, max_val=E - 1) for j in range(2)]
                for j in range(2):
                    e = es[j]
                    sp.wait_ge(pe_s, PE(i, f"G{j}"))
                    sp.dma_start(wg[:, j], A["w_gate"][0, bass.ds(e, 1)].rearrange("e (p k) f -> p (e k) f", p=P)).then_inc(wg_in[j], 16)
                    sp.wait_ge(pe_s, PE(i, f"U{j}"))
                    sp.dma_start(wu[:, j], A["w_up"][0, bass.ds(e, 1)].rearrange("e (p k) f -> p (e k) f", p=P)).then_inc(wu_in[j], 16)
                    sp.wait_ge(pe_s, PE(i, f"D{j}"))
                    sp.dma_start(wd[:, j], A["w_down"][0, bass.ds(e, 1)].rearrange("e (p c) d -> p (e c) d", p=P)).then_inc(wd_in[j], 16)

        @block.gpsimd
        def _(pool):
            with pool.Fori(0, rounds(pool)) as i:
                for j in range(2):
                    pool.sem_clear(idx_set[j])
                    pool.wait_ge(pe_s, PE(i, f"T{j}"))
                    nc.gpsimd.tensor_copy(idx[:, j:j + 1], M.idx_all[:, bass.ds(2 * i + j, 1)]).then_inc(idx_set[j], 1)
                    pool.wait_ge(idx_set[j], 1)
                    nc.gpsimd.indirect_dma_start(out=xg[:, j, :], out_offset=None, in_=M.x2d,
                                                 in_offset=bass.IndirectOffsetOnAxis(ap=idx[:, j:j + 1], axis=0)
                                                 ).then_inc(xg_in[j], 16)

        @block.tensor
        def _(pe):
            mm, tr = nc.tensor.matmul, nc.tensor.transpose
            pe.sem_inc(pe_s, PE.per_head)

            def turn(i, j):
                pe.wait_ge(ac_s, AC(i, f"x{j}"))
                pe.wait_ge(xg_in[j], (i + 1) * 16)
                rows = xg[:, j, :].rearrange("n (p k) -> n k p", k=KC)
                mm(bT[j][:, 0:BLK], rows[:, 0, :], M.ident[0:BLK, 0:BLK], start=True, stop=True)
                for k in range(1, KC):
                    m = tr(bT[j][:, k * BLK:(k + 1) * BLK], rows[:, k, :], M.ident[0:BLK, 0:BLK])
                m.then_inc(pe_s, 1)

            def hidden(i, j):
                pe.wait_ge(ac_s, AC(i + 1, f"x{j}"))
                pe.wait_ge(dv_s, DV(i, f"h{j}"))
                for a, (w, w_in) in enumerate(((wg, wg_in), (wu, wu_in))):
                    pe.wait_ge(w_in[j], (i + 1) * 16)
                    wv = w[:, j].rearrange("p k (f c) -> p k c f", c=2)
                    for c in range(2):
                        for k in range(KC):
                            m = mm(bH[j][:, (2 * a + c) * BLK:(2 * a + c + 1) * BLK], wv[:, k, c, :], xT[:, j, k, :],
                                   start=(k == 0), stop=(k == KC - 1))
                    m.then_inc(pe_s, 1)

            def down(i, j):
                pe.wait_ge(wd_in[j], (i + 1) * 16)
                pe.wait_ge(dv_s, DV(i + 1, f"h{j}"))
                pe.wait_ge(ac_s, AC(i, f"y{j}"))
                pe.wait_ge(dv_s, DV(i, f"z{j}"))
                for half in range(2):
                    for c in range(2):
                        m = mm(bY[j][0:BLK, half, :], hh[:, j, c, :], wd[:, j, c, half * 512:(half + 1) * 512],
                               start=(c == 0), stop=(c == 1))
                m.then_inc(pe_s, 1)

            with pe.Fori(0, rounds(pe)) as i:
                turn(i, 0)
                hidden(i, 0)
                turn(i, 1)
                down(i, 0)
                hidden(i, 1)
                down(i, 1)

        @block.scalar
        def _(act):
            a = nc.scalar
            act.sem_inc(ac_s, AC.per_head)
            act.sem_inc(y_out[0], 16)
            act.sem_inc(y_out[1], 16)

            def x(i, j):
                act.wait_ge(pe_s, PE(i + 1, f"T{j}"))
                a.copy(xT[:, j], bT[j][:, :].rearrange("p (k n) -> p k n", n=BLK)).then_inc(ac_s, 1)

            def t(i, j):
                act.wait_ge(pe_s, PE(i + 1, f"U{j}"))
                a.activation(th[:, j], bH[j][:, 0:2 * BLK].rearrange("p (c n) -> p c n", n=BLK), ACT.Tanh, scale=0.5).then_inc(ac_s, 1)

            def y(i, j):
                act.wait_ge(pe_s, PE(i + 1, f"D{j}"))
                act.wait_ge(y_out[j], (i + 1) * 16)
                a.copy(yb[:, j, 0:512], bY[j][0:BLK, 0, :]).then_inc(ac_s, 1)
                act.wait_ge(ac_s, AC(i + 1, f"y{j}"))
                act.wait_ge(dv_s, DV(i + 1, f"z{j}"))
                act.dma_start(M.y_rows[bass.ds((2 * i + j) * BLK, BLK), :], yb[:, j, :]).then_inc(y_out[j], 16)

            n = rounds(act)
            with act.Fori(0, n) as i:
                x(i, 0)
                t(i, 0)
                x(i, 1)
                y(i, 0)
                t(i, 1)
                y(i, 1)
            for j in range(2):
                act.wait_ge(y_out[j], n * 16 + 16)
                a.copy(th[0:1, j, 0, 0:1], th[0:1, j, 0, 1:2])

        @block.vector
        def _(dve):
            v = nc.vector
            dve.sem_inc(dv_s, DV.per_head)
            with dve.Fori(0, rounds(dve)) as i:
                dve.sem_clear(link_s)
                for j in range(2):
                    dve.wait_ge(ac_s, AC(i + 1, f"t{j}"))
                    v.scalar_tensor_tensor(th[:, j], th[:, j], 1.0, bH[j][:, 0:2 * BLK].rearrange("p (c n) -> p c n", n=BLK),
                                           ALU.add, ALU.mult).then_inc(link_s, 1)
                    dve.wait_ge(link_s, j + 1)
                    dve.wait_ge(pe_s, PE(i + 1, f"U{j}"))
                    v.scalar_tensor_tensor(hh[:, j], th[:, j], 0.5, bH[j][:, 2 * BLK:4 * BLK].rearrange("p (c n) -> p c n", n=BLK),
                                           ALU.mult, ALU.mult).then_inc(dv_s, 1)
                    dve.wait_ge(pe_s, PE(i + 1, f"D{j}"))
                    dve.wait_ge(y_out[j], (i + 1) * 16)
                    v.tensor_copy(yb[:, j, 512:], bY[j][0:BLK, 1, :]).then_inc(dv_s, 1)


def phase_e(nc, A, O, M):
    with ExitStack() as ctx:
        def sb(name, shape, dt=F32):
            return ctx.enter_context(nc.sbuf_tensor(name, shape, dt))

        def sem(name):
            return ctx.enter_context(nc.semaphore(name))

        RB = 3
        lng, lnb = sb("lng_e", [P, D]), sb("lnb_e", [P, D])
        x2 = sb("x2", [P, RB, D])
        ys = sb("ys", [P, RB, 2, D])
        ro = sb("ro", [P, RB, D])
        stats = sb("stats_e", [P, 2, 6])
        mv = sb("mv_e", [P, RB, 2])
        rs = sb("rs_e", [P, RB, 4])
        ln_in = sem("e_ln_in")
        x2_in = [sem(f"e_x2_in{i}") for i in range(RB)]
        ys_in = [sem(f"e_ys_in{i}") for i in range(RB)]
        out = [sem(f"e_out{i}") for i in range(RB)]
        scaled, summed, counted, normed, gained, shifted = (sem("e_" + n) for n in
            ("scaled", "summed", "counted", "normed", "gained", "shifted"))
        link_s, alink_s = sem("e_link"), sem("e_alink")

        def dst(t):
            return O["y_prompt"][0, t * P:(t + 1) * P, :] if t < NT - 1 else O["y_sample"].rearrange("b l d -> (b l) d")

        block = ctx.enter_context(nc.Block())

        @block.sync
        def _(sp):
            sp.dma_start(lng[:, :], A["ln3_g"].to_broadcast((P, D))).then_inc(ln_in, 16)
            sp.dma_start(lnb[:, :], A["ln3_b"].to_broadcast((P, D))).then_inc(ln_in, 16)
            for t in range(NT + 1):
                if t < NT:
                    if t >= RB:
                        sp.wait_ge(gained, t - RB + 1)
                    sp.dma_start(x2[0:rows_of(t), t % RB, :], M.x2d[t * P:t * P + rows_of(t), :]).then_inc(x2_in[t % RB], 16)
                if t:
                    i = t - 1
                    sp.wait_ge(shifted, t)
                    sp.dma_start(dst(i), ro[0:rows_of(i), i % RB, :]).then_inc(out[i % RB], 16)
            for i in range(RB):
                sp.wait_ge(out[i], 16 * ((NT - 1 - i) // RB + 1))

        @block.gpsimd
        def _(pool):
            def gather(t):
                n = rows_of(t)
                if t >= RB:
                    pool.wait_ge(summed, t - RB + 1)
                for i in range(2):
                    nc.gpsimd.indirect_dma_start(out=ys[0:n, t % RB, i, :], out_offset=None, in_=M.y_rows,
                                                 in_offset=bass.IndirectOffsetOnAxis(ap=M.dest[0:n, i, t:t + 1], axis=0)
                                                 ).then_inc(ys_in[t % RB], 16)

            for t in range(RB):
                gather(t)
            pool.wait_ge(ln_in, 32)
            for t in range(NT):
                n = rows_of(t)
                if t and t + RB - 1 < NT:
                    gather(t + RB - 1)
                pool.wait_ge(gained, t + 1)
                nc.gpsimd.tensor_tensor(ro[0:n, t % RB, :], ro[0:n, t % RB, :], lnb[0:n, :], ALU.add).then_inc(shifted, 1)

        @block.scalar
        def _(act):
            a = nc.scalar
            n_link = [0]

            def link(ins):
                n_link[0] += 1
                ins.then_inc(alink_s, 1)
                act.wait_ge(alink_s, n_link[0])

            def scale(t):
                n = rows_of(t)
                act.wait_ge(x2_in[t % RB], 16 * (t // RB + 1))
                a.mul(x2[0:n, t % RB, :], x2[0:n, t % RB, :], ALPHA).then_inc(scaled, 1)

            scale(0)
            scale(1)
            for t in range(NT):
                n, i = rows_of(t), t % RB
                act.wait_ge(counted, t + 1)
                link(a.activation(rs[0:n, i, 0:1], mv[0:n, i, 1:2], ACT.Ln, bias=M.lneps[0:n]))
                link(a.activation(rs[0:n, i, 1:2], rs[0:n, i, 0:1], ACT.Exp, scale=-0.5))
                a.activation(rs[0:n, i, 2:3], mv[0:n, i, 0:1], ACT.Copy, scale=-1.0).then_inc(alink_s, 1)
                n_link[0] += 1
                act.wait_ge(alink_s, n_link[0])
                link(a.activation(rs[0:n, i, 3:4], rs[0:n, i, 2:3], ACT.Copy, scale=rs[0:n, i, 1:2]))
                a.activation(x2[0:n, i, :], x2[0:n, i, :], ACT.Identity, scale=rs[0:n, i, 1:2],
                             bias=rs[0:n, i, 3:4]).then_inc(normed, 1)
                if t + 2 < NT:
                    scale(t + 2)

        @block.vector
        def _(dve):
            v = nc.vector
            n_link = [0]

            def link(ins):
                n_link[0] += 1
                ins.then_inc(link_s, 1)
                dve.wait_ge(link_s, n_link[0])

            def gain(t):
                n, i = rows_of(t), t % RB
                dve.wait_ge(normed, t + 1)
                if t >= RB:
                    dve.wait_ge(out[i], 16 * (t // RB))
                v.tensor_tensor(ro[0:n, i, :], x2[0:n, i, :], lng[0:n, :], ALU.mult).then_inc(gained, 1)

            dve.wait_ge(ln_in, 32)
            for t in range(NT):
                n, i = rows_of(t), t % RB
                dve.wait_ge(scaled, t + 1)
                dve.wait_ge(ys_in[i], 32 * (t // RB + 1))
                x = x2[0:n, i, :]
                link(v.scalar_tensor_tensor(x, ys[0:n, i, 0, :], M.w12[0:n, 0, t:t + 1], x, ALU.mult, ALU.add))
                v.scalar_tensor_tensor(x, ys[0:n, i, 1, :], M.w12[0:n, 1, t:t + 1], x, ALU.mult, ALU.add).then_inc(summed, 1)
                dve.wait_ge(summed, t + 1)
                layer_norm_rows(v, link, x, stats, mv[:, i], n).then_inc(counted, 1)
                if t:
                    gain(t - 1)
            gain(NT - 1)


def build(nc, A, O):
    with ExitStack() as ctx:
        def sb(name, shape, dt=F32):
            return ctx.enter_context(nc.sbuf_tensor(name, shape, dt))

        M = Persistent()
        M.const = sb("const", [P, C_ALL])
        M.eps, M.epshd, M.lneps = (M.const[:, n:n + 1] for n in range(3))
        M.ident = M.const[:, C_ID:C_ID + P]
        M.upper = M.const[:, C_UP:C_UP + P]
        M.ones = M.const[:, C_ONE:C_ONE + P]
        M.upper8 = M.const[:, C_UP8:C_UP8 + P]
        M.block8 = M.const[:, C_BLK8:C_BLK8 + P]
        M.inseq = M.const[:, C_SEQ:C_SEQ + NB]
        M.early = M.const[:, C_EARLY:C_LEVEL].rearrange("p (g t) -> p g t", t=PM)
        M.level = M.const[:, C_LEVEL:C_ALL].rearrange("p (l n) -> p l n", n=P)
        M.xT = sb("xT", [P, KC, T])
        M.mT = sb("mT", [P, KC, T])
        M.y_rows = nc.dram_tensor("y_rows", (SLOTS, D), F32, kind="Internal").ap()
        with ExitStack() as early:
            M.par = early.enter_context(nc.sbuf_tensor("par", [P, R_ALL], F32))
            M.stateT = early.enter_context(nc.sbuf_tensor("stateT", [P, 24, (CW - 1) * NB], F32))
            M.scal = early.enter_context(nc.sbuf_tensor("scal", [P, H, S_ALL], F32))
            phase_a(nc, A, O, M)
            phase_b(nc, A, O, M)
        M.logits = sb("logits", [P, NT, EG + E])
        M.dest = sb("dest", [P, 2, NT], I32)
        M.w12 = sb("w12", [P, 2, NT])
        M.idx_all = sb("idx_all", [BLK, NBLK], I32)
        M.row_tok = nc.dram_tensor("row_tok", (SLOTS, 1), I32, kind="Internal").ap()
        M.blk_d = nc.dram_tensor("blk_d", (NBLK + 1, 1), I32, kind="Internal").ap()
        M.x1d = nc.dram_tensor("x1_rows", (T, D), F32, kind="Internal").ap()
        M.x2d = nc.dram_tensor("x2_rows", (T, D), F32, kind="Internal").ap()
        phase_c(nc, A, O, M)
        phase_r(nc, A, O, M)
        phase_d(nc, A, O, M)
        phase_e(nc, A, O, M)


_INS = ['x_prompt', 'x_sample', 'cache_mem_k', 'cache_mem_v', 'state_delta', 'state_conv', 'state_pool', 'mem_prompt',
        'w_in', 'w_conv', 'a_log', 'dt_bias', 'w_onorm', 'w_pool', 'pool_scale', 'w_out', 'ln1_g', 'ln1_b',
        'w_cq', 'w_ck', 'w_cv', 'w_co', 'ln2_g', 'ln2_b', 'w_router_group', 'w_router_expert', 'w_gate', 'w_up',
        'w_down', 'ln3_g', 'ln3_b']
_OUTS = [('y_prompt', (1, SEQ, D)), ('y_sample', (NB, DS, D)), ('delta_prompt', (1, 1, H, HD, HD)),
         ('conv_prompt', (1, 1, CW - 1, QKV)), ('pool_prompt', (1, 1, PM - 1, D)), ('mem_k', (1, 1, MEM, CAH, CAD)),
         ('mem_v', (1, 1, MEM, CAH, CAD)), ('delta_sample', (1, NB, H, HD, HD)),
         ('conv_sample', (1, NB, CW - 1, QKV)), ('pool_sample', (1, NB, PM - 1, D))]


def kernel(**inputs):
    import concourse.bacc as bacc
    from concourse.bass_utils import run_bass_kernel_spmd

    nc = bacc.Bacc("TRN2", target_bir_lowering=False, num_devices=1)
    arrays, A, O = {}, {}, {}
    for name in _INS:
        a = np.ascontiguousarray(inputs[name])
        arrays[f"in_{name}"] = a
        A[name] = nc.dram_tensor(f"in_{name}", a.shape, mybir.dt.from_np(a.dtype), kind="ExternalInput").ap()
    arrays["in_const"] = constants()
    A["const"] = nc.dram_tensor("in_const", arrays["in_const"].shape, F32, kind="ExternalInput").ap()
    arrays["in_rconst"] = routing_constants()
    A["rconst"] = nc.dram_tensor("in_rconst", (P, RC_ALL), F32, kind="ExternalInput").ap()
    arrays["in_tokens"] = np.ascontiguousarray(np.arange(NT * P, dtype=np.int32).reshape(NT, P).T)
    A["tokens"] = nc.dram_tensor("in_tokens", (P, NT), I32, kind="ExternalInput").ap()
    for name, shape in _OUTS:
        O[name] = nc.dram_tensor(f"out_{name}", shape, F32, kind="ExternalOutput").ap()
    build(nc, A, O)
    r = run_bass_kernel_spmd(nc, [arrays], core_ids=[0])
    return tuple(r.results[0][f"out_{name}"] for name, _ in _OUTS)
```

```python
from contextlib import ExitStack

import numpy as np
import concourse.bass as bass
from concourse import mybir

ALU = mybir.AluOpType
ACT = mybir.ActivationFunctionType
F32 = mybir.dt.float32
BF16 = mybir.dt.bfloat16
I32 = mybir.dt.int32
U32 = mybir.dt.uint32
AX_X = mybir.AxisListType.X

P = 128
D = 1024
KC = D // P
SEQ, NB, DS = 1024, 8, 8
NS = NB * DS
T = SEQ + NS
NT = SEQ // P + 1
H, HD = 8, 128
QKV = 3 * H * HD
CW = 4
POOLW = (2, 4, 8, 16)
PG = 256
PM = 16
MEM = 256
CAH, CAD = 4, 256
EG, EPG, E, FF = 8, 8, 64, 256
O_Z = QKV
O_A = O_Z + H * HD
O_P = O_A + 2 * H
O_GA = O_P + D
O_GB = O_GA + D
ALPHA = 2.0 ** 0.25
LN_EPS = 1e-5
NORM_EPS = 1e-6
LEVELS = 7
SLEVELS = 3
SEGS = ((0, 512), (512, 512), (1024, 64))
BLK = 64
NBLK = (2 * T + E * (BLK - 1)) // BLK
RND = 3
NBLK = -(-NBLK // RND) * RND
LEAD = RND - 1
SLOTS = (LEAD + NBLK) * BLK
MIN_SLOTS = LEAD * BLK + 2 * T
FILL_ROWS = (SLOTS - MIN_SLOTS) // H
FILL_P = max(n for n in range(1, P + 1) if FILL_ROWS % n == 0)


def rows_of(t):
    return P if t < NT - 1 else NS


def constants():
    i = np.arange(P)
    level = np.zeros((P, LEVELS, P), np.float32)
    for n in range(LEVELS):
        s = 1 << n
        same = (i[:, None] // (2 * s)) == (i[None, :] // (2 * s))
        level[:, n] = same & ((i[:, None] // s) % 2 == 1) & ((i[None, :] // s) % 2 == 0)
    block8 = (i[:, None] // DS == i[None, :] // DS).astype(np.float32)
    upper = (i[:, None] <= i[None, :]).astype(np.float32)
    ident = np.eye(P, dtype=np.float32)
    ones = np.ones((P, P), np.float32)
    inseq = (i[:, None] // DS == np.arange(NB)[None, :]).astype(np.float32)
    early = np.ones((P, len(POOLW), PM), np.float32)
    for g, w in enumerate(POOLW):
        for t in range(w):
            early[:, g, t] = w / (t + 1)
    eps = np.tile(np.array([NORM_EPS, NORM_EPS * HD, LN_EPS, 1.0], np.float32), (P, 1))
    parts = [eps, ident, upper, ones, upper * block8, block8, inseq, early.reshape(P, -1), level.reshape(P, -1)]
    return np.concatenate(parts, axis=1)


C_EPS = 0
C_ID, C_UP, C_ONE, C_UP8, C_BLK8 = (4 + n * P for n in range(5))
C_SEQ = 4 + 5 * P
C_EARLY = C_SEQ + NB
C_LEVEL = C_EARLY + len(POOLW) * PM
C_ALL = C_LEVEL + LEVELS * P

S_GC, S_KG, S_KBE, S_BETA, S_G, S_EGL, S_EGLS = 0, 9, 18, 27, 36, 45, 53
S_ALL = 64
R_CONV, R_PS, R_ON = 0, CW * 24, CW * 24 + 8
R_ALL = R_ON + 1


def routing_constants():
    i = np.arange(P)
    row = np.ones((P, 1), np.float32)
    strict = (i[:, None] < i[None, :]).astype(np.float32)
    valid = (np.arange(NT)[None, :] * P + i[:, None] < T).astype(np.float32)
    parts = [strict, row * np.arange(EG), row * np.arange(E), valid, row * np.arange(NMAX) * BLK,
             row * np.arange(NBLK // RND) * RND, i[:, None]]
    return np.concatenate([p.astype(np.float32) for p in parts], axis=1)


NMAX = -(-T // BLK)
FAR = 1e30
RC_STRICT, RC_I8, RC_I64 = 0, P, P + EG
RC_VALID = RC_I64 + E
RC_START = RC_VALID + NT
RC_ROUND = RC_START + NMAX
RC_PART = RC_ROUND + NBLK // RND
RC_ALL = RC_PART + 1


class Persistent:
    pass


def phase_a(nc, A, O, M):
    with ExitStack() as ctx:
        def sb(name, shape, dt=F32):
            return ctx.enter_context(nc.sbuf_tensor(name, shape, dt))

        def sem(name):
            return ctx.enter_context(nc.semaphore(name))

        bank = [ctx.enter_context(nc.psum_tensor(f"a_bank{i}", [P, 512], F32)) for i in range(8)]
        rowbuf = sb("rowbuf", [P, 2, D])
        memT = sb("memT", [P, KC, MEM])
        wckv = sb("wckv", [P, KC, D])
        kvrow = sb("kvrow", [P, 2, D])
        wab = sb("wab", [P, KC, 2 * H])
        ab = sb("ab", [P, NT, 2 * H])
        dtb = sb("dtb", [P, H])
        alog = sb("alog", [P, H])
        u = sb("u", [P, NT, H])
        u2 = sb("u2", [P, NT, H])
        gtm = sb("gtm", [P, NT, H])
        gseq = sb("gseq", [NS, NB, H])
        gl = sb("gl", [P, NT, H])
        prow = sb("prow", [R_ALL, P])
        sprow = sb("sprow", [(PM - 1) * NB, D])
        wp = sb("wp", [P, KC, PG])
        wg = sb("wg", [P, KC, PG])
        wpool = sb("wpool", [P, 2, PG])
        praw = sb("praw", [P, 2, PM - 1 + SEQ])
        psam = sb("psam", [P, 2, NB, PM - 1 + DS])
        statep = sb("statep", [P, KC, NB * (PM - 1)])
        pw_a = sb("pw_a", [P, 2, PM - 1 + SEQ])
        pw_as = sb("pw_as", [P, 2, NB, PM - 1 + DS])
        pw_bs = sb("pw_bs", [P, 2, NB, PM - 1 + DS])
        pooled_gate = sb("pooled_gate", [P, 2, 2, T])
        pooled, gate = pooled_gate[:, 0], pooled_gate[:, 1]
        scrow = pooled_gate[:, :, :, :].rearrange("p a c t -> p (a c t)")[0:(CW - 1) * NB, 0:QKV]
        ptok = sb("ptok", [NS, D])
        ptail = sprow[0:PM - 1, :]

        row_in = [sem(f"row_in{i}") for i in range(2)]
        const_in = sem("const_in")
        param_in = sem("param_in")
        wab_in = sem("wab_in")
        state_in = sem("state_in")
        wkv_in = sem("wkv_in")
        wpool_in = [sem(f"wpool_in{i}") for i in range(3)]
        unit_ready = sem("unit_ready")
        unit_out = sem("unit_out")
        act_step = sem("act_step")
        dve_step = sem("dve_step")
        pooled_ready = sem("pooled_ready")
        merged_ready = sem("merged_ready")
        zeroed = sem("zeroed")
        out_done = sem("a_out_done")
        kv_out = [sem(f"kv_out{i}") for i in range(2)]

        U_X = 0
        U_PAR = U_X + 2 * (NT + 2)
        U_SC = U_PAR + 1
        U_SP = U_SC + 2
        U_AB = U_SP + 2
        U_GC = U_AB + 1
        U_KV = U_GC + 1
        U_POOL = U_KV + 8
        PER_G = 6 + 1 + 6 + 6
        src = [A["x_prompt"][0, t * P:(t + 1) * P, :] for t in range(NT - 1)]
        src += [A["x_sample"].rearrange("b l d -> (b l) d")]
        src += [A["mem_prompt"][0, t * P:(t + 1) * P, :] for t in range(2)]

        def nrow(t):
            return NS if t == NT - 1 else P

        DVE_ABS, DVE_G, DVE_ALL = 1, 2, 3

        def load_pool(sp, g):
            base = U_POOL + (g - 1) * PER_G
            if g:
                sp.wait_ge(unit_ready, base + 6)
            sp.dma_start(wp[:, :, :], A["w_in"][0, :, O_P + g * PG:O_P + (g + 1) * PG]
                         .rearrange("(c p) n -> p c n", p=P)).then_inc(wpool_in[0], 16)
            if g:
                sp.wait_ge(unit_ready, base + 13)
            sp.dma_start(wg[:, :, :], A["w_in"][0, :, O_GB + g * PG:O_GB + (g + 1) * PG]
                         .rearrange("(c p) n -> p c n", p=P)).then_inc(wpool_in[1], 16)
            if g:
                sp.wait_ge(unit_ready, base + PER_G)
            sp.dma_start(wpool[:, :, :], A["w_pool"][0, g].rearrange("(c p) n -> p c n", p=P)).then_inc(wpool_in[2], 16)

        block = ctx.enter_context(nc.Block())

        @block.sync
        def _(sp):
            sp.dma_start(M.const[:, :], A["const"]).then_inc(const_in, 16)
            for t in range(NT + 2):
                if t >= 2:
                    sp.wait_ge(unit_ready, 2 * (t - 1))
                sp.dma_start(rowbuf[0:nrow(t), t % 2, :], src[t]).then_inc(row_in[t % 2], 16)
                if t == 1:
                    wv = A["w_conv"][0].rearrange("i (j h p) -> (i j h) p", j=3, p=P)
                    sp.dma_start(prow[0:R_PS, :], wv).then_inc(param_in, 16)
                    sp.dma_start(prow[R_PS:R_ON, :], A["pool_scale"].rearrange("o (c p) -> (o c) p", p=P)).then_inc(param_in, 16)
                    sp.dma_start(prow[R_ON:R_ALL, :], A["w_onorm"]).then_inc(param_in, 16)
                    sp.dma_start(scrow, A["state_conv"].rearrange("o b j c -> (o b j) c")).then_inc(state_in, 16)
                    sp.dma_start(sprow[:, :], A["state_pool"].rearrange("o b j c -> (o b j) c")).then_inc(state_in, 16)
                    sp.dma_start(wab[:, :, :], A["w_in"][0, :, O_A:O_P].rearrange("(c p) n -> p c n", p=P)).then_inc(wab_in, 16)
                    sp.dma_start(dtb[:, :], A["dt_bias"].to_broadcast((P, H))).then_inc(wab_in, 16)
                    sp.dma_start(alog[:, :], A["a_log"].to_broadcast((P, H))).then_inc(wab_in, 16)
            sp.dma_start(wckv[:, :, :], A["w_ck"][0].rearrange("(c p) n -> p c n", p=P)).then_inc(wkv_in, 16)
            for g in range(2):
                load_pool(sp, g)
                if g == 0:
                    sp.wait_ge(unit_ready, U_KV + 4)
                    sp.dma_start(wckv[:, :, :], A["w_cv"][0].rearrange("(c p) n -> p c n", p=P)).then_inc(wkv_in, 16)
            for g in range(2, 4):
                load_pool(sp, g)
            sp.dma_start(O["pool_sample"][0, :, 0:PM - 1 - DS, :], A["state_pool"][0, :, DS:PM - 1, :]).then_inc(out_done, 16)
            sp.wait_ge(unit_out, U_POOL + 3 * PER_G + 7)
            for b in range(NB):
                sp.dma_start(O["pool_sample"][0, b, PM - 1 - DS:PM - 1, :], ptok[b * DS:(b + 1) * DS, :]).then_inc(out_done, 16)
            sp.dma_start(O["pool_prompt"][0, 0], ptail[:, :]).then_inc(out_done, 16)
            sp.wait_ge(out_done, 16 * (NB + 2))
            sp.wait_ge(kv_out[0], 32)
            sp.wait_ge(kv_out[1], 32)

        @block.tensor
        def _(pe):
            def begin(unit):
                if unit >= 8:
                    pe.wait_ge(unit_out, unit - 7)
                return bank[unit % 8]

            pe.wait_ge(const_in, 16)
            for t in range(NT + 2):
                pe.wait_ge(row_in[t % 2], 16 * (t // 2 + 1))
                n = nrow(t)
                for half in range(2):
                    b = begin(U_X + 2 * t + half)
                    for c in range(4):
                        k = 4 * half + c
                        mm = nc.tensor.transpose(b[:, c * P:c * P + n], rowbuf[0:n, t % 2, k * P:(k + 1) * P], M.ident[0:n, 0:n])
                    mm.then_inc(unit_ready, 1)
            b = begin(U_PAR)
            pe.wait_ge(param_in, 48)
            nc.tensor.transpose(b[:, 0:R_ALL], prow[:, :], M.ident[0:R_ALL, 0:R_ALL]).then_inc(unit_ready, 1)
            pe.wait_ge(state_in, 32)
            n = (CW - 1) * NB
            for half in range(2):
                b = begin(U_SC + half)
                for c in range(12):
                    k = 12 * half + c
                    mm = nc.tensor.transpose(b[:, c * n:(c + 1) * n], scrow[:, k * P:(k + 1) * P], M.ident[0:n, 0:n])
                mm.then_inc(unit_ready, 1)
            n = (PM - 1) * NB
            for half in range(2):
                b = begin(U_SP + half)
                for c in range(4):
                    k = 4 * half + c
                    mm = nc.tensor.transpose(b[:, c * n:(c + 1) * n], sprow[:, k * P:(k + 1) * P], M.ident[0:n, 0:n])
                mm.then_inc(unit_ready, 1)
            b = begin(U_AB)
            pe.wait_ge(wab_in, 48)
            pe.wait_ge(unit_out, U_X + 2 * NT)
            for t in range(NT):
                n = rows_of(t)
                for k in range(KC):
                    mm = nc.tensor.matmul(b[0:n, t * 2 * H:(t + 1) * 2 * H], M.xT[:, k, t * P:t * P + n], wab[:, k, :],
                                          start=(k == 0), stop=(k == KC - 1))
            mm.then_inc(unit_ready, 1)
            b = begin(U_GC)
            pe.wait_ge(dve_step, DVE_G)
            np_ = (NT - 1) * H
            gp = gtm[:, 0:NT - 1, :].rearrange("p t h -> p (t h)")
            nc.tensor.matmul(b[:, 0:np_], M.upper, gp, start=True, stop=True)
            nc.tensor.matmul(b[:, 64:64 + np_], M.ones, gp, start=True, stop=True)
            nc.tensor.matmul(b[0:NS, 128:128 + H], M.upper8[0:NS, 0:NS], gtm[0:NS, NT - 1, :], start=True, stop=True)
            nc.tensor.matmul(b[0:NS, 136:136 + H], M.block8[0:NS, 0:NS], gtm[0:NS, NT - 1, :], start=True, stop=True)
            nc.tensor.matmul(b[:, 192:256], M.ones[0:NS, :], gseq[:, :, :].rearrange("p b h -> p (b h)"),
                             start=True, stop=True).then_inc(unit_ready, 1)

            def memory(i):
                pe.wait_ge(wkv_in, 16 * (i // 2 + 1))
                pe.wait_ge(unit_out, U_X + 2 * (NT + 2))
                for half in range(2):
                    b = begin(U_KV + 2 * i + half)
                    for k in range(KC):
                        mm = nc.tensor.matmul(b[:, :], memT[:, k, (i % 2) * P:(i % 2 + 1) * P],
                                              wckv[:, k, half * 512:(half + 1) * 512], start=(k == 0), stop=(k == KC - 1))
                    mm.then_inc(unit_ready, 1)

            for i in range(4):
                memory(i)
            for g in range(4):
                base = U_POOL + g * PER_G

                def project(w, first):
                    for c in range(2):
                        for s, (at, n) in enumerate(SEGS):
                            b = begin(first + 3 * c + s)
                            for k in range(KC):
                                mm = nc.tensor.matmul(b[:, 0:n], w[:, k, c * P:(c + 1) * P], M.xT[:, k, at:at + n],
                                                      start=(k == 0), stop=(k == KC - 1))
                            mm.then_inc(unit_ready, 1)

                pe.wait_ge(wpool_in[0], 16 * (g + 1))
                project(wp, base)
                b = begin(base + 6)
                pe.wait_ge(unit_out, base + 6)
                pe.wait_ge(dve_step, DVE_ALL + g + 1)
                for c in range(2):
                    nc.tensor.transpose(b[0:NS, c * P:(c + 1) * P], pooled[:, c, SEQ:T], M.ident)
                    mm = nc.tensor.transpose(b[0:PM - 1, (2 + c) * P:(3 + c) * P], praw[:, c, SEQ:SEQ + PM - 1], M.ident)
                mm.then_inc(unit_ready, 1)
                pe.wait_ge(wpool_in[1], 16 * (g + 1))
                project(wg, base + 7)
                pe.wait_ge(wpool_in[2], 16 * (g + 1))
                pe.wait_ge(pooled_ready, g + 1)
                for c in range(2):
                    for s, (at, n) in enumerate(SEGS):
                        b = begin(base + 13 + 3 * c + s)
                        for k in range(2):
                            mm = nc.tensor.matmul(b[:, 0:n], wpool[:, k, c * P:(c + 1) * P], pooled[:, k, at:at + n],
                                                  start=(k == 0), stop=(k == 1))
                        mm.then_inc(unit_ready, 1)

        @block.scalar
        def _(act):
            def leave(unit):
                act.wait_ge(unit_ready, unit + 1)
                return bank[unit % 8]

            for t in range(NT + 2):
                n = nrow(t)
                for half in range(2):
                    b = leave(U_X + 2 * t + half)
                    v = b[:, :].rearrange("p (c n) -> p c n", n=P)[:, :, 0:n]
                    if t < NT:
                        dst = M.xT[:, 4 * half:4 * half + 4, t * P:t * P + n]
                    else:
                        dst = memT[:, 4 * half:4 * half + 4, (t - NT) * P:(t - NT + 1) * P]
                    nc.scalar.copy(dst, v).then_inc(unit_out, 1)
            b = leave(U_PAR)
            nc.scalar.copy(M.par[:, :], b[:, 0:R_ALL]).then_inc(unit_out, 1)
            for half in range(2):
                b = leave(U_SC + half)
                n = (CW - 1) * NB
                nc.scalar.copy(M.stateT[:, 12 * half:12 * half + 12, :], b[:, 0:12 * n].rearrange("p (c n) -> p c n", n=n)
                               ).then_inc(unit_out, 1)
            for half in range(2):
                b = leave(U_SP + half)
                n = (PM - 1) * NB
                nc.scalar.copy(statep[:, 4 * half:4 * half + 4, :], b[:, 0:4 * n].rearrange("p (c n) -> p c n", n=n)
                               ).then_inc(unit_out, 1)
            b = leave(U_AB)
            act.wait_ge(zeroed, 4)
            np_ = (NT - 1) * 2 * H
            nc.scalar.copy(ab[:, 0:NT - 1, :], b[:, 0:np_].rearrange("p (t n) -> p t n", n=2 * H))
            nc.scalar.copy(ab[0:NS, NT - 1, :], b[0:NS, np_:np_ + 2 * H]).then_inc(unit_out, 1)
            act.wait_ge(wab_in, 48)
            nc.scalar.activation(alog[:, :], alog[:, :], ACT.Exp).then_inc(act_step, 1)
            act.wait_ge(dve_step, DVE_ABS)
            nc.scalar.activation(u2[:, :, :], u2[:, :, :], ACT.Exp, scale=-1.0).then_inc(act_step, 1)
            act.wait_ge(act_step, 2)
            nc.scalar.activation(u2[:, :, :], u2[:, :, :], ACT.Ln, bias=1.0).then_inc(act_step, 1)
            act.wait_ge(unit_out, U_AB + 1)
            nc.scalar.activation(ab[:, :, H:2 * H], ab[:, :, H:2 * H], ACT.Tanh, scale=0.5).then_inc(act_step, 1)
            b = leave(U_GC)
            np_ = (NT - 1) * H
            nc.scalar.copy(M.scal[:, :, S_GC:S_GC + 8], b[:, 0:np_].rearrange("p (t h) -> p h t", h=H))
            nc.scalar.copy(M.scal[0:NS, :, S_GC + 8], b[0:NS, 128:128 + H])
            nc.scalar.copy(gl[:, 0:NT - 1, :], b[:, 64:64 + np_].rearrange("p (t h) -> p t h", h=H))
            nc.scalar.activation(M.scal[:, :, S_EGLS:S_EGLS + 8], b[:, 192:256].rearrange("p (b h) -> p h b", h=H), ACT.Exp)
            nc.scalar.activation(M.scal[:, :, S_EGL:S_EGL + 8], b[:, 64:64 + np_].rearrange("p (t h) -> p h t", h=H), ACT.Exp)
            nc.scalar.copy(gl[0:NS, NT - 1, :], b[0:NS, 136:136 + H]).then_inc(unit_out, 1)
            act.wait_ge(dve_step, DVE_ALL)
            nc.scalar.activation(M.scal[:, :, S_KG:S_KG + 9], M.scal[:, :, S_KG:S_KG + 9], ACT.Exp).then_inc(act_step, 1)
            nc.scalar.activation(M.scal[:, :, S_KBE:S_KBE + 9], M.scal[:, :, S_GC:S_GC + 9], ACT.Exp).then_inc(act_step, 1)
            for i in range(4):
                if i >= 2:
                    act.wait_ge(kv_out[i % 2], 16)
                for half in range(2):
                    b = leave(U_KV + 2 * i + half)
                    nc.scalar.copy(kvrow[:, i % 2, half * 512:(half + 1) * 512], b[:, :]).then_inc(unit_out, 1)
                out = O["mem_k"] if i < 2 else O["mem_v"]
                act.wait_ge(unit_out, U_KV + 2 * i + 2)
                act.dma_start(out[0, 0, (i % 2) * P:(i % 2 + 1) * P, :, :].rearrange("m h d -> m (h d)"),
                              kvrow[:, i % 2, :]).then_inc(kv_out[i % 2], 16)
            for g in range(4):
                base = U_POOL + g * PER_G
                if g:
                    act.wait_ge(pooled_ready, g)
                for c in range(2):
                    for s, (at, n) in enumerate(SEGS):
                        b = leave(base + 3 * c + s)
                        if at < SEQ:
                            nc.scalar.copy(praw[:, c, PM - 1 + at:PM - 1 + at + n], b[:, 0:n]).then_inc(unit_out, 1)
                        else:
                            nc.scalar.copy(psam[:, c, :, PM - 1:], b[:, 0:n].rearrange("p (b l) -> p b l", b=NB)
                                           ).then_inc(unit_out, 1)
                b = leave(base + 6)
                nc.scalar.copy(ptok[:, g * PG:(g + 1) * PG], b[0:NS, 0:PG])
                nc.scalar.copy(ptail[:, g * PG:(g + 1) * PG], b[0:PM - 1, PG:2 * PG]).then_inc(unit_out, 1)
                if g:
                    act.wait_ge(merged_ready, g)
                for c in range(2):
                    for s, (at, n) in enumerate(SEGS):
                        b = leave(base + 7 + 3 * c + s)
                        nc.scalar.activation(gate[:, c, at:at + n], b[:, 0:n], ACT.Tanh, scale=0.5).then_inc(unit_out, 1)
                act.wait_ge(dve_step, DVE_ALL + 1)
                for c in range(2):
                    for s, (at, n) in enumerate(SEGS):
                        b = leave(base + 13 + 3 * c + s)
                        nc.scalar.activation(M.mT[:, 2 * g + c, at:at + n], b[:, 0:n], ACT.Copy,
                                             scale=M.par[:, R_PS + 2 * g + c:R_PS + 2 * g + c + 1]).then_inc(unit_out, 1)

        @block.gpsimd
        def _(pool):
            nc.gpsimd.memset(ab[:, :, :], 0.0).then_inc(zeroed, 1)
            nc.gpsimd.memset(praw[:, :, 0:PM - 1], 0.0).then_inc(zeroed, 1)
            nc.gpsimd.memset(gl[:, :, :], 0.0).then_inc(zeroed, 1)
            nc.gpsimd.memset(M.scal[:, :, :], 0.0).then_inc(zeroed, 1)

        @block.vector
        def _(dve):
            link_sem = ctx.enter_context(nc.semaphore("a_link"))
            link_n = [0]

            def link(ins):
                link_n[0] += 1
                ins.then_inc(link_sem, 1)
                dve.wait_ge(link_sem, link_n[0])

            v = nc.vector
            dve.wait_ge(wab_in, 48)
            dve.wait_ge(unit_out, U_AB + 1)
            link(v.tensor_tensor(u[:, :, :], ab[:, :, 0:H], dtb[:, :].unsqueeze(1).to_broadcast((P, NT, H)), ALU.add))
            v.scalar_tensor_tensor(u2[:, :, :], u[:, :, :], -1.0, u[:, :, :], ALU.mult, ALU.max).then_inc(dve_step, 1)
            link(v.tensor_scalar(u[:, :, :], u[:, :, :], 0.0, None, ALU.max))
            dve.wait_ge(act_step, 3)
            link(v.tensor_tensor(u[:, :, :], u[:, :, :], u2[:, :, :], ALU.add))
            link(v.scalar_tensor_tensor(gtm[:, :, :], u[:, :, :], -1.0, alog[:, :].unsqueeze(1).to_broadcast((P, NT, H)),
                                        ALU.mult, ALU.mult))
            v.tensor_tensor(gseq[:, :, :], gtm[0:NS, NT - 1, :].unsqueeze(1).to_broadcast((NS, NB, H)),
                            M.inseq[0:NS, :].unsqueeze(2).to_broadcast((NS, NB, H)), ALU.mult).then_inc(dve_step, 1)
            dve.wait_ge(zeroed, 4)
            dve.wait_ge(act_step, 4)
            link(v.tensor_scalar(M.scal[:, :, S_BETA:S_BETA + 9], ab[:, :, H:2 * H].rearrange("p t h -> p h t"),
                                 0.5, 0.5, ALU.mult, ALU.add))
            dve.wait_ge(dve_step, DVE_G)
            v.tensor_copy(M.scal[:, :, S_G:S_G + 9], gtm[:, :, :].rearrange("p t h -> p h t"))
            dve.wait_ge(unit_out, U_GC + 1)
            v.tensor_tensor(M.scal[:, :, S_KG:S_KG + 9], gl[:, :, :].rearrange("p t h -> p h t"),
                            M.scal[:, :, S_GC:S_GC + 9], ALU.subtract).then_inc(dve_step, 1)
            dve.wait_ge(act_step, 6)
            link(v.tensor_tensor(M.scal[:, :, S_KBE:S_KBE + 9], M.scal[:, :, S_KBE:S_KBE + 9],
                                 M.scal[:, :, S_BETA:S_BETA + 9], ALU.mult))
            link(v.tensor_scalar(M.par[:, R_PS:R_ON], M.par[:, R_PS:R_ON], 0.5, None, ALU.mult))
            link(v.tensor_scalar(M.par[:, R_CONV:R_PS], M.par[:, R_CONV:R_PS], 0.5, None, ALU.mult))
            link(v.tensor_scalar(M.par[:, R_ON:R_ALL], M.par[:, R_ON:R_ALL], 0.25 * float(HD) ** 0.5, None, ALU.mult))
            for g in range(4):
                base = U_POOL + g * PER_G
                w = POOLW[g]
                v.tensor_copy(psam[:, :, :, 0:PM - 1], statep[:, 2 * g:2 * g + 2, :].rearrange("p c (b j) -> p c b j", b=NB))
                if g:
                    dve.wait_ge(unit_ready, base)
                dve.wait_ge(unit_out, base + 6)
                v.tensor_copy(pooled[:, :, SEQ:T].rearrange("p c (b l) -> p c b l", b=NB),
                              psam[:, :, :, PM - 1:]).then_inc(dve_step, 1)
                dve.wait_ge(dve_step, DVE_ALL + g + 1)
                a, s = praw, psam
                for lev in range(g + 1):
                    d = 1 << lev
                    lo = 2 * d - 1
                    for c in range(2):
                        dst = pw_a if lev % 2 == 0 else pooled
                        dc = dst[:, c, 0:PM - 1 + SEQ] if dst is pw_a else pooled[:, c, 0:PM - 1 + SEQ]
                        if c == 0 and lev % 2 == 1:
                            dve.wait_ge(unit_ready, base + 7)
                        v.tensor_tensor(dc[:, lo:], a[:, c, lo:PM - 1 + SEQ], a[:, c, lo - d:PM - 1 + SEQ - d], ALU.add)
                    sd = pw_as if lev % 2 == 0 else pw_bs
                    link(v.tensor_tensor(sd[:, :, :, lo:], s[:, :, :, lo:], s[:, :, :, lo - d:PM - 1 + DS - d], ALU.add))
                    a, s = dst, sd
                link(v.tensor_tensor(a[:, :, PM - 1:PM - 1 + w], a[:, :, PM - 1:PM - 1 + w],
                                     M.early[:, g, 0:w].unsqueeze(1).to_broadcast((P, 2, w)), ALU.mult))
                if a is pooled:
                    for c in range(2):
                        v.tensor_copy(pw_a[:, c, PM - 1:], pooled[:, c, PM - 1:PM - 1 + SEQ])
                    link(v.tensor_copy(pw_as[:, :, :, PM - 1:], s[:, :, :, PM - 1:]))
                dve.wait_ge(unit_ready, base + 7)
                for c in range(2):
                    v.scalar_tensor_tensor(pooled[:, c, 0:SEQ], pw_a[:, c, PM - 1:], 1.0 / w, praw[:, c, PM - 1:],
                                           ALU.mult, ALU.subtract)
                for c in range(2):
                    last = v.scalar_tensor_tensor(pooled[:, c, SEQ:T].rearrange("p (b l) -> p b l", b=NB), pw_as[:, c, :, PM - 1:],
                                                  1.0 / w, psam[:, c, :, PM - 1:], ALU.mult, ALU.subtract)
                last.then_inc(pooled_ready, 1)
                dve.wait_ge(pooled_ready, g + 1)
                dve.wait_ge(unit_out, base + PER_G)
                v.scalar_tensor_tensor(M.mT[:, 2 * g:2 * g + 2, :], gate[:, :, :], 1.0, M.mT[:, 2 * g:2 * g + 2, :],
                                       ALU.add, ALU.mult).then_inc(merged_ready, 1)
            dve.wait_ge(merged_ready, 4)


GROUPS = (("0", 4, LEVELS), ("1", 4, LEVELS), ("s", 1, SLEVELS))


def steps_b():
    pe, dv, ac, pl = [], [], [], []
    dv += ["head", "pack", "conv1", "conv0", "silu1", "silu0", "conv2", "silu2", "nk", "nq"]
    ac += ["cst", "tanh1", "tanh0", "sqk", "sqq", "tanh2", "rk", "rq"]
    for g, c, levels in GROUPS:
        pe += ["T" + g, "M" + g]
        dv += ["row" + g, "dec" + g, "A" + g, "PT" + g]
        ac += ["eA" + g, "eT" + g, "eR" + g]
        pl += ["tri" + g, "eB" + g, "eM" + g, "qg" + g]
        for n in range(levels):
            pe += [f"Z{g}{n}"] + ([f"W{g}{n}"] if n else [])
            dv += [f"X{g}{n}"]
            ac += [f"Z{g}{n}"] if n else []
            pl += [f"off{g}{n}"]
        pe += ["w" + g]
        ac += ["w" + g]
        if g == "s":
            pe += ["us", "vs", "vt", "os", "kvs"]
            ac += ["ut", "vn"]
            dv += ["vnT", "vexp", "oTs", "Ss"]
            pl += ["sdec"]
        else:
            for i in range(c):
                pe += [f"v{g}{i}", f"kv{g}{i}", f"o{g}{i}"]
                ac += [f"v{g}{i}"]
                dv += [f"S{g}{i}"]
            ac += ["o" + g]
    ac += ["tz", "tga", "sqo", "ro"]
    dv += ["z", "final"]
    return pe, dv, ac, pl


class Steps:

    def __init__(self, names, start=0):
        assert len(set(names)) == len(names)
        self.names = names
        self.per_head = len(names)
        self.start = start

    def before(self, h):
        return h * self.per_head + self.start

    def last(self, h, name):
        return h * self.per_head + (self.start - self.per_head + self.names.index(name) + 1)

    def __call__(self, h, name):
        return h * self.per_head + (self.start + self.names.index(name) + 1)


FILL = {"T": 0, "M": 5, "Z0": 1, "Z": 0.8, "W": 1.5, "w": 0.5, "v": 0.3, "kv": 0.3,
        "sM": 3, "sZ0": 0.5, "sZ": 0.8, "sW": 0.8, "sw": 0.8, "sv": 0.8, "svt": 0.8, "end": 99}
U_FIRST = 9
U_PER = 24
NP_UNITS = 5 * len(SEGS)
BODY = ((3, 0), (4, 0), (0, 1), (1, 1), (2, 1))


def fill_steps(n, done, steps, budget):
    budget[0] += n
    count = 0
    while done + count < steps and budget[0] > 0:
        budget[0] -= SEGS[(done + count) // KC % len(SEGS)][1] / 512
        count += 1
    return count


def phase_b(nc, A, O, M):
    with ExitStack() as ctx:
        def sb(name, shape, dt=F32):
            return ctx.enter_context(nc.sbuf_tensor(name, shape, dt))

        def sem(name):
            return ctx.enter_context(nc.semaphore(name))

        ring = [ctx.enter_context(nc.psum_tensor(f"b_ring{i}", [P, 512], F32)) for i in range(2)]
        b2, b3, b4, b5, b6, b7 = (ctx.enter_context(nc.psum_tensor(f"b_bank{i}", [P, 512], F32)) for i in range(2, 8))
        win = sb("win", [P, 5, KC, P])
        raw = sb("raw", [P, 3, CW - 1 + SEQ])
        raws = sb("raws", [P, 3, NB, CW - 1 + DS])
        zraw = sb("zraw", [P, T])
        garaw = sb("garaw", [P, T])
        cur = sb("cur", [P, 3, T])
        zc = sb("zc", [P, T])
        gc = sb("gc", [P, T])
        tmp = sb("tmp", [P, 2, T])
        oT = sb("oT", [P, T])
        ssq = sb("ssq", [P, T])
        wch = sb("wch", [P, CW, 3])
        sch = sb("sch", [P, S_ALL])
        pack = sb("pack", [P, 3, 27])
        cst = sb("cst", [27, 3, P])
        kbe, kg, vb, ET, PT, qg, nw, Zs, X, XT, tri = (sb(n, [P, 4, P]) for n in
                                                      ("kbe", "kg", "vb", "ET", "PT", "qg", "nw", "Zs", "X", "XT", "tri"))
        ea_a = sb("ea_a", [P, 2, 4, P])
        EA, Am = ea_a[:, 0], ea_a[:, 1]
        vexp = ea_a[0:NS].rearrange("p a c n -> p (a c) n")
        off = sb("off", [P, 2, 4, P])
        nwq = sb("nwq", [P, NB, 2 * DS])
        ut = sb("ut", [P, NS])
        vnT = sb("vnT", [P, P])
        qS = sb("qS", [P, NS])
        vnew = sb("vnew", [P, 2, P])
        S = sb("S", [P, 2, P])
        Sb = sb("Sb", [P, NB, P])

        w_in = [sem(f"w_in{f}") for f in range(5)]
        sb_in = sem("sb_in")
        filled = sem("filled")
        pe_s, dv_s, ac_s, pl_s = sem("pe_step"), sem("dve_step_b"), sem("act_step_b"), sem("pool_step")
        unit_ready, unit_out = sem("b_unit_ready"), sem("b_unit_out")
        pre = sem("b_zeroed")
        conv_out, dp_out, ds_out = sem("conv_out"), sem("dp_out"), sem("ds_out")
        link_s = sem("b_link")
        plink_s = sem("b_plink")
        PE, DV, AC, PL = (Steps(x, len(x)) for x in steps_b())

        w_feat = [j * H * HD for j in range(3)] + [O_Z, O_GA]

        def w_src(f, j):
            v = A["w_in"][0, :, w_feat[f]:w_feat[f] + H * HD].rearrange("(c p) (h n) -> p c h n", p=P, n=P)
            return v[:, :, j, :]

        block = ctx.enter_context(nc.Block())

        @block.sync
        def _(sp):
            for f in range(5):
                sp.dma_start(win[:, f, :, :], w_src(f, 0)).then_inc(w_in[f], 16)
            for f in range(3):
                sp.wait_ge(unit_ready, 3 * f + 3)
                sp.dma_start(win[:, f, :, :], w_src(f, 1)).then_inc(w_in[f], 16)

            def body(h, zload, load):
                sp.wait_ge(ds_out, 16 * h + 16)
                sp.dma_start(Sb[:, :, :], A["state_delta"][0].rearrange("b h k v -> k b h v")[:, :, h, :]).then_inc(sb_in, 16)
                sp.wait_ge(ac_s, AC(h, "cst"))
                cs = O["conv_sample"].rearrange("o b i (j h p) -> (o b i) j h p", j=3, p=P)
                cp = O["conv_prompt"].rearrange("o b i (j h p) -> (o b i) j h p", j=3, p=P)
                sp.dma_start(cs[:, :, h, :], cst[0:24, :, :]).then_inc(conv_out, 16)
                sp.dma_start(cp[:, :, h, :], cst[24:27, :, :]).then_inc(conv_out, 16)

                def load_w(f):
                    done = {3: 3, 4: 12, 0: 15, 1: 18, 2: 21}[f]
                    ahead = 1 if f > 2 else 2
                    if zload if f > 2 else load:
                        sp.wait_ge(unit_ready, h * U_PER + (U_FIRST + done))
                        sp.dma_start(win[:, f, :, :], w_src(f, h + ahead)).then_inc(w_in[f], 16)

                load_w(3)
                load_w(4)
                load_w(0)
                load_w(1)
                sp.wait_ge(dv_s, DV(h, "S13"))
                sp.dma_start(O["delta_prompt"][0, 0, h, :, :], S[:, 0, :]).then_inc(dp_out, 16)
                load_w(2)
                rows = M.y_rows[bass.ds(h * FILL_ROWS + MIN_SLOTS, FILL_ROWS), :].rearrange("(c p) d -> p c d", p=FILL_P)
                src = M.const[0:FILL_P, 4:4 + D].unsqueeze(1).to_broadcast((FILL_P, FILL_ROWS // FILL_P, D))
                sp.dma_start(rows, src).then_inc(filled, 16)
                sp.wait_ge(dv_s, DV(h, "Ss"))
                sp.dma_start(O["delta_sample"][0].rearrange("b h k v -> k b h v")[:, :, h, :], Sb[:, :, :]).then_inc(ds_out, 16)

            for out, n in ((conv_out, 32), (dp_out, 16), (ds_out, 16)):
                sp.sem_inc(out, n)
            with sp.Fori(0, H - 2) as h:
                body(h, True, True)
            body(H - 2, True, False)
            body(H - 1, False, False)
            sp.wait_ge(conv_out, 32 * H + 32)
            sp.wait_ge(dp_out, 16 * H + 16)
            sp.wait_ge(ds_out, 16 * H + 16)
            sp.wait_ge(filled, 16 * H)

        @block.tensor
        def _(pe):
            mm = nc.tensor.matmul
            tr = nc.tensor.transpose
            pe.sem_inc(pe_s, PE.start)

            def proj_step(j, f, i, base, pos):
                s, k = divmod(i, KC)
                at, n = SEGS[s]
                if k == 0:
                    if s == 0:
                        pe.wait_ge(w_in[f], (j + 1) * 16)
                    if isinstance(base, int) and base + pos < 2:
                        pass
                    else:
                        pe.wait_ge(unit_out, base + (pos - 1))
                m = mm(ring[pos % 2][:, 0:n], win[:, f, k, :], M.xT[:, k, at:at + n], start=(k == 0), stop=(k == KC - 1))
                if k == KC - 1:
                    m.then_inc(unit_ready, 1)

            for f in range(3):
                for i in range(3 * KC):
                    proj_step(0, f, i, 0, 3 * f + i // KC)

            def body(h, more):
                base = h * U_PER
                pos = [U_FIRST]
                nxt = [0]
                steps = (NP_UNITS if more else 6) * KC
                budget = [0.0]

                def fill(n):
                    for _ in range(fill_steps(n, nxt[0], steps, budget)):
                        feature, i = divmod(nxt[0], 3 * KC)
                        f, ahead = BODY[feature]
                        proj_step(h + ahead, f, i, base, pos[0])
                        nxt[0] += 1
                        if nxt[0] % KC == 0:
                            pos[0] += 1

                def ring_bank():
                    pe.wait_ge(unit_out, base + (pos[0] - 1))
                    b = ring[pos[0] % 2]
                    pos[0] += 1
                    return b

                fill(17)
                pe.wait_ge(dv_s, DV(h, "pack"))
                b = ring_bank()
                for j in range(3):
                    m = tr(b[0:27, j * P:(j + 1) * P], pack[:, j, :], M.ident)
                m.then_inc(unit_ready, 1)
                fill(8)
                pe.wait_ge(ac_s, AC(h, "sqk"))
                for half in range(2):
                    mm(ring_bank()[:, :], M.ones, tmp[:, 0, half * 512:half * 512 + 512], start=True, stop=True).then_inc(unit_ready, 1)
                pe.wait_ge(ac_s, AC(h, "sqq"))
                for half in range(2):
                    mm(ring_bank()[:, :], M.ones, tmp[:, 1, half * 512:half * 512 + 512], start=True, stop=True).then_inc(unit_ready, 1)
                mm(ring_bank()[:, 0:2 * NS].rearrange("p (a n) -> p a n", a=2), M.ones, tmp[:, :, SEQ:T],
                   start=True, stop=True).then_inc(unit_ready, 1)
                fill(9)

                for g, nch, levels in GROUPS:
                    smp = g == "s"
                    n = NS if smp else P
                    at = [SEQ] if smp else [(4 * int(g) + c) * P for c in range(4)]
                    f_ = (lambda key: FILL.get("s" + key, 0)) if smp else (lambda key: FILL.get(key, 0))
                    if g == "0":
                        pe.wait_ge(dv_s, DV(h, "nq"))
                    elif g == "1":
                        pe.wait_ge(dv_s, DV(h, "S03"))
                    else:
                        pe.wait_ge(dv_s, DV(h, "S13"))
                    for c in range(nch):
                        tr(b2[:, c * P:(c + 1) * P], cur[:, 1:3, :].rearrange("p j t -> p (j t)")[:, at[c]:at[c] + P], M.ident)
                    for c in range(nch):
                        m = tr(b3[0:n, c * P:(c + 1) * P], cur[:, 2, at[c]:at[c] + n], M.ident)
                    m.then_inc(pe_s, 1)
                    fill(f_("T"))
                    if g != "0":
                        pe.wait_ge(ac_s, AC(h, "o" + {"1": "0", "s": "1"}[g]))
                    for c in range(nch):
                        mm(b4[0:n, c * P:c * P + n], cur[:, 1, at[c]:at[c] + n], cur[:, 1, at[c]:at[c] + n], start=True, stop=True)
                        mm(b5[0:n, c * P:c * P + n], cur[:, 1, at[c]:at[c] + n], cur[:, 0, at[c]:at[c] + n], start=True, stop=True)
                    pe.wait_ge(pl_s, PL(h, "tri" + g))
                    for c in range(nch):
                        m = mm(b6[:, c * P:c * P + n], M.ones[0:n, :], tri[0:n, c, 0:n], start=True, stop=True)
                    m.then_inc(pe_s, 1)
                    fill(f_("M"))
                    pe.wait_ge(dv_s, DV(h, "row" + g))
                    for lev in range(levels):
                        pe.wait_ge(pl_s, PL(h, f"off{g}{lev}"))
                        if lev:
                            pe.wait_ge(dv_s, DV(h, f"X{g}{lev - 1}"))
                        for c in range(nch):
                            rhs = XT[0:n, c, 0:n] if lev else M.ident[0:n, 0:n]
                            m = mm(b2[:, c * P:c * P + n], off[0:n, lev % 2, c, :], rhs, start=True, stop=True)
                        m.then_inc(pe_s, 1)
                        if lev == 0:
                            fill(f_("Z0"))
                            continue
                        fill(f_("Z"))
                        pe.wait_ge(ac_s, AC(h, f"Z{g}{lev}"))
                        for c in range(nch):
                            m = mm(b3[:, c * P:c * P + n], X[0:n, c, :], Zs[0:n, c, 0:n], start=True, stop=True)
                        if lev < levels - 1:
                            for c in range(nch):
                                m = mm(b7[0:n, c * P:c * P + n], Zs[0:n, c, 0:n], X[0:n, c, 0:n], start=True, stop=True)
                        m.then_inc(pe_s, 1)
                        fill(f_("W"))
                    pe.wait_ge(dv_s, DV(h, f"X{g}{levels - 1}"))
                    for c in range(nch):
                        m = mm(b4[:, c * P:c * P + n], kbe[0:n, c, :], XT[0:n, c, 0:n], start=True, stop=True)
                    m.then_inc(pe_s, 1)
                    fill(f_("w"))
                    if smp:
                        break
                    for c in range(4):
                        cc = 4 * int(g) + c
                        if c == 0:
                            pe.wait_ge(dv_s, DV(h, "PT" + g))
                        mm(b5[:, 0:P], XT[:, c, :], vb[:, c, :], start=True, stop=False)
                        if c == 0:
                            pe.wait_ge(ac_s, AC(h, "w" + g))
                            pe.wait_ge(pl_s, PL(h, "qg" + g))
                        elif c or g == "1":
                            prev = f"S{g}{c - 1}"
                            pe.wait_ge(dv_s, DV(h, prev))
                        mm(b5[:, 0:P], nw[:, c, :], S[:, cc % 2, :], start=False, stop=True).then_inc(pe_s, 1)
                        mm(b6[:, c * P:(c + 1) * P], S[:, cc % 2, :], qg[:, c, :], start=True, stop=False)
                        fill(f_("v"))
                        pe.wait_ge(ac_s, AC(h, f"v{g}{c}"))
                        mm(b3[:, 0:P], kg[:, c, :], vnew[:, c % 2, :], start=True, stop=True).then_inc(pe_s, 1)
                        mm(b6[:, c * P:(c + 1) * P], vnew[:, c % 2, :], PT[:, c, :], start=False, stop=True).then_inc(pe_s, 1)
                        fill(f_("kv"))
                mm(b3[:, 0:NS], vb[0:NS, 0, :], XT[0:NS, 0, 0:NS], start=True, stop=True).then_inc(pe_s, 1)
                pe.wait_ge(sb_in, (h + 1) * 16)
                pe.wait_ge(ac_s, AC(h, "ws"))
                pe.wait_ge(pl_s, PL(h, "qgs"))
                pe.wait_ge(dv_s, DV(h, "PTs"))
                for b in range(NB):
                    m = mm(b5[:, b * 2 * DS:(b + 1) * 2 * DS], Sb[:, b, :], nwq[:, b, :], start=True, stop=True)
                m.then_inc(pe_s, 1)
                fill(FILL["sv"])
                pe.wait_ge(dv_s, DV(h, "vnT"))
                tr(b2[:, 0:P], vnT[:, :], M.ident).then_inc(pe_s, 1)
                fill(FILL["svt"])
                pe.wait_ge(ac_s, AC(h, "vn"))
                pe.wait_ge(ac_s, AC(h, "eRs"))
                mm(b6[:, 0:NS], vnew[0:NS, 0, :], PT[0:NS, 0, 0:NS], start=True, stop=True).then_inc(pe_s, 1)
                pe.wait_ge(dv_s, DV(h, "vexp"))
                mm(b3[:, :], kg[0:NS, 0, :], vexp[:, 0:4, :], start=True, stop=True)
                mm(b7[:, :], kg[0:NS, 0, :], vexp[:, 4:8, :], start=True, stop=True).then_inc(pe_s, 1)
                fill(FILL["end"])
                pe.wait_ge(ac_s, AC(h, "sqo"))
                for at, n in SEGS:
                    mm(ring_bank()[:, 0:n], M.ones, tmp[:, 0, at:at + n], start=True, stop=True).then_inc(unit_ready, 1)

            with pe.Fori(0, H - 1) as h:
                body(h, True)
            body(H - 1, False)

        @block.scalar
        def _(act):
            a = nc.scalar
            act.sem_inc(ac_s, AC.start)

            def proj_out(f, s, base, pos):
                at, n = SEGS[s]
                act.wait_ge(unit_ready, base + (pos + 1))
                b = ring[pos % 2]
                if f < 3 and s < 2:
                    dst, src = raw[:, f, CW - 1 + at:CW - 1 + at + n], b[:, 0:n]
                elif f < 3:
                    dst, src = raws[:, f, :, CW - 1:], b[:, 0:n].rearrange("p (b l) -> p b l", b=NB)
                else:
                    dst, src = (zraw, garaw)[f - 3][:, at:at + n], b[:, 0:n]
                a.copy(dst, src).then_inc(unit_out, 1)

            act.wait_ge(pre, 2)
            for unit in range(3 * len(SEGS)):
                proj_out(unit // len(SEGS), unit % len(SEGS), 0, unit)

            def body(h, more):
                base = h * U_PER
                pos = [U_FIRST]
                nxt = [0]

                steps = (NP_UNITS if more else 6) * KC
                budget = [0.0]

                def fill(n):
                    for _ in range(fill_steps(n, nxt[0], steps, budget)):
                        nxt[0] += 1
                        if nxt[0] % KC == 0:
                            unit = nxt[0] // KC - 1
                            f = BODY[unit // 3][0]
                            if unit % 3 == 0:
                                if f == 3:
                                    act.wait_ge(dv_s, DV.last(h, "z"))
                                elif f == 4:
                                    act.wait_ge(ac_s, AC.last(h, "tga"))
                                else:
                                    act.wait_ge(dv_s, DV(h, f"conv{f}"))
                            proj_out(f, unit % 3, base, pos[0])
                            pos[0] += 1

                def leave():
                    act.wait_ge(unit_ready, base + (pos[0] + 1))
                    b = ring[pos[0] % 2]
                    pos[0] += 1
                    return b

                fill(17)
                act.wait_ge(conv_out, 32 * h + 32)
                b = leave()
                a.copy(cst[:, :, :], b[0:27, 0:3 * P].rearrange("p (j n) -> p j n", j=3)).then_inc(unit_out, 1)
                act.wait_ge(unit_out, base + pos[0])
                a.nop().then_inc(ac_s, 1)
                act.wait_ge(dv_s, DV(h, "conv1"))
                act.wait_ge(unit_out, base + U_FIRST)
                a.activation(tmp[:, 0, :], cur[:, 1, :], ACT.Tanh).then_inc(ac_s, 1)
                act.wait_ge(dv_s, DV(h, "conv0"))
                a.activation(tmp[:, 1, :], cur[:, 0, :], ACT.Tanh).then_inc(ac_s, 1)
                fill(8)
                act.wait_ge(dv_s, DV(h, "silu1"))
                a.activation(tmp[:, 0, :], cur[:, 1, :], ACT.Square).then_inc(ac_s, 1)
                act.wait_ge(dv_s, DV(h, "silu0"))
                a.activation(tmp[:, 1, :], cur[:, 0, :], ACT.Square, scale=float(HD) ** 0.5).then_inc(ac_s, 1)
                act.wait_ge(dv_s, DV(h, "conv2"))
                a.activation(zc[:, :], cur[:, 2, :], ACT.Tanh).then_inc(ac_s, 1)
                for half in range(2):
                    a.activation(oT[:, half * 512:half * 512 + 512], leave()[:, :], ACT.Ln, bias=M.eps).then_inc(unit_out, 1)
                for half in range(2):
                    a.activation(ssq[:, half * 512:half * 512 + 512], leave()[:, :], ACT.Ln, bias=M.epshd).then_inc(unit_out, 1)
                b = leave()
                a.activation(oT[:, SEQ:T], b[:, 0:NS], ACT.Ln, bias=M.eps)
                a.activation(ssq[:, SEQ:T], b[:, NS:2 * NS], ACT.Ln, bias=M.epshd).then_inc(unit_out, 1)
                act.wait_ge(unit_out, base + pos[0])
                a.activation(oT[:, :], oT[:, :], ACT.Exp, scale=-0.5).then_inc(ac_s, 1)
                a.activation(ssq[:, :], ssq[:, :], ACT.Exp, scale=-0.5).then_inc(ac_s, 1)
                fill(9)

                for g, nch, levels in GROUPS:
                    smp = g == "s"
                    n = NS if smp else P
                    f_ = (lambda key: FILL.get("s" + key, 0)) if smp else (lambda key: FILL.get(key, 0))
                    fill(f_("T"))

                    def grid(b, rows=n):
                        return b[0:rows, 0:nch * P].rearrange("p (c n) -> p c n", n=P)[:, :, 0:n]

                    act.wait_ge(dv_s, DV(h, "dec" + g))
                    a.activation(EA[0:n, 0:nch, 0:n], EA[0:n, 0:nch, 0:n], ACT.Exp).then_inc(ac_s, 1)
                    a.activation(ET[0:n, 0:nch, 0:n], ET[0:n, 0:nch, 0:n], ACT.Exp).then_inc(ac_s, 1)
                    a.activation(qg[:, 0:nch, 0:n], grid(b6, P), ACT.Exp).then_inc(ac_s, 1)
                    fill(f_("M"))
                    for lev in range(levels):
                        if lev == 0:
                            fill(f_("Z0"))
                            continue
                        act.wait_ge(pe_s, PE(h, f"Z{g}{lev}"))
                        a.copy(Zs[0:n, 0:nch, 0:n], grid(b2)).then_inc(ac_s, 1)
                        fill(f_("Z"))
                        fill(f_("W"))
                    act.wait_ge(pe_s, PE(h, "w" + g))
                    if smp:
                        a.mul(nwq[:, :, 0:DS], b4[:, 0:NS].rearrange("p (b l) -> p b l", b=NB), -1.0).then_inc(ac_s, 1)
                        fill(f_("w"))
                        break
                    a.mul(nw[:, :, :], grid(b4), -1.0).then_inc(ac_s, 1)
                    fill(f_("w"))
                    for c in range(4):
                        act.wait_ge(pe_s, PE(h, f"v{g}{c}"))
                        a.copy(vnew[:, c % 2, :], b5[:, 0:P]).then_inc(ac_s, 1)
                        fill(f_("v"))
                        fill(f_("kv"))
                    act.wait_ge(pe_s, PE(h, f"o{g}3"))
                    a.copy(oT[:, int(g) * 512:int(g) * 512 + 512], b6[:, :]).then_inc(ac_s, 1)
                act.wait_ge(pe_s, PE(h, "us"))
                a.copy(ut[:, :], b3[:, 0:NS]).then_inc(ac_s, 1)
                fill(FILL["sv"])
                act.wait_ge(pe_s, PE(h, "vt"))
                a.copy(vnew[0:NS, 0, :], b2[0:NS, 0:P]).then_inc(ac_s, 1)
                fill(FILL["svt"])
                fill(FILL["end"])
                act.wait_ge(dv_s, DV(h, "silu2"))
                a.activation(zc[:, :], zraw[:, :], ACT.Tanh, scale=0.5).then_inc(ac_s, 1)
                a.activation(gc[:, :], garaw[:, :], ACT.Tanh, scale=0.5).then_inc(ac_s, 1)
                act.wait_ge(dv_s, DV(h, "oTs"))
                a.activation(tmp[:, 0, :], oT[:, :], ACT.Square).then_inc(ac_s, 1)
                for at, n in SEGS:
                    a.activation(ssq[:, at:at + n], leave()[:, 0:n], ACT.Ln, bias=M.epshd).then_inc(unit_out, 1)
                act.wait_ge(unit_out, base + pos[0])
                a.activation(ssq[:, :], ssq[:, :], ACT.Exp, scale=-0.5).then_inc(ac_s, 1)

            with act.Fori(0, H - 1) as h:
                body(h, True)
            body(H - 1, False)

        @block.gpsimd
        def _(pool):
            g_ = nc.gpsimd
            pool.sem_inc(pl_s, PL.start)
            g_.memset(vnT[:, :], 0.0).then_inc(pre, 1)
            g_.memset(raw[:, :, 0:CW - 1], 0.0).then_inc(pre, 1)

            def body(h):
                for g, nch, levels in GROUPS:
                    smp = g == "s"
                    n = NS if smp else P
                    t0 = 8 if smp else 4 * int(g)
                    causal = M.upper8 if smp else M.upper

                    def col(base):
                        return sch[0:n, base + t0:base + t0 + nch].unsqueeze(2).to_broadcast((n, nch, n))

                    def cols(m):
                        return m[0:n, 0:n].unsqueeze(1).to_broadcast((n, nch, n))

                    pool.wait_ge(dv_s, DV(h, "head"))
                    if g != "0":
                        pool.wait_ge(pe_s, PE(h, "M" + {"1": "0", "s": "1"}[g]))
                    g_.tensor_tensor(tri[0:n, 0:nch, 0:n], cols(causal), col(S_G), ALU.mult).then_inc(pl_s, 1)
                    pool.wait_ge(ac_s, AC(h, "eA" + g))
                    g_.tensor_tensor(EA[0:n, 0:nch, 0:n], EA[0:n, 0:nch, 0:n], col(S_BETA), ALU.mult).then_inc(pl_s, 1)
                    pool.wait_ge(ac_s, AC(h, "eT" + g))
                    g_.tensor_tensor(ET[0:n, 0:nch, 0:n], ET[0:n, 0:nch, 0:n], cols(causal), ALU.mult).then_inc(pl_s, 1)
                    pool.wait_ge(ac_s, AC(h, "eR" + g))
                    if smp:
                        g_.tensor_tensor(nwq[:, :, DS:], qg[:, 0, 0:NS].rearrange("p (b l) -> p b l", b=NB),
                                         cur[:, 0, SEQ:T].rearrange("p (b l) -> p b l", b=NB), ALU.mult).then_inc(pl_s, 1)
                    else:
                        g_.tensor_tensor(qg[:, :, :], qg[:, :, :], cur[:, 0, int(g) * 512:int(g) * 512 + 512]
                                         .rearrange("p (c n) -> p c n", n=P), ALU.mult).then_inc(pl_s, 1)
                    for lev in range(levels):
                        if lev == 0:
                            pool.wait_ge(dv_s, DV(h, "A" + g))
                        if lev == 2:
                            pool.wait_ge(dv_s, DV(h, f"X{g}0"))
                        elif lev > 2:
                            pool.wait_ge(pe_s, PE(h, f"Z{g}{lev - 2}"))
                        g_.tensor_tensor(off[0:n, lev % 2, 0:nch, 0:n], Am[0:n, 0:nch, 0:n], cols(M.level[:, lev, :]),
                                         ALU.mult).then_inc(pl_s, 1)
                pool.wait_ge(pe_s, PE(h, "vs"))
                g_.tensor_tensor(Sb[:, :, :], Sb[:, :, :], sch[:, S_EGLS:S_EGLS + NB].unsqueeze(2).to_broadcast((P, NB, P)),
                                 ALU.mult).then_inc(pl_s, 1)

            with pool.Fori(0, H) as h:
                body(h)

        @block.vector
        def _(dve):
            v = nc.vector
            dve.sem_inc(dv_s, DV.start)

            def body(h):
                n_link = [0]

                def link(ins):
                    n_link[0] += 1
                    ins.then_inc(link_s, 1)
                    dve.wait_ge(link_s, n_link[0])

                dve.sem_clear(link_s)
                dve.wait_ge(pl_s, PL.before(h))
                dve.wait_ge(unit_out, h * U_PER + U_FIRST)
                v.tensor_copy(wch[:, :, :], M.par[:, R_CONV:R_PS].rearrange("p (i j h) -> p i j h", i=CW, j=3)[:, :, :, h])
                v.tensor_copy(raws[:, :, :, 0:CW - 1], M.stateT.rearrange("p (j h) n -> p j h n", j=3)[:, :, h, :]
                              .rearrange("p j (b i) -> p j b i", b=NB))
                v.tensor_copy(sch[:, :], M.scal[:, h, :]).then_inc(dv_s, 1)
                dve.wait_ge(dv_s, DV(h, "head"))
                v.tensor_copy(pack[:, :, 0:24].rearrange("p j (b i) -> p j b i", b=NB), raws[:, :, :, DS:])
                v.tensor_copy(pack[:, :, 24:27], raw[:, :, SEQ:]).then_inc(dv_s, 1)
                dve.wait_ge(pe_s, PE.before(h))
                dve.wait_ge(dp_out, 16 * h + 16)
                link(v.memset(S[:, 0, :], 0.0))

                def conv(j):
                    cs = cur[:, j, SEQ:T].rearrange("p (b l) -> p b l", b=NB)
                    v.tensor_scalar(cur[:, j, 0:SEQ], raw[:, j, 0:SEQ], wch[:, 0, j:j + 1], None, ALU.mult)
                    link(v.tensor_scalar(cs, raws[:, j, :, 0:DS], wch[:, 0, j:j + 1], None, ALU.mult))
                    for i in range(1, CW):
                        v.scalar_tensor_tensor(cur[:, j, 0:SEQ], raw[:, j, i:i + SEQ], wch[:, i, j:j + 1],
                                               cur[:, j, 0:SEQ], ALU.mult, ALU.add)
                        ins = v.scalar_tensor_tensor(cs, raws[:, j, :, i:i + DS], wch[:, i, j:j + 1], cs, ALU.mult, ALU.add)
                        if i < CW - 1:
                            link(ins)
                    ins.then_inc(dv_s, 1)

                def silu(j, tanh):
                    dve.wait_ge(ac_s, AC(h, f"tanh{j}"))
                    v.scalar_tensor_tensor(cur[:, j, :], tanh, 1.0, cur[:, j, :], ALU.add, ALU.mult).then_inc(dv_s, 1)

                conv(1)
                conv(0)
                silu(1, tmp[:, 0, :])
                silu(0, tmp[:, 1, :])
                conv(2)
                silu(2, zc[:, :])
                dve.wait_ge(ac_s, AC(h, "rk"))
                v.tensor_tensor(cur[:, 1, :], cur[:, 1, :], oT[:, :], ALU.mult).then_inc(dv_s, 1)
                dve.wait_ge(ac_s, AC(h, "rq"))
                v.tensor_tensor(cur[:, 0, :], cur[:, 0, :], ssq[:, :], ALU.mult).then_inc(dv_s, 1)
                for g, nch, levels in GROUPS:
                    smp = g == "s"
                    n = NS if smp else P
                    t0 = 8 if smp else 4 * int(g)

                    def col(base, m):
                        return sch[0:n, base + t0:base + t0 + nch].unsqueeze(2).to_broadcast((n, nch, m))

                    def grid(b, m=n):
                        return b[0:n, 0:nch * P].rearrange("p (c n) -> p c n", n=P)[:, :, 0:m]

                    dve.wait_ge(pe_s, PE(h, "T" + g))
                    v.tensor_tensor(kbe[0:n, 0:nch, :], grid(b2, P), col(S_KBE, P), ALU.mult)
                    v.tensor_tensor(kg[0:n, 0:nch, :], grid(b2, P), col(S_KG, P), ALU.mult)
                    v.tensor_tensor(vb[0:n, 0:nch, :], grid(b3, P), col(S_BETA, P), ALU.mult).then_inc(dv_s, 1)
                    dve.wait_ge(pe_s, PE(h, "M" + g))
                    link(v.tensor_tensor(EA[0:n, 0:nch, 0:n], grid(b6), col(S_GC, n), ALU.subtract))
                    link(v.tensor_scalar(ET[0:n, 0:nch, 0:n], EA[0:n, 0:nch, 0:n], 0.0, None, ALU.min))
                    v.tensor_scalar(EA[0:n, 0:nch, 0:n], EA[0:n, 0:nch, 0:n], -1.0, 0.0, ALU.mult, ALU.min).then_inc(dv_s, 1)
                    dve.wait_ge(pl_s, PL(h, "eB" + g))
                    v.tensor_tensor(Am[0:n, 0:nch, 0:n], grid(b4), EA[0:n, 0:nch, 0:n], ALU.mult).then_inc(dv_s, 1)
                    dve.wait_ge(pl_s, PL(h, "eM" + g))
                    v.tensor_tensor(PT[0:n, 0:nch, 0:n], grid(b5), ET[0:n, 0:nch, 0:n], ALU.mult).then_inc(dv_s, 1)
                    ident = M.ident[0:n, 0:n].unsqueeze(1).to_broadcast((n, nch, n))
                    for lev in range(levels):
                        if lev == 0:
                            dve.wait_ge(pe_s, PE(h, f"Z{g}0"))
                            v.tensor_tensor(XT[0:n, 0:nch, 0:n], ident, grid(b2), ALU.subtract)
                            v.tensor_tensor(X[0:n, 0:nch, 0:n], ident, off[0:n, 0, 0:nch, 0:n], ALU.subtract).then_inc(dv_s, 1)
                            continue
                        dve.wait_ge(dv_s, DV(h, f"X{g}{lev - 1}"))
                        dve.wait_ge(pe_s, PE(h, f"W{g}{lev}"))
                        ins = v.tensor_tensor(XT[0:n, 0:nch, 0:n], XT[0:n, 0:nch, 0:n], grid(b3), ALU.subtract)
                        if lev < levels - 1:
                            ins = v.tensor_tensor(X[0:n, 0:nch, 0:n], X[0:n, 0:nch, 0:n], grid(b7), ALU.subtract)
                        ins.then_inc(dv_s, 1)
                    if smp:
                        break
                    for c in range(4):
                        cc = 4 * int(g) + c
                        if c or g == "1":
                            prev = f"S{g}{c - 1}" if c else "S03"
                            dve.wait_ge(dv_s, DV(h, prev))
                        dve.wait_ge(pe_s, PE(h, f"kv{g}{c}"))
                        v.scalar_tensor_tensor(S[:, (cc + 1) % 2, :], S[:, cc % 2, :], sch[:, S_EGL + cc:S_EGL + cc + 1],
                                               b3[:, 0:P], ALU.mult, ALU.add).then_inc(dv_s, 1)
                dve.wait_ge(ac_s, AC(h, "ut"))
                dve.wait_ge(pe_s, PE(h, "vs"))
                sv = b5[:, 0:2 * NS].rearrange("p (b l) -> p b l", b=NB)
                v.tensor_copy(qS.rearrange("p (b l) -> p b l", b=NB), sv[:, :, DS:])
                v.tensor_tensor(vnT[:, 0:NS].rearrange("p (b l) -> p b l", b=NB), sv[:, :, 0:DS],
                                ut.rearrange("p (b l) -> p b l", b=NB), ALU.add).then_inc(dv_s, 1)
                dve.wait_ge(ac_s, AC(h, "vn"))
                v.tensor_tensor(vexp, vnew[0:NS, 0, :].unsqueeze(1).to_broadcast((NS, NB, P)),
                                M.inseq[0:NS, :].unsqueeze(2).to_broadcast((NS, NB, P)), ALU.mult).then_inc(dv_s, 1)
                dve.wait_ge(pe_s, PE(h, "os"))
                v.tensor_tensor(oT[:, SEQ:T], b6[:, 0:NS], qS[:, :], ALU.add).then_inc(dv_s, 1)
                dve.wait_ge(pe_s, PE(h, "kvs"))
                dve.wait_ge(pl_s, PL(h, "sdec"))
                v.tensor_tensor(Sb[:, 0:4, :], Sb[:, 0:4, :], b3[:, :].rearrange("p (b n) -> p b n", n=P), ALU.add)
                v.tensor_tensor(Sb[:, 4:8, :], Sb[:, 4:8, :], b7[:, :].rearrange("p (b n) -> p b n", n=P), ALU.add).then_inc(dv_s, 1)
                dve.wait_ge(ac_s, AC(h, "tz"))
                v.scalar_tensor_tensor(zc[:, :], zc[:, :], 1.0, zraw[:, :], ALU.add, ALU.mult).then_inc(dv_s, 1)
                dve.wait_ge(dv_s, DV(h, "z"))
                dve.wait_ge(ac_s, AC(h, "ro"))
                link(v.tensor_tensor(oT[:, :], oT[:, :], ssq[:, :], ALU.mult))
                link(v.scalar_tensor_tensor(oT[:, :], oT[:, :], M.par[:, R_ON:R_ALL], zc[:, :], ALU.mult, ALU.mult))
                link(v.scalar_tensor_tensor(oT[:, :], gc[:, :], 1.0, oT[:, :], ALU.add, ALU.mult))
                v.tensor_tensor(M.mT[:, h, :], M.mT[:, h, :], oT[:, :], ALU.add).then_inc(dv_s, 1)
                dve.wait_ge(dv_s, DV(h, "final"))

            with dve.Fori(0, H - 1) as h:
                body(h)
            body(H - 1)


def layer_norm_rows(v, link, r, stats, mv, n):
    v.bn_stats(stats[0:n, 0, :], r[0:n, 0:512])
    link(v.bn_stats(stats[0:n, 1, :], r[0:n, 512:D]))
    return v.bn_aggr(mv[0:n, :], stats[0:n, :, :])


def steps_c():
    pe, dv, ac, pl = [], [], [], []
    for t in range(NT):
        pe += [f"y{t}"]
        dv += [f"r{t}", f"v{t}", f"n{t}"]
        ac += [f"s{t}"]
        pl += [f"x{t}"]
        if t:
            pe += [f"t{t - 1}"]
            ac += [f"t{t - 1}"]
    pe += [f"t{NT - 1}", "kt"]
    ac += [f"t{NT - 1}", "kt"]
    for u in range(KC * len(SEGS)):
        pe += [f"q{u}"]
        ac += [f"q{u}"]
    pl += ["qpad"]
    for t in range(NT - 1):
        pe += [f"S{t}"]
        dv += [f"m{t}"]
        ac += [f"e{t}"]
        dv += [f"p{t}"]
        if t:
            pe += [f"Y{t - 1}"]
            dv += [f"R{t - 1}", f"V{t - 1}", f"N{t - 1}"]
            pl += [f"X{t - 1}"]
        if t > 1:
            pe += [f"T{t - 2}", f"G{t - 2}"]
            ac += [f"T{t - 2}", f"G{t - 2}"]
        if t:
            ac += [f"s_{t - 1}"]
        pe += [f"P{t}", f"O{t}"]
        ac += [f"P{t}", f"O{t}"]
    t = NT - 1
    pe += [f"Y{t - 1}"]
    dv += [f"R{t - 1}", f"V{t - 1}", f"N{t - 1}"]
    ac += [f"s_{t - 1}"]
    pl += [f"X{t - 1}"]
    pe += ["K0"]
    ac += ["K0"]
    for b in range(NB):
        ahead = [f"K{b + 1}"] if b + 1 < NB else []
        pe += [f"s{b}"] + ahead + [f"p{b}", f"o{b}"]
        ac += [f"e_{b}", f"p{b}"] + ahead + [f"o{b}"]
        dv += [f"m_{b}", f"p_{b}"]
    for i in (t - 2, t - 1):
        pe += [f"T{i}", f"G{i}"]
        ac += [f"T{i}", f"G{i}"]
    pe += [f"Y{t}"]
    dv += [f"R{t}", f"V{t}", f"N{t}"]
    ac += [f"s_{t}"]
    pl += [f"X{t}"]
    pe += [f"T{t}", f"G{t}"]
    ac += [f"T{t}", f"G{t}"]
    return pe, dv, ac, pl


def phase_c(nc, A, O, M):
    with ExitStack() as ctx:
        def sb(name, shape, dt=F32):
            return ctx.enter_context(nc.sbuf_tensor(name, shape, dt))

        def sem(name):
            return ctx.enter_context(nc.semaphore(name))

        bank = [ctx.enter_context(nc.psum_tensor(f"c_bank{i}", [P, 512], F32)) for i in range(8)]
        w0 = sb("w0", [P, KC, D])
        w1 = sb("w1", [P, KC, D])
        kvb = w1[:, :, :].rearrange("p (s a m) n -> p s a m n", s=2, a=2)
        lng = sb("lng", [P, D])
        lnb = sb("lnb", [P, D])
        xrow = sb("xrow", [P, 2, D])
        r = sb("r", [P, 2, D])
        xo = sb("xo", [P, 2, D])
        kT = sb("kT", [P, KC, MEM])
        vm = sb("vm", [P, 2, D])
        pr = sb("pr", [P, CAH, MEM])
        prT = sb("prT", [P, 2, CAH, P])
        oTt = sb("oTt", [P, KC, P])
        qs = sb("qs", [P, KC, NS + 32])
        wr = sb("wr", [P, KC, EG + E])
        stats = sb("stats", [P, 2, 6])
        mv = sb("mv", [P, 2])
        rs = sb("rs", [P, 2])
        mx = sb("mx", [P, 2, CAH])
        sm = sb("sm", [P, 2, CAH])
        qT = M.mT

        wo_in = [sem(f"wo_in{i}") for i in range(2)]
        w0_in, w1_in, ln_in, km_in, wr_in = sem("w0_in"), sem("w1_in"), sem("ln_in"), sem("km_in"), sem("wr_in")
        xr_in = [sem(f"xr_in{i}") for i in range(2)]
        kv_in = [sem(f"kv_in{i}") for i in range(2)]
        x_out = [sem(f"x_out{i}") for i in range(2)]
        pe_s, dv_s, ac_s, pl_s = sem("c_pe"), sem("c_dve"), sem("c_act"), sem("c_pool")
        link_s, alink_s, plink_s = sem("c_link"), sem("c_alink"), sem("c_plink")
        st = [Steps(x) for x in steps_c()]
        PE, DV, AC, PL = ((lambda name, s=s: s(0, name)) for s in st)

        def rows(ap, t):
            return ap[t * P:t * P + rows_of(t), :]

        def src(t):
            return A["x_prompt"][0, t * P:(t + 1) * P, :] if t < NT - 1 else A["x_sample"].rearrange("b l d -> (b l) d")

        def load_kv(sp, b):
            for i, name in enumerate(("cache_mem_k", "cache_mem_v")):
                sp.dma_start(kvb[:, b % 2, i, :, :], A[name][0, b].rearrange("(m p) h d -> p m (h d)", p=P)
                             ).then_inc(kv_in[b % 2], 16)

        block = ctx.enter_context(nc.Block())

        @block.sync
        def _(sp):
            for half in range(2):
                sp.dma_start(w0[:, :, half * 512:(half + 1) * 512], A["w_out"][0].rearrange("(c p) n -> p c n", p=P)
                             [:, :, half * 512:(half + 1) * 512]).then_inc(wo_in[half], 16)
            sp.dma_start(lng[:, :], A["ln1_g"].to_broadcast((P, D))).then_inc(ln_in, 16)
            sp.dma_start(lnb[:, :], A["ln1_b"].to_broadcast((P, D))).then_inc(ln_in, 16)
            for t in range(NT):
                if t >= 2:
                    sp.wait_ge(dv_s, DV(f"r{t - 2}"))
                sp.dma_start(xrow[0:rows_of(t), t % 2, :], src(t)).then_inc(xr_in[t % 2], 16)
                if t == 0:
                    sp.dma_start(w1[:, :, :], A["w_cq"][0].rearrange("(c p) n -> p c n", p=P)).then_inc(w1_in, 16)
                    sp.dma_start(vm[:, :, :], O["mem_v"][0, 0].rearrange("(m p) h d -> p m (h d)", p=P)).then_inc(km_in, 16)
                    sp.dma_start(oTt[:, :, :].rearrange("p (m a) n -> p m (a n)", m=2),
                                 O["mem_k"][0, 0, :, 0:2].rearrange("(m p) h d -> p m (h d)", p=P)).then_inc(km_in, 16)
                    sp.dma_start(prT[:, :, :, :].rearrange("p m h n -> p m (h n)"),
                                 O["mem_k"][0, 0, :, 2:4].rearrange("(m p) h d -> p m (h d)", p=P)).then_inc(km_in, 16)
                    sp.dma_start(wr[:, :, 0:EG], A["w_router_group"][0].rearrange("(c p) n -> p c n", p=P)).then_inc(wr_in, 16)
                    sp.dma_start(wr[:, :, EG:], A["w_router_expert"][0].rearrange("(c p) n -> p c n", p=P)).then_inc(wr_in, 16)
                if t >= 1:
                    sp.wait_ge(pl_s, PL(f"x{t - 1}"))
                    sp.dma_start(rows(M.x1d, t - 1), xo[0:rows_of(t - 1), (t - 1) % 2, :]).then_inc(x_out[(t - 1) % 2], 16)
            t = NT - 1
            sp.wait_ge(pl_s, PL(f"x{t}"))
            sp.dma_start(rows(M.x1d, t), xo[0:rows_of(t), t % 2, :]).then_inc(x_out[t % 2], 16)
            sp.dma_start(lng[:, :], A["ln2_g"].to_broadcast((P, D))).then_inc(ln_in, 16)
            sp.dma_start(lnb[:, :], A["ln2_b"].to_broadcast((P, D))).then_inc(ln_in, 16)
            sp.wait_ge(pe_s, PE(f"y{t}"))
            sp.dma_start(w0[:, :, :], A["w_co"][0].rearrange("(c p) n -> p c n", p=P)).then_inc(w0_in, 16)
            sp.wait_ge(x_out[0], 16 * 5)
            sp.wait_ge(x_out[1], 16 * 4)
            for t in range(NT):
                i = NT + t
                sp.wait_ge(dv_s, DV(f"r{NT - 2 + t}") if t < 2 else DV(f"R{t - 2}"))
                sp.dma_start(xrow[0:rows_of(t), i % 2, :], rows(M.x1d, t)).then_inc(xr_in[i % 2], 16)
                if t == 1:
                    sp.wait_ge(pe_s, PE(f"q{KC * len(SEGS) - 1}"))
                    for b in range(2):
                        load_kv(sp, b)
                if t >= 1:
                    sp.wait_ge(pl_s, PL(f"X{t - 1}"))
                    sp.dma_start(rows(M.x2d, t - 1), xo[0:rows_of(t - 1), (i - 1) % 2, :]).then_inc(x_out[(i - 1) % 2], 16)
            for b in range(2, NB):
                sp.wait_ge(pe_s, PE(f"o{b - 2}"))
                load_kv(sp, b)
            t = NT - 1
            sp.wait_ge(pl_s, PL(f"X{t}"))
            sp.dma_start(rows(M.x2d, t), xo[0:rows_of(t), (NT + t) % 2, :]).then_inc(x_out[(NT + t) % 2], 16)
            sp.wait_ge(x_out[0], 16 * 9)
            sp.wait_ge(x_out[1], 16 * 9)

        @block.tensor
        def _(pe):
            mm, tr = nc.tensor.matmul, nc.tensor.transpose

            def wide(t, lhs, i, w, w_in=None):
                n = rows_of(t)
                for half in range(2):
                    if w_in:
                        pe.wait_ge(w_in[half], 16)
                    for k in range(KC):
                        m = mm(bank[2 * (i % 2) + half][0:n, :], lhs(k), w[:, k, half * 512:(half + 1) * 512],
                               start=(k == 0), stop=(k == KC - 1))
                m.then_inc(pe_s, 1)

            def rows_T(t, i):
                n = rows_of(t)
                for k in range(KC):
                    m = tr(bank[4 + k // 4][:, (k % 4) * P:(k % 4) * P + n], xo[0:n, i % 2, k * P:(k + 1) * P], M.ident[0:n, 0:n])
                m.then_inc(pe_s, 1)

            def x1_T(t):
                pe.wait_ge(pl_s, PL(f"x{t}"))
                if t:
                    pe.wait_ge(ac_s, AC(f"t{t - 1}"))
                rows_T(t, t)

            for t in range(NT):
                if t >= 2:
                    pe.wait_ge(dv_s, DV(f"r{t - 2}"))
                n = rows_of(t)
                wide(t, lambda k: M.mT[:, k, t * P:t * P + n], t, w0, wo_in)
                if t:
                    x1_T(t - 1)
            x1_T(NT - 1)
            pe.wait_ge(km_in, 48)
            pe.wait_ge(ac_s, AC(f"t{NT - 1}"))
            kr = (oTt[:, :, :].rearrange("p (m a) n -> p m (a n)", m=2), prT[:, :, :, :].rearrange("p m h n -> p m (h n)"))
            for m_ in range(2):
                for k in range(KC):
                    m = tr(bank[4 + k // 2][:, (k % 2) * MEM + m_ * P:(k % 2) * MEM + (m_ + 1) * P],
                           kr[k // 4][:, m_, (k % 4) * P:(k % 4 + 1) * P], M.ident)
            m.then_inc(pe_s, 1)
            pe.wait_ge(w1_in, 16)
            for c in range(KC):
                for s, (at, n) in enumerate(SEGS):
                    u = 3 * c + s
                    if u < 2:
                        pe.wait_ge(ac_s, AC("kt"))
                    else:
                        pe.wait_ge(ac_s, AC(f"q{u - 2}"))
                    for k in range(KC):
                        m = mm(bank[6 + u % 2][:, 0:n], w1[:, k, c * P:(c + 1) * P], M.xT[:, k, at:at + n],
                               start=(k == 0), stop=(k == KC - 1))
                    m.then_inc(pe_s, 1)
            pe.wait_ge(ac_s, AC(f"q{KC * len(SEGS) - 1}"))
            pe.wait_ge(w0_in, 16)

            def out(t):
                if t < 2:
                    pe.wait_ge(dv_s, DV(f"r{NT - 2 + t}"))
                else:
                    pe.wait_ge(dv_s, DV(f"R{t - 2}"))
                pe.wait_ge(ac_s, AC(f"O{t}") if t < NT - 1 else AC(f"o{NB - 1}"))
                wide(t, lambda k: oTt[:, k, 0:rows_of(t)], NT + t, w0)

            def route(t, last):
                pe.wait_ge(pl_s, PL(f"X{t}"))
                pe.wait_ge(ac_s, last)
                rows_T(t, NT + t)
                pe.wait_ge(ac_s, AC(f"T{t}"))
                if t == 0:
                    pe.wait_ge(wr_in, 32)
                n = rows_of(t)
                for k in range(KC):
                    m = mm(bank[6][0:n, 0:EG + E], M.xT[:, k, t * P:t * P + n], wr[:, k, :], start=(k == 0), stop=(k == KC - 1))
                m.then_inc(pe_s, 1)

            for t in range(NT - 1):
                if t:
                    pe.wait_ge(ac_s, AC(f"O{t - 1}"))
                for h in range(CAH):
                    for k in range(2):
                        m = mm(bank[6 + h // 2][:, (h % 2) * MEM:(h % 2 + 1) * MEM], qT[:, 2 * h + k, t * P:(t + 1) * P],
                               kT[:, 2 * h + k, :], start=(k == 0), stop=(k == 1))
                m.then_inc(pe_s, 1)
                if t:
                    out(t - 1)
                pe.wait_ge(ac_s, AC(f"e{t}"))
                if t > 1:
                    route(t - 2, AC(f"P{t - 1}"))
                pe.wait_ge(dv_s, DV(f"p{t}"))
                if t > 1:
                    pe.wait_ge(ac_s, AC(f"G{t - 2}"))
                elif t:
                    pe.wait_ge(ac_s, AC(f"P{t - 1}"))
                for h in range(CAH):
                    for k in range(2):
                        m = tr(bank[4 + k][:, h * P:(h + 1) * P], pr[:, h, k * P:(k + 1) * P], M.ident)
                m.then_inc(pe_s, 1)
                pe.wait_ge(ac_s, AC(f"P{t}"))
                for c in range(KC):
                    for k in range(2):
                        m = mm(bank[6 + c // 4][:, (c % 4) * P:(c % 4 + 1) * P], vm[:, k, c * P:(c + 1) * P],
                               prT[:, k, c // 2, :], start=(k == 0), stop=(k == 1))
                m.then_inc(pe_s, 1)
            out(NT - 2)

            def k_T(b):
                pe.wait_ge(kv_in[b % 2], 32 * (b // 2 + 1))
                for k in range(KC):
                    for m_ in range(2):
                        m = tr(bank[4 + k // 2][:, (k % 2) * MEM + m_ * P:(k % 2) * MEM + (m_ + 1) * P],
                               kvb[:, b % 2, 0, m_, k * P:(k + 1) * P], M.ident)
                m.then_inc(pe_s, 1)

            pe.wait_ge(ac_s, AC(f"O{NT - 2}"))
            k_T(0)
            pe.wait_ge(pl_s, PL("qpad"))
            pe.wait_ge(dv_s, DV(f"R{NT - 3}"))
            for b in range(NB):
                pe.wait_ge(ac_s, AC(f"K{b}"))
                for h in range(CAH):
                    for k in range(2):
                        m = mm(bank[2][32 * h:32 * h + 32, 0:MEM], qs[:, 2 * h + k, b * DS:b * DS + 32], kT[:, 2 * h + k, :],
                               start=(k == 0), stop=(k == 1))
                m.then_inc(pe_s, 1)
                if b + 1 < NB:
                    k_T(b + 1)
                pe.wait_ge(dv_s, DV(f"p_{b}"))
                if b:
                    pe.wait_ge(ac_s, AC(f"o{b - 1}"))
                for k in range(2):
                    m = tr(bank[3][:, k * P:(k + 1) * P], pr[:, 0, k * P:(k + 1) * P], M.ident)
                m.then_inc(pe_s, 1)
                pe.wait_ge(ac_s, AC(f"p{b}"))
                for c in range(KC):
                    for k in range(2):
                        m = mm(bank[3][:, 2 * P + c * DS:2 * P + (c + 1) * DS], kvb[:, b % 2, 1, k, c * P:(c + 1) * P],
                               prT[:, k, 0, 32 * (c // 2):32 * (c // 2) + DS], start=(k == 0), stop=(k == 1))
                m.then_inc(pe_s, 1)
            t = NT - 1
            route(t - 2, AC(f"o{NB - 1}"))
            pe.wait_ge(ac_s, AC(f"G{t - 2}"))
            route(t - 1, AC(f"G{t - 2}"))
            out(t)
            pe.wait_ge(ac_s, AC(f"G{t - 1}"))
            route(t, AC(f"G{t - 1}"))

        @block.scalar
        def _(act):
            a = nc.scalar
            n_link = [0]

            def link(ins):
                n_link[0] += 1
                ins.then_inc(alink_s, 1)
                act.wait_ge(alink_s, n_link[0])

            def rstd(t, name):
                n = rows_of(t)
                act.wait_ge(dv_s, DV(name))
                link(a.activation(rs[0:n, 0:1], mv[0:n, 1:2], ACT.Ln, bias=M.lneps[0:n]))
                a.activation(rs[0:n, 1:2], rs[0:n, 0:1], ACT.Exp, scale=-0.5).then_inc(ac_s, 1)

            def rows_T(t, name):
                n = rows_of(t)
                act.wait_ge(pe_s, PE(name))
                for half in range(2):
                    ins = a.copy(M.xT[:, 4 * half:4 * half + 4, t * P:t * P + n],
                                 bank[4 + half][:, :].rearrange("p (c n) -> p c n", n=P)[:, :, 0:n])
                ins.then_inc(ac_s, 1)

            for t in range(NT):
                rstd(t, f"v{t}")
                if t:
                    rows_T(t - 1, f"t{t - 1}")
            rows_T(NT - 1, f"t{NT - 1}")
            act.wait_ge(pe_s, PE("kt"))
            for i in range(4):
                ins = a.copy(kT[:, 2 * i:2 * i + 2, :], bank[4 + i][:, :].rearrange("p (c n) -> p c n", n=MEM))
            ins.then_inc(ac_s, 1)
            for c in range(KC):
                for s, (at, n) in enumerate(SEGS):
                    u = 3 * c + s
                    act.wait_ge(pe_s, PE(f"q{u}"))
                    dst = qT[:, c, at:at + n] if at < SEQ else qs[:, c, 0:n]
                    a.copy(dst, bank[6 + u % 2][:, 0:n]).then_inc(ac_s, 1)

            def route(t):
                rows_T(t, f"T{t}")
                n = rows_of(t)
                act.wait_ge(pe_s, PE(f"G{t}"))
                a.copy(M.logits[0:n, t, :], bank[6][0:n, 0:EG + E]).then_inc(ac_s, 1)

            scale = float(CAD) ** -0.5
            for t in range(NT - 1):
                act.wait_ge(dv_s, DV(f"m{t}"))
                for h in range(CAH):
                    ins = a.activation(pr[:, h, :], bank[6 + h // 2][:, (h % 2) * MEM:(h % 2 + 1) * MEM], ACT.Exp,
                                       bias=mx[:, 1, h:h + 1], scale=scale, accum_out=sm[:, 0, h:h + 1])
                ins.then_inc(ac_s, 1)
                if t > 1:
                    route(t - 2)
                if t:
                    rstd(t - 1, f"V{t - 1}")
                act.wait_ge(pe_s, PE(f"P{t}"))
                for k in range(2):
                    ins = a.copy(prT[:, k, :, :], bank[4 + k][:, :].rearrange("p (h n) -> p h n", n=P))
                ins.then_inc(ac_s, 1)
                act.wait_ge(pe_s, PE(f"O{t}"))
                for k in range(2):
                    ins = a.copy(oTt[:, 4 * k:4 * k + 4, :], bank[6 + k][:, :].rearrange("p (h n) -> p h n", n=P))
                ins.then_inc(ac_s, 1)
            rstd(NT - 2, f"V{NT - 2}")

            def k_out(b):
                act.wait_ge(pe_s, PE(f"K{b}"))
                for i in range(4):
                    ins = a.copy(kT[:, 2 * i:2 * i + 2, :], bank[4 + i][:, :].rearrange("p (c n) -> p c n", n=MEM))
                ins.then_inc(ac_s, 1)

            k_out(0)
            for b in range(NB):
                act.wait_ge(dv_s, DV(f"m_{b}"))
                a.activation(pr[:, 0, :], bank[2][:, 0:MEM], ACT.Exp, bias=mx[:, 1, 0:1], scale=scale,
                             accum_out=sm[:, 0, 0:1]).then_inc(ac_s, 1)
                act.wait_ge(pe_s, PE(f"p{b}"))
                a.copy(prT[:, :, 0, :], bank[3][:, 0:2 * P].rearrange("p (k n) -> p k n", n=P)).then_inc(ac_s, 1)
                if b + 1 < NB:
                    k_out(b + 1)
                act.wait_ge(pe_s, PE(f"o{b}"))
                a.copy(oTt[:, :, b * DS:(b + 1) * DS], bank[3][:, 2 * P:2 * P + KC * DS]
                       .rearrange("p (c l) -> p c l", l=DS)).then_inc(ac_s, 1)
            t = NT - 1
            route(t - 2)
            route(t - 1)
            rstd(t, f"V{t}")
            route(t)

        @block.gpsimd
        def _(pool):
            g_ = nc.gpsimd
            n_link = [0]

            def link(ins):
                n_link[0] += 1
                ins.then_inc(plink_s, 1)
                pool.wait_ge(plink_s, n_link[0])

            def affine(t, i, name, tname):
                n = rows_of(t)
                pool.wait_ge(dv_s, DV(name))
                if i >= 2:
                    pool.wait_ge(x_out[i % 2], 16 * (i // 2))
                if tname:
                    pool.wait_ge(pe_s, PE(tname))
                link(g_.tensor_tensor(xo[0:n, i % 2, :], r[0:n, i % 2, :], lng[0:n, :], ALU.mult))
                g_.tensor_tensor(xo[0:n, i % 2, :], xo[0:n, i % 2, :], lnb[0:n, :], ALU.add).then_inc(pl_s, 1)

            pool.wait_ge(ln_in, 32)
            for t in range(NT):
                affine(t, t, f"n{t}", f"t{t - 2}" if t >= 2 else None)
            g_.memset(qs[:, :, NS:], 0.0).then_inc(pl_s, 1)
            pool.wait_ge(ln_in, 64)
            for t in range(NT):
                affine(t, NT + t, f"N{t}", f"t{NT - 2 + t}" if t < 2 else f"T{t - 2}")

        @block.vector
        def _(dve):
            v = nc.vector
            n_link = [0]

            def link(ins):
                n_link[0] += 1
                ins.then_inc(link_s, 1)
                dve.wait_ge(link_s, n_link[0])

            def norm(t, i, y, s, freed):
                n = rows_of(t)
                dve.wait_ge(pe_s, PE(y))
                dve.wait_ge(xr_in[i % 2], 16 * (i // 2 + 1))
                if freed:
                    dve.wait_ge(pl_s, PL(freed))
                ri = r[0:n, i % 2, :]
                for half in range(2):
                    ins = v.scalar_tensor_tensor(ri[:, half * 512:half * 512 + 512], xrow[0:n, i % 2, half * 512:half * 512 + 512],
                                                 ALPHA, bank[2 * (i % 2) + half][0:n, :], ALU.mult, ALU.add)
                ins.then_inc(dv_s, 1)
                dve.wait_ge(dv_s, n_after[0] + 1)
                layer_norm_rows(v, link, ri, stats, mv, n).then_inc(dv_s, 1)
                dve.wait_ge(ac_s, AC(s))
                v.tensor_scalar(ri, ri, mv[0:n, 0:1], rs[0:n, 1:2], ALU.subtract, ALU.mult).then_inc(dv_s, 1)
                n_after[0] += 3

            n_after = [0]
            for t in range(NT):
                norm(t, t, f"y{t}", f"s{t}", f"x{t - 2}" if t >= 2 else None)

            def soft(banks, heads, e):
                for lo, b in banks:
                    ins = v.tensor_reduce(mx[:, 0, lo:lo + (2 if heads > 1 else 1)],
                                          b[:, 0:MEM * (2 if heads > 1 else 1)].rearrange("p (h n) -> p h n", n=MEM), AX_X, ALU.max)
                link(ins)
                v.tensor_scalar(mx[:, 1, 0:heads], mx[:, 0, 0:heads], -float(CAD) ** -0.5, None, ALU.mult).then_inc(dv_s, 1)
                dve.wait_ge(ac_s, AC(e))
                link(v.reciprocal(sm[:, 1, 0:heads], sm[:, 0, 0:heads]))
                v.tensor_tensor(pr[:, 0:heads, :], pr[:, 0:heads, :], sm[:, 1, 0:heads].unsqueeze(2).to_broadcast((P, heads, MEM)),
                                ALU.mult).then_inc(dv_s, 1)
                n_after[0] += 2

            for t in range(NT - 1):
                dve.wait_ge(pe_s, PE(f"S{t}"))
                soft(((0, bank[6]), (2, bank[7])), CAH, f"e{t}")
                if t:
                    norm(t - 1, NT + t - 1, f"Y{t - 1}", f"s_{t - 1}", f"x{NT - 3 + t}" if t < 3 else f"X{t - 3}")
            t = NT - 1
            norm(t - 1, NT + t - 1, f"Y{t - 1}", f"s_{t - 1}", f"X{t - 3}")
            for b in range(NB):
                dve.wait_ge(pe_s, PE(f"s{b}"))
                soft(((0, bank[2]),), 1, f"e_{b}")
            norm(t, NT + t, f"Y{t}", f"s_{t}", f"X{t - 2}")


def phase_r(nc, A, O, M):
    with ExitStack() as ctx:
        def sb(name, shape, dt=F32):
            return ctx.enter_context(nc.sbuf_tensor(name, shape, dt))

        def sem(name):
            return ctx.enter_context(nc.semaphore(name))

        bank = [ctx.enter_context(nc.psum_tensor(f"r_bank{i}", [P, 512], F32)) for i in range(4)]
        rc = sb("rc", [P, RC_ALL])
        strict = rc[:, RC_STRICT:RC_STRICT + P]
        iota8 = rc[:, RC_I8:RC_I8 + EG]
        iota64 = rc[:, RC_I64:RC_I64 + E]
        valid = rc[:, RC_VALID:RC_VALID + NT]
        starts = rc[:, RC_START:RC_START + NMAX]
        rounds = rc[:, RC_ROUND:RC_ROUND + NBLK // RND]
        part = rc[:, RC_PART:RC_PART + 1]
        tok = sb("tok", [P, NT], I32)
        g3 = [sb(f"g3_{i}", [P, NT, EG]) for i in range(2)]
        e3 = [sb(f"e3_{i}", [P, NT, E]) for i in range(2)]
        em = sb("em", [P, NT, E])
        oh = sb("oh", [P, 2, NT, E])
        before = sb("before", [P, NT, E])
        both = sb("both", [P, NT, E])
        s1 = [sb(f"s1_{i}", [P, NT]) for i in range(8)]
        cnt = sb("cnt", [P, E])
        big = sb("big", [P, E, NMAX])
        nb = sb("nb", [P, E])
        bend = sb("bend", [P, E])
        base = sb("base", [P, E])
        one = sb("one", [P, E])
        destf = sb("destf", [P, 2, NT])
        bexp = sb("bexp", [P, 1])
        bexpi = sb("bexpi", [P, 1], I32)
        npf = sb("npf", [P, NBLK // RND])
        npi = sb("npi", [P, 1], I32)
        zero = sb("zero", [BLK, LEAD + NBLK], I32)
        rowsf = sb("rowsf", [NBLK, BLK])
        rowsi = sb("rowsi", [NBLK, BLK], I32)

        rc_in, tok_in, zeroed = sem("rc_in"), sem("tok_in"), sem("r_zeroed")
        table_zero, scat, rows_in, tab_out = sem("table_zero"), sem("scattered"), sem("rows_in"), sem("tab_out")
        link_s = sem("r_link")
        to_act, from_act, to_pe, from_pe, dest_ready, tab_ready = (sem(n) for n in
            ("to_act", "from_act", "to_pe", "from_pe", "dest_ready", "tab_ready"))
        block = ctx.enter_context(nc.Block())

        @block.sync
        def _(sp):
            sp.dma_start(rc[:, :], A["rconst"]).then_inc(rc_in, 16)
            sp.dma_start(tok[:, :], A["tokens"]).then_inc(tok_in, 16)
            sp.wait_ge(zeroed, 1)
            sp.dma_start(M.row_tok.rearrange("(p n) o -> p (n o)", p=BLK), zero[:, :]).then_inc(table_zero, 16)
            sp.wait_ge(tab_ready, 1)
            sp.dma_start(M.blk_d[0:NBLK, :], bexpi[0:NBLK, :]).then_inc(tab_out, 16)
            sp.dma_start(M.blk_d[NBLK:NBLK + 1, :], npi[0:1, :]).then_inc(tab_out, 16)
            sp.wait_ge(scat, 16 * 2 * NT)
            sp.dma_start(rowsi[:, :], M.row_tok[LEAD * BLK:, :].rearrange("(b n) o -> b (n o)", n=BLK)).then_inc(rows_in, 16)
            sp.wait_ge(tab_out, 32)

        @block.gpsimd
        def _(pool):
            nc.gpsimd.memset(zero[:, :], 0).then_inc(zeroed, 1)
            pool.wait_ge(table_zero, 16)
            pool.wait_ge(tok_in, 16)
            pool.wait_ge(dest_ready, 1)
            for t in range(NT):
                for i in range(2):
                    n = rows_of(t)
                    nc.gpsimd.indirect_dma_start(
                        out=M.row_tok, out_offset=bass.IndirectOffsetOnAxis(ap=M.dest[0:n, i, t:t + 1], axis=0),
                        in_=tok[0:n, t:t + 1], in_offset=None).then_inc(scat, 16)

        @block.scalar
        def _(act):
            act.wait_ge(to_act, 1)
            nc.scalar.activation(g3[0][:, :, :], g3[0][:, :, :], ACT.Exp).then_inc(from_act, 1)
            act.wait_ge(to_act, 2)
            nc.scalar.activation(s1[4][:, :], s1[4][:, :], ACT.Exp).then_inc(from_act, 1)

        @block.tensor
        def _(pe):
            mm = nc.tensor.matmul
            pe.wait_ge(to_pe, 1)
            flat = both[:, :, :].rearrange("p t e -> p (t e)")
            bef = before[:, :, :].rearrange("p t e -> p (t e)")
            for b, (at, n) in enumerate(((0, 512), (512, E))):
                mm(bank[b][:, 0:n], strict, flat[:, at:at + n], start=True, stop=False)
                mm(bank[b][:, 0:n], M.ones, bef[:, at:at + n], start=False, stop=True)
            mm(bank[2][:, 0:E], M.ones, before[:, NT - 1, :], start=True, stop=False)
            mm(bank[2][:, 0:E], M.ones, both[:, NT - 1, :], start=False, stop=True).then_inc(from_pe, 1)
            pe.wait_ge(to_pe, 2)
            nc.tensor.transpose(bank[3][0:BLK, 0:NBLK], rowsf[:, :], M.ident[0:NBLK, 0:NBLK]).then_inc(from_pe, 1)

        @block.vector
        def _(dve):
            v = nc.vector
            n_link = [0]

            def link(ins):
                n_link[0] += 1
                ins.then_inc(link_s, 1)
                dve.wait_ge(link_s, n_link[0])

            def wide(a, m):
                return a.unsqueeze(2).to_broadcast((P, NT, m))

            def first_hot(out, x, best, iota, m, scratch, idx):
                over = iota.unsqueeze(1).to_broadcast((P, NT, m))
                link(v.tensor_tensor(scratch, x, wide(best, m), ALU.is_equal))
                link(v.scalar_tensor_tensor(scratch, scratch, -float(m), over, ALU.mult, ALU.add))
                link(v.tensor_reduce(idx, scratch, AX_X, ALU.min))
                link(v.tensor_scalar(idx, idx, float(m), None, ALU.add))
                link(v.tensor_tensor(out, over, wide(idx, m), ALU.is_equal))

            v.memset(M.logits[NS:P, NT - 1, :], 0.0).then_inc(link_s, 1)
            n_link[0] += 1
            dve.wait_ge(link_s, 1)
            dve.wait_ge(rc_in, 16)
            gl, el = M.logits[:, :, 0:EG], M.logits[:, :, EG:]
            link(v.memset(one[:, :], 1.0))
            link(v.tensor_reduce(s1[0][:, :], gl, AX_X, ALU.max))
            v.tensor_tensor(g3[0][:, :, :], gl, wide(s1[0][:, :], EG), ALU.subtract).then_inc(to_act, 1)
            first_hot(g3[1][:, :, :], gl, s1[0][:, :], iota8, EG, e3[0][:, :, 0:EG], s1[1][:, :])
            link(v.tensor_scalar(g3[1][:, :, :], g3[1][:, :, :], -1.0, FAR, ALU.add, ALU.mult))
            link(v.tensor_copy(e3[0][:, :, :].rearrange("p t (g e) -> p t g e", g=EG),
                               g3[1][:, :, :].unsqueeze(3).to_broadcast((P, NT, EG, EPG))))
            link(v.tensor_tensor(em[:, :, :], el, e3[0][:, :, :], ALU.add))
            link(v.tensor_reduce(s1[2][:, :], em[:, :, :], AX_X, ALU.max))
            first_hot(oh[:, 0], em[:, :, :], s1[2][:, :], iota64, E, e3[1][:, :, :], s1[1][:, :])
            link(v.scalar_tensor_tensor(em[:, :, :], oh[:, 0], -2.0 * FAR, em[:, :, :], ALU.mult, ALU.add))
            link(v.tensor_reduce(s1[3][:, :], em[:, :, :], AX_X, ALU.max))
            first_hot(oh[:, 1], em[:, :, :], s1[3][:, :], iota64, E, e3[1][:, :, :], s1[1][:, :])
            v.tensor_tensor(s1[4][:, :], s1[3][:, :], s1[2][:, :], ALU.subtract).then_inc(to_act, 1)
            link(v.tensor_tensor(both[:, :, :], oh[:, 0], oh[:, 1], ALU.add))
            link(v.tensor_tensor(both[:, :, :], both[:, :, :], wide(valid, E), ALU.mult))
            link(v.memset(before[:, 0, :], 0.0))
            for t in range(1, NT):
                link(v.tensor_tensor(before[:, t, :], before[:, t - 1, :], both[:, t - 1, :], ALU.add))
            v.tensor_copy(s1[7][:, 0:1], part).then_inc(to_pe, 1)
            dve.wait_ge(from_act, 1)
            link(v.tensor_reduce(s1[5][:, :], g3[0][:, :, :], AX_X, ALU.add))
            dve.wait_ge(from_act, 2)
            link(v.scalar_tensor_tensor(s1[6][:, :], s1[4][:, :], 1.0, s1[5][:, :], ALU.add, ALU.mult))
            link(v.reciprocal(M.w12[:, 0, :], s1[6][:, :]))
            link(v.tensor_tensor(M.w12[:, 1, :], s1[4][:, :], M.w12[:, 0, :], ALU.mult))
            dve.wait_ge(from_pe, 1)
            link(v.tensor_copy(cnt[:, :], bank[2][:, 0:E]))
            link(v.tensor_tensor(big[:, :, :], cnt[:, :].unsqueeze(2).to_broadcast((P, E, NMAX)),
                                 starts.unsqueeze(1).to_broadcast((P, E, NMAX)), ALU.is_gt))
            link(v.tensor_reduce(nb[:, :], big[:, :, :], AX_X, ALU.add))
            link(v.tensor_tensor_scan(bend[:, :], one[:, :], nb[:, :], 0.0, ALU.mult, ALU.add))
            link(v.tensor_tensor(base[:, :], bend[:, :], nb[:, :], ALU.subtract))
            link(v.tensor_scalar(base[:, :], base[:, :], float(BLK), float(LEAD * BLK), ALU.mult, ALU.add))
            v.tensor_tensor(em[:, 0:8, :], bank[0][:, :].rearrange("p (t e) -> p t e", e=E),
                            base[:, :].unsqueeze(1).to_broadcast((P, 8, E)), ALU.add)
            link(v.tensor_tensor(em[:, 8, :], bank[1][:, 0:E], base[:, :], ALU.add))
            for i in range(2):
                link(v.tensor_tensor(e3[i][:, :, :], em[:, :, :], oh[:, i], ALU.mult))
                link(v.tensor_reduce(destf[:, i, :], e3[i][:, :, :], AX_X, ALU.add))
            v.tensor_copy(M.dest[:, :, :], destf[:, :, :]).then_inc(dest_ready, 1)
            link(v.tensor_scalar(e3[0][:, 0, :], bend[:, :], part, None, ALU.is_le))
            link(v.tensor_reduce(bexp[:, :], e3[0][:, 0, :], AX_X, ALU.add))
            link(v.tensor_scalar(bexp[:, :], bexp[:, :], float(E - 1), None, ALU.min))
            link(v.tensor_copy(bexpi[:, :], bexp[:, :]))
            link(v.tensor_scalar(npf[:, :], rounds, bend[:, E - 1:E], None, ALU.is_lt))
            link(v.tensor_reduce(bexp[:, :], npf[:, :], AX_X, ALU.add))
            v.tensor_copy(npi[:, :], bexp[:, :]).then_inc(tab_ready, 1)
            dve.wait_ge(rows_in, 16)
            v.tensor_copy(rowsf[:, :], rowsi[:, :]).then_inc(to_pe, 1)
            dve.wait_ge(from_pe, 2)
            link(v.tensor_copy(M.idx_all[:, :], bank[3][0:BLK, 0:NBLK]))


def due(j):
    return (j + 1) % RND


def steps_d():
    pe, dv, ac = [], [], []
    for j in range(RND):
        pe += [f"T{j}", f"D{due(j)}", f"H{j}"]
        ac += [f"x{j}", f"y{due(j)}", f"t{j}"]
        dv += [f"z{due(j)}", f"h{j}"]
    return pe, dv, ac


def phase_d(nc, A, O, M):
    with ExitStack() as ctx:
        def sb(name, shape, dt=F32):
            return ctx.enter_context(nc.sbuf_tensor(name, shape, dt))

        def sem(name):
            return ctx.enter_context(nc.semaphore(name))

        bT = ctx.enter_context(nc.psum_tensor("d_t", [P, 512], F32))
        bH = ctx.enter_context(nc.psum_tensor("d_h", [P, 512], F32))
        bY = [ctx.enter_context(nc.psum_tensor(f"d_y{i}", [P, 2, 512], F32)) for i in range(RND)]
        wg = sb("wg_e", [P, RND, KC, FF])
        wu = sb("wu_e", [P, RND, KC, FF])
        wd = sb("wd_e", [P, RND, 2, D])
        idx = sb("idx", [BLK, RND], I32)
        xg = sb("xg", [BLK, RND, D])
        xT = sb("xT_e", [P, RND, KC, BLK])
        th = sb("th", [P, RND, 2, BLK])
        hh = sb("hh", [P, RND, 2, BLK])
        yb = sb("yb", [BLK, RND, D])
        wg_in, wu_in, wd_in, xg_in, idx_set, y_out = ([sem(f"{n}{j}") for j in range(RND)] for n in
                                                      ("wg_in", "wu_in", "wd_in", "xg_in", "idx_set", "y_out"))
        pe_s, dv_s, ac_s = sem("d_pe"), sem("d_dve"), sem("d_act")
        link_s = sem("d_link")
        cleared, pe_tail, act_tail, dve_tail = (sem("d_" + n) for n in ("cleared", "pe_tail", "act_tail", "dve_tail"))
        PE, DV, AC = (Steps(x, len(x)) for x in steps_d())
        most = NBLK // RND

        def rounds(eng):
            return eng.value_load(M.blk_d[NBLK:NBLK + 1, 0:1], min_val=1, max_val=most)

        def chunks(b, n):
            return b.rearrange("p (c n) -> p c n", n=n)

        block = ctx.enter_context(nc.Block())

        @block.sync
        def _(sp):
            with sp.Fori(0, rounds(sp)) as i:
                es = [sp.value_load(M.blk_d[bass.ds(RND * i + j, 1), 0:1], min_val=0, max_val=E - 1) for j in range(RND)]
                for j in range(RND):
                    e = es[j]
                    sp.wait_ge(pe_s, PE.last(i, f"H{j}"))
                    sp.dma_start(wg[:, j], A["w_gate"][0, bass.ds(e, 1)].rearrange("e (p k) f -> p (e k) f", p=P)).then_inc(wg_in[j], 16)
                    sp.dma_start(wu[:, j], A["w_up"][0, bass.ds(e, 1)].rearrange("e (p k) f -> p (e k) f", p=P)).then_inc(wu_in[j], 16)
                    sp.wait_ge(pe_s, PE(i, f"D{j}") if j else PE.last(i, f"D{j}"))
                    sp.dma_start(wd[:, j], A["w_down"][0, bass.ds(e, 1)].rearrange("e (p c) d -> p (e c) d", p=P)).then_inc(wd_in[j], 16)

        @block.gpsimd
        def _(pool):
            with pool.Fori(0, rounds(pool)) as i:
                for j in range(RND):
                    pool.sem_clear(idx_set[j])
                    pool.wait_ge(pe_s, PE.last(i, f"T{j}"))
                    nc.gpsimd.tensor_copy(idx[:, j:j + 1], M.idx_all[:, bass.ds(RND * i + j, 1)]).then_inc(idx_set[j], 1)
                    pool.wait_ge(idx_set[j], 1)
                    nc.gpsimd.indirect_dma_start(out=xg[:, j, :], out_offset=None, in_=M.x2d,
                                                 in_offset=bass.IndirectOffsetOnAxis(ap=idx[:, j:j + 1], axis=0)
                                                 ).then_inc(xg_in[j], 16)

        @block.tensor
        def _(pe):
            mm, tr = nc.tensor.matmul, nc.tensor.transpose
            pe.sem_inc(pe_s, PE.start)

            def turn(i, j):
                pe.wait_ge(ac_s, AC(i, f"x{j - 1}") if j else AC.last(i, f"x{RND - 1}"))
                pe.wait_ge(xg_in[j], (i + 1) * 16)
                rows = xg[:, j, :].rearrange("n (p k) -> n k p", k=KC)
                mm(bT[:, 0:BLK], rows[:, 0, :], M.ident[0:BLK, 0:BLK], start=True, stop=True)
                for k in range(1, KC):
                    m = tr(bT[:, k * BLK:(k + 1) * BLK], rows[:, k, :], M.ident[0:BLK, 0:BLK])
                m.then_inc(pe_s, 1)

            def hidden(i, j):
                pe.wait_ge(ac_s, AC(i, f"x{j}"))
                pe.wait_ge(dv_s, DV(i, f"h{j - 1}") if j else DV.last(i, f"h{RND - 1}"))
                for a, (w, w_in) in enumerate(((wg, wg_in), (wu, wu_in))):
                    pe.wait_ge(w_in[j], (i + 1) * 16)
                    wv = w[:, j].rearrange("p k (f c) -> p k c f", c=2)
                    for c in range(2):
                        for k in range(KC):
                            m = mm(bH[:, (2 * a + c) * BLK:(2 * a + c + 1) * BLK], wv[:, k, c, :], xT[:, j, k, :],
                                   start=(k == 0), stop=(k == KC - 1))
                m.then_inc(pe_s, 1)

            def down(i, s, done):
                pe.wait_ge(wd_in[s], (i + 1) * 16)
                pe.wait_ge(dv_s, DV.last(i, f"h{s}") if s else DV(i, f"h{s}"))
                pe.wait_ge(ac_s, AC.last(i, f"y{s}"))
                pe.wait_ge(dv_s, DV.last(i, f"z{s}"))
                for half in range(2):
                    for c in range(2):
                        m = mm(bY[s][0:BLK, half, :], hh[:, s, c, :], wd[:, s, c, half * 512:(half + 1) * 512],
                               start=(c == 0), stop=(c == 1))
                m.then_inc(done, 1)

            for s in range(1, RND):
                pe.sem_inc(wd_in[s], 16)
            pe.wait_ge(cleared, 2)
            n = rounds(pe)
            with pe.Fori(0, n) as i:
                for j in range(RND):
                    turn(i, j)
                    down(i, due(j), pe_s)
                    hidden(i, j)
            for s in range(1, RND):
                down(n, s, pe_tail)

        @block.scalar
        def _(act):
            a = nc.scalar
            act.sem_inc(ac_s, AC.start)
            for j in range(RND):
                act.sem_inc(y_out[j], 16)

            def x(i, j):
                act.wait_ge(pe_s, PE(i, f"T{j}"))
                a.copy(xT[:, j], chunks(bT[:, :], BLK)).then_inc(ac_s, 1)

            def t(i, j):
                act.wait_ge(pe_s, PE(i, f"H{j}"))
                a.activation(th[:, j], chunks(bH[:, 0:2 * BLK], BLK), ACT.Tanh, scale=0.5).then_inc(ac_s, 1)

            def y(i, s, ready, level, done, other):
                act.wait_ge(ready, level)
                act.wait_ge(y_out[s], (i + 1) * 16)
                a.copy(yb[:, s, 0:512], bY[s][0:BLK, 0, :]).then_inc(*done)
                for sem_, at in other:
                    act.wait_ge(sem_, at)
                at = RND * i + (s - 1) if s else RND * i + LEAD
                act.dma_start(M.y_rows[bass.ds(at * BLK, BLK), :], yb[:, s, :]).then_inc(y_out[s], 16)

            n = rounds(act)
            with act.Fori(0, n) as i:
                for j in range(RND):
                    s = due(j)
                    x(i, j)
                    y(i, s, pe_s, PE(i, f"D{s}"), (ac_s, 1), ((ac_s, AC(i, f"y{s}")), (dv_s, DV(i, f"z{s}"))))
                    t(i, j)
            for s in range(1, RND):
                y(n, s, pe_tail, s, (act_tail, 1), ((act_tail, s), (dve_tail, s)))
            for j in range(RND):
                act.wait_ge(y_out[j], n * 16 + (32 if j else 16))
                a.copy(th[0:1, j, 0, 0:1], th[0:1, j, 0, 1:2])

        @block.vector
        def _(dve):
            v = nc.vector
            dve.sem_inc(dv_s, DV.start)
            v.memset(hh[:, 1:, :, :], 0.0).then_inc(cleared, 1)
            v.memset(wd[:, 1:, :, :], 0.0).then_inc(cleared, 1)

            def z(i, s):
                dve.wait_ge(y_out[s], (i + 1) * 16)
                return v.tensor_copy(yb[:, s, 512:], bY[s][0:BLK, 1, :])

            n = rounds(dve)
            with dve.Fori(0, n) as i:
                dve.sem_clear(link_s)
                for j in range(RND):
                    dve.wait_ge(pe_s, PE(i, f"D{due(j)}"))
                    z(i, due(j)).then_inc(dv_s, 1)
                    dve.wait_ge(ac_s, AC(i, f"t{j}"))
                    v.scalar_tensor_tensor(th[:, j], th[:, j], 1.0, chunks(bH[:, 0:2 * BLK], BLK),
                                           ALU.add, ALU.mult).then_inc(link_s, 1)
                    dve.wait_ge(link_s, j + 1)
                    v.scalar_tensor_tensor(hh[:, j], th[:, j], 0.5, chunks(bH[:, 2 * BLK:4 * BLK], BLK),
                                           ALU.mult, ALU.mult).then_inc(dv_s, 1)
            for s in range(1, RND):
                dve.wait_ge(pe_tail, s)
                z(n, s).then_inc(dve_tail, 1)


def phase_e(nc, A, O, M):
    with ExitStack() as ctx:
        def sb(name, shape, dt=F32):
            return ctx.enter_context(nc.sbuf_tensor(name, shape, dt))

        def sem(name):
            return ctx.enter_context(nc.semaphore(name))

        lng, lnb = sb("lng_e", [P, D]), sb("lnb_e", [P, D])
        x2 = sb("x2", [P, NT, D])
        ys = sb("ys", [P, NT, 2, D])
        stats = sb("stats_e", [P, 2, 6])
        mv = sb("mv_e", [P, NT, 2])
        rs = sb("rs_e", [P, NT, 4])
        ln_in = sem("e_ln_in")
        x2_in = [sem(f"e_x2_in{i}") for i in range(NT)]
        ys_in = [sem(f"e_ys_in{i}") for i in range(NT)]
        out = sem("e_out")
        scaled, summed, counted, normed, gained, shifted = (sem("e_" + n) for n in
            ("scaled", "summed", "counted", "normed", "gained", "shifted"))
        link_s, alink_s = sem("e_link"), sem("e_alink")

        def dst(t):
            return O["y_prompt"][0, t * P:(t + 1) * P, :] if t < NT - 1 else O["y_sample"].rearrange("b l d -> (b l) d")

        block = ctx.enter_context(nc.Block())

        @block.sync
        def _(sp):
            for t in range(NT):
                sp.dma_start(x2[0:rows_of(t), t, :], M.x2d[t * P:t * P + rows_of(t), :]).then_inc(x2_in[t], 16)
                if t == 0:
                    sp.dma_start(lng[:, :], A["ln3_g"].to_broadcast((P, D))).then_inc(ln_in, 16)
                    sp.dma_start(lnb[:, :], A["ln3_b"].to_broadcast((P, D))).then_inc(ln_in, 16)
            for t in range(NT):
                sp.wait_ge(shifted, t + 1)
                sp.dma_start(dst(t), x2[0:rows_of(t), t, :]).then_inc(out, 16)
            sp.wait_ge(out, 16 * NT)

        @block.gpsimd
        def _(pool):
            for t in range(NT):
                n = rows_of(t)
                for i in range(2):
                    nc.gpsimd.indirect_dma_start(out=ys[0:n, t, i, :], out_offset=None, in_=M.y_rows,
                                                 in_offset=bass.IndirectOffsetOnAxis(ap=M.dest[0:n, i, t:t + 1], axis=0)
                                                 ).then_inc(ys_in[t], 16)
            pool.wait_ge(ln_in, 32)
            for t in range(NT):
                n = rows_of(t)
                pool.wait_ge(gained, t + 1)
                nc.gpsimd.tensor_tensor(x2[0:n, t, :], x2[0:n, t, :], lnb[0:n, :], ALU.add).then_inc(shifted, 1)

        @block.scalar
        def _(act):
            a = nc.scalar
            n_link = [0]

            def link(ins):
                n_link[0] += 1
                ins.then_inc(alink_s, 1)
                act.wait_ge(alink_s, n_link[0])

            def scale(t):
                n = rows_of(t)
                act.wait_ge(x2_in[t], 16)
                a.mul(x2[0:n, t, :], x2[0:n, t, :], ALPHA).then_inc(scaled, 1)

            scale(0)
            scale(1)
            scale(2)
            for t in range(NT):
                n, i = rows_of(t), t
                act.wait_ge(counted, t + 1)
                link(a.activation(rs[0:n, i, 0:1], mv[0:n, i, 1:2], ACT.Ln, bias=M.lneps[0:n]))
                link(a.activation(rs[0:n, i, 1:2], rs[0:n, i, 0:1], ACT.Exp, scale=-0.5))
                a.activation(rs[0:n, i, 2:3], mv[0:n, i, 0:1], ACT.Copy, scale=-1.0).then_inc(alink_s, 1)
                n_link[0] += 1
                act.wait_ge(alink_s, n_link[0])
                link(a.activation(rs[0:n, i, 3:4], rs[0:n, i, 2:3], ACT.Copy, scale=rs[0:n, i, 1:2]))
                a.activation(x2[0:n, i, :], x2[0:n, i, :], ACT.Identity, scale=rs[0:n, i, 1:2],
                             bias=rs[0:n, i, 3:4]).then_inc(normed, 1)
                if t + 3 < NT:
                    scale(t + 3)

        @block.vector
        def _(dve):
            v = nc.vector
            n_link = [0]

            def link(ins):
                n_link[0] += 1
                ins.then_inc(link_s, 1)
                dve.wait_ge(link_s, n_link[0])

            def gain(t):
                n, i = rows_of(t), t
                dve.wait_ge(normed, t + 1)
                v.tensor_tensor(x2[0:n, i, :], x2[0:n, i, :], lng[0:n, :], ALU.mult).then_inc(gained, 1)

            for t in range(NT):
                n, i = rows_of(t), t
                dve.wait_ge(scaled, t + 1)
                dve.wait_ge(ys_in[i], 32)
                x = x2[0:n, i, :]
                link(v.scalar_tensor_tensor(x, ys[0:n, i, 0, :], M.w12[0:n, 0, t:t + 1], x, ALU.mult, ALU.add))
                v.scalar_tensor_tensor(x, ys[0:n, i, 1, :], M.w12[0:n, 1, t:t + 1], x, ALU.mult, ALU.add).then_inc(summed, 1)
                dve.wait_ge(summed, t + 1)
                layer_norm_rows(v, link, x, stats, mv[:, i], n).then_inc(counted, 1)
                if t == 1:
                    dve.wait_ge(ln_in, 32)
                if t:
                    gain(t - 1)
            gain(NT - 1)


def build(nc, A, O):
    with ExitStack() as ctx:
        def sb(name, shape, dt=F32):
            return ctx.enter_context(nc.sbuf_tensor(name, shape, dt))

        M = Persistent()
        M.const = sb("const", [P, C_ALL])
        M.eps, M.epshd, M.lneps = (M.const[:, n:n + 1] for n in range(3))
        M.ident = M.const[:, C_ID:C_ID + P]
        M.upper = M.const[:, C_UP:C_UP + P]
        M.ones = M.const[:, C_ONE:C_ONE + P]
        M.upper8 = M.const[:, C_UP8:C_UP8 + P]
        M.block8 = M.const[:, C_BLK8:C_BLK8 + P]
        M.inseq = M.const[:, C_SEQ:C_SEQ + NB]
        M.early = M.const[:, C_EARLY:C_LEVEL].rearrange("p (g t) -> p g t", t=PM)
        M.level = M.const[:, C_LEVEL:C_ALL].rearrange("p (l n) -> p l n", n=P)
        M.xT = sb("xT", [P, KC, T])
        M.mT = sb("mT", [P, KC, T])
        M.y_rows = nc.dram_tensor("y_rows", (SLOTS, D), F32, kind="Internal").ap()
        with ExitStack() as early:
            M.par = early.enter_context(nc.sbuf_tensor("par", [P, R_ALL], F32))
            M.stateT = early.enter_context(nc.sbuf_tensor("stateT", [P, 24, (CW - 1) * NB], F32))
            M.scal = early.enter_context(nc.sbuf_tensor("scal", [P, H, S_ALL], F32))
            phase_a(nc, A, O, M)
            phase_b(nc, A, O, M)
        M.logits = sb("logits", [P, NT, EG + E])
        M.dest = sb("dest", [P, 2, NT], I32)
        M.w12 = sb("w12", [P, 2, NT])
        M.idx_all = sb("idx_all", [BLK, NBLK], I32)
        M.row_tok = nc.dram_tensor("row_tok", (SLOTS, 1), I32, kind="Internal").ap()
        M.blk_d = nc.dram_tensor("blk_d", (NBLK + 1, 1), I32, kind="Internal").ap()
        M.x1d = nc.dram_tensor("x1_rows", (T, D), F32, kind="Internal").ap()
        M.x2d = nc.dram_tensor("x2_rows", (T, D), F32, kind="Internal").ap()
        phase_c(nc, A, O, M)
        phase_r(nc, A, O, M)
        phase_d(nc, A, O, M)
        phase_e(nc, A, O, M)


_INS = ['x_prompt', 'x_sample', 'cache_mem_k', 'cache_mem_v', 'state_delta', 'state_conv', 'state_pool', 'mem_prompt',
        'w_in', 'w_conv', 'a_log', 'dt_bias', 'w_onorm', 'w_pool', 'pool_scale', 'w_out', 'ln1_g', 'ln1_b',
        'w_cq', 'w_ck', 'w_cv', 'w_co', 'ln2_g', 'ln2_b', 'w_router_group', 'w_router_expert', 'w_gate', 'w_up',
        'w_down', 'ln3_g', 'ln3_b']
_OUTS = [('y_prompt', (1, SEQ, D)), ('y_sample', (NB, DS, D)), ('delta_prompt', (1, 1, H, HD, HD)),
         ('conv_prompt', (1, 1, CW - 1, QKV)), ('pool_prompt', (1, 1, PM - 1, D)), ('mem_k', (1, 1, MEM, CAH, CAD)),
         ('mem_v', (1, 1, MEM, CAH, CAD)), ('delta_sample', (1, NB, H, HD, HD)),
         ('conv_sample', (1, NB, CW - 1, QKV)), ('pool_sample', (1, NB, PM - 1, D))]


def kernel(**inputs):
    import concourse.bacc as bacc
    from concourse.bass_utils import run_bass_kernel_spmd

    nc = bacc.Bacc("TRN2", target_bir_lowering=False, num_devices=1)
    arrays, A, O = {}, {}, {}
    for name in _INS:
        a = np.ascontiguousarray(inputs[name])
        arrays[f"in_{name}"] = a
        A[name] = nc.dram_tensor(f"in_{name}", a.shape, mybir.dt.from_np(a.dtype), kind="ExternalInput").ap()
    arrays["in_const"] = constants()
    A["const"] = nc.dram_tensor("in_const", arrays["in_const"].shape, F32, kind="ExternalInput").ap()
    arrays["in_rconst"] = routing_constants()
    A["rconst"] = nc.dram_tensor("in_rconst", (P, RC_ALL), F32, kind="ExternalInput").ap()
    arrays["in_tokens"] = np.ascontiguousarray(np.arange(NT * P, dtype=np.int32).reshape(NT, P).T)
    A["tokens"] = nc.dram_tensor("in_tokens", (P, NT), I32, kind="ExternalInput").ap()
    for name, shape in _OUTS:
        O[name] = nc.dram_tensor(f"out_{name}", shape, F32, kind="ExternalOutput").ap()
    build(nc, A, O)
    r = run_bass_kernel_spmd(nc, [arrays], core_ids=[0])
    return tuple(r.results[0][f"out_{name}"] for name, _ in _OUTS)
```
